# Optimizing a Trainium2 kernel written in Bass

```python
import math
import jax, jax.numpy as jnp
from jax import lax
import numpy as np

D_MODEL = 1024
BATCH = 1
SEQ = 256
DEPTH = 2

EPS = 1e-6
D_MIX = D_MODEL
LRU_WIDTH = D_MIX // 2
LRU_BLOCKS = 8
LRU_BLOCK_W = LRU_WIDTH // LRU_BLOCKS
LRU_C = 8.0
CONV_W = 4
N_HEADS = 8
QK_NOPE = 64
QK_ROPE = 32
V_HEAD = 64
Q_LORA = 256
KV_LORA = 128
ROPE_THETA = 10000.0
Q_BLOCK = 128
IN_SPLITS = (LRU_WIDTH, 2 * LRU_WIDTH, 2 * LRU_WIDTH + Q_LORA,
             2 * LRU_WIDTH + Q_LORA + KV_LORA)
IN_COLS = 2 * LRU_WIDTH + Q_LORA + KV_LORA + QK_ROPE
D_FF_DENSE = 2816
N_EXPERTS = 8
TOP_K = 2
D_FF_EXPERT = 1792
N_DENSE = (DEPTH + 1) // 2
N_MOE = DEPTH // 2

kernel_name = "hymba_rglru_mla_moe_trunk"

def rmsnorm(x, g):
    xf = x.astype(jnp.float32)
    y = xf * lax.rsqrt(jnp.mean(xf * xf, axis=-1, keepdims=True) + EPS)
    return (y * g.astype(jnp.float32)).astype(x.dtype)

def rope_tables(positions):
    half = QK_ROPE // 2
    inv = 1.0 / (ROPE_THETA ** (jnp.arange(half, dtype=jnp.float32) / half))
    ang = positions.astype(jnp.float32)[..., None] * inv
    return jnp.cos(ang), jnp.sin(ang)

def apply_rope(x, cos, sin):
    xf = x.astype(jnp.float32)
    x1, x2 = xf[..., : QK_ROPE // 2], xf[..., QK_ROPE // 2:]
    out = jnp.concatenate([x1 * cos - x2 * sin, x2 * cos + x1 * sin], axis=-1)
    return out.astype(x.dtype)

def causal_depthwise_conv(x, w, b):
    y = lax.conv_general_dilated(
        x, w[:, None, :].astype(x.dtype), window_strides=(1,),
        padding=((CONV_W - 1, 0),), dimension_numbers=("NWC", "WIO", "NWC"),
        feature_group_count=x.shape[-1])
    return y + b

def rg_lru(x, wa, ba, wx, bx, lam):
    B, S, C = x.shape
    xb = x.reshape(B, S, LRU_BLOCKS, LRU_BLOCK_W)
    r = jax.nn.sigmoid(jnp.einsum("bsnc,ncd->bsnd", xb, wa) + ba).reshape(B, S, C)
    i = jax.nn.sigmoid(jnp.einsum("bsnc,ncd->bsnd", xb, wx) + bx).reshape(B, S, C)
    log_a = -LRU_C * r.astype(jnp.float32) * jax.nn.softplus(-lam.astype(jnp.float32))
    a = jnp.exp(log_a)
    mult = jnp.sqrt(-jnp.expm1(2.0 * log_a))
    mult = jnp.where((jnp.arange(S) == 0)[None, :, None], jnp.float32(1.0), mult)
    u = mult * (i * x).astype(jnp.float32)

    def combine(left, right):
        a_l, b_l = left
        a_r, b_r = right
        return a_l * a_r, a_r * b_l + b_r

    _, h = lax.associative_scan(combine, (a, u), axis=1)
    return h.astype(x.dtype)

def mla_causal_attention(q_nope, q_rope, k_nope, k_rope, v):
    B, S, H, _ = q_nope.shape
    nb = S // Q_BLOCK
    scale = 1.0 / math.sqrt(QK_NOPE + QK_ROPE)
    qn = q_nope.reshape(B, nb, Q_BLOCK, H, QK_NOPE).transpose(1, 0, 2, 3, 4)
    qr = q_rope.reshape(B, nb, Q_BLOCK, H, QK_ROPE).transpose(1, 0, 2, 3, 4)
    k_pos = jnp.arange(S)

    def one_block(args):
        qn_b, qr_b, bi = args
        s = (jnp.einsum("bqhd,bkhd->bhqk", qn_b, k_nope, preferred_element_type=jnp.float32)
             + jnp.einsum("bqhd,bkd->bhqk", qr_b, k_rope, preferred_element_type=jnp.float32)) * scale
        q_pos = bi * Q_BLOCK + jnp.arange(Q_BLOCK)
        s = jnp.where((k_pos[None, :] <= q_pos[:, None])[None, None], s, -jnp.inf)
        p = jax.nn.softmax(s, axis=-1)
        return jnp.einsum("bhqk,bkhd->bqhd", p.astype(v.dtype), v)

    o = lax.map(one_block, (qn, qr, jnp.arange(nb)))
    return o.transpose(1, 0, 2, 3, 4).reshape(B, S, H * V_HEAD)

def swiglu(t, wg, wu, wd):
    return (jax.nn.silu(t @ wg) * (t @ wu)) @ wd

def moe_swiglu(h, router_w, wg, wu, wd):
    B, S, D = h.shape
    t = h.reshape(B * S, D)
    logits = (t @ router_w).astype(jnp.float32)
    top_v, top_i = lax.top_k(logits, TOP_K)
    top_w = jax.nn.softmax(top_v, axis=-1)
    gates = jnp.sum(jax.nn.one_hot(top_i, N_EXPERTS, dtype=jnp.float32) * top_w[..., None], axis=1)
    out = jnp.zeros((B * S, D), jnp.float32)
    for e in range(N_EXPERTS):
        out = out + gates[:, e:e + 1] * swiglu(t, wg[e], wu[e], wd[e]).astype(jnp.float32)
    return out.astype(h.dtype).reshape(B, S, D)

def setup_inputs(seed: int = 0) -> dict:
    key = jax.random.key(seed)
    ks = jax.random.split(key, 32)
    f32 = jnp.float32

    def nrm(k, shape, fan_in):
        return jax.random.normal(k, shape, f32) * (fan_in ** -0.5)

    def gain(k, shape):
        return 1.0 + 0.02 * jax.random.normal(k, shape, f32)

    def bias(k, shape):
        return 0.02 * jax.random.normal(k, shape, f32)

    u = jax.random.uniform(ks[10], (DEPTH, LRU_WIDTH), f32, minval=0.9, maxval=0.999)
    a0 = u ** (1.0 / LRU_C)
    lru_lambda = jnp.log(a0) - jnp.log1p(-a0)

    return {
        "x": jax.random.normal(ks[0], (BATCH, SEQ, D_MODEL), f32),
        "positions": jnp.broadcast_to(jnp.arange(SEQ, dtype=jnp.int32), (BATCH, SEQ)),
        "norm_mix": gain(ks[1], (DEPTH, D_MODEL)),
        "w_in": nrm(ks[2], (DEPTH, D_MODEL, IN_COLS), D_MODEL),
        "conv_w": nrm(ks[3], (DEPTH, CONV_W, LRU_WIDTH), CONV_W),
        "conv_b": bias(ks[4], (DEPTH, LRU_WIDTH)),
        "lru_wa": nrm(ks[5], (DEPTH, LRU_BLOCKS, LRU_BLOCK_W, LRU_BLOCK_W), LRU_BLOCK_W),
        "lru_ba": bias(ks[6], (DEPTH, LRU_BLOCKS, LRU_BLOCK_W)),
        "lru_wx": nrm(ks[7], (DEPTH, LRU_BLOCKS, LRU_BLOCK_W, LRU_BLOCK_W), LRU_BLOCK_W),
        "lru_bx": bias(ks[8], (DEPTH, LRU_BLOCKS, LRU_BLOCK_W)),
        "lru_lambda": lru_lambda,
        "q_norm": gain(ks[11], (DEPTH, Q_LORA)),
        "w_uq": nrm(ks[12], (DEPTH, Q_LORA, N_HEADS * (QK_NOPE + QK_ROPE)), Q_LORA),
        "kv_norm": gain(ks[13], (DEPTH, KV_LORA)),
        "w_ukv": nrm(ks[14], (DEPTH, KV_LORA, N_HEADS * (QK_NOPE + V_HEAD)), KV_LORA),
        "w_out": nrm(ks[15], (DEPTH, D_MIX, D_MODEL), D_MIX),
        "norm_ffn": gain(ks[16], (DEPTH, D_MODEL)),
        "dense_w_gate": nrm(ks[17], (N_DENSE, D_MODEL, D_FF_DENSE), D_MODEL),
        "dense_w_up": nrm(ks[18], (N_DENSE, D_MODEL, D_FF_DENSE), D_MODEL),
        "dense_w_down": nrm(ks[19], (N_DENSE, D_FF_DENSE, D_MODEL), D_FF_DENSE),
        "router_w": nrm(ks[20], (N_MOE, D_MODEL, N_EXPERTS), D_MODEL),
        "expert_w_gate": nrm(ks[21], (N_MOE, N_EXPERTS, D_MODEL, D_FF_EXPERT), D_MODEL),
        "expert_w_up": nrm(ks[22], (N_MOE, N_EXPERTS, D_MODEL, D_FF_EXPERT), D_MODEL),
        "expert_w_down": nrm(ks[23], (N_MOE, N_EXPERTS, D_FF_EXPERT, D_MODEL), D_FF_EXPERT),
        "norm_final": gain(ks[24], (D_MODEL,)),
    }

def reference(x, positions, norm_mix, w_in, conv_w, conv_b, lru_wa, lru_ba, lru_wx, lru_bx,
              lru_lambda, q_norm, w_uq, kv_norm, w_ukv, w_out, norm_ffn, dense_w_gate,
              dense_w_up, dense_w_down, router_w, expert_w_gate, expert_w_up, expert_w_down,
              norm_final):
    B, S, _ = x.shape
    cos, sin = rope_tables(positions)
    for l in range(DEPTH):
        h = rmsnorm(x, norm_mix[l])
        z = h @ w_in[l]
        x_lru, y_gate, c_q, c_kv, k_rope = jnp.split(z, IN_SPLITS, axis=-1)

        xc = causal_depthwise_conv(x_lru, conv_w[l], conv_b[l])
        hl = rg_lru(xc, lru_wa[l], lru_ba[l], lru_wx[l], lru_bx[l], lru_lambda[l])
        lru_out = hl * jax.nn.gelu(y_gate)

        q = (rmsnorm(c_q, q_norm[l]) @ w_uq[l]).reshape(B, S, N_HEADS, QK_NOPE + QK_ROPE)
        kv = (rmsnorm(c_kv, kv_norm[l]) @ w_ukv[l]).reshape(B, S, N_HEADS, QK_NOPE + V_HEAD)
        q_nope = q[..., :QK_NOPE]
        q_rope = apply_rope(q[..., QK_NOPE:], cos[:, :, None, :], sin[:, :, None, :])
        k_nope, v = kv[..., :QK_NOPE], kv[..., QK_NOPE:]
        k_rope = apply_rope(k_rope, cos, sin)
        attn_out = mla_causal_attention(q_nope, q_rope, k_nope, k_rope, v)

        x = x + jnp.concatenate([lru_out, attn_out], axis=-1) @ w_out[l]

        h2 = rmsnorm(x, norm_ffn[l])
        if l % 2 == 0:
            j = l // 2
            ffn = swiglu(h2, dense_w_gate[j], dense_w_up[j], dense_w_down[j])
        else:
            j = l // 2
            ffn = moe_swiglu(h2, router_w[j], expert_w_gate[j], expert_w_up[j], expert_w_down[j])
        x = x + ffn
    return rmsnorm(x, norm_final)


_drawn_inputs = setup_inputs


def setup_inputs(seed=0):
    import zlib

    import numpy as np

    out = dict(_drawn_inputs(seed))
    spreads = {}
    factors = {'lru_ba': 21.452, 'lru_bx': 8.0, 'q_norm': 5.045, 'kv_norm': 3.364, 'norm_final': 8.116}
    for name, (base, spread) in spreads.items():
        noise = np.random.default_rng([zlib.crc32(name.encode()), seed]).standard_normal(out[name].shape)
        drawn = base * np.exp(spread * noise) if base else spread * noise
        out[name] = __import__('jax').numpy.asarray(drawn.astype(out[name].dtype))
    for name, factor in factors.items():
        out[name] = (out[name] * factor).astype(out[name].dtype)
    return out
```

```python
import math
from contextlib import ExitStack

import numpy as np
import concourse.bass as bass
from concourse import mybir

P = 128
F32, F32R, I32, U32 = mybir.dt.float32, mybir.dt.float32r, mybir.dt.int32, mybir.dt.uint32
ALU = mybir.AluOpType
ACT = mybir.ActivationFunctionType
AX = mybir.AxisListType.X

EPS = 1e-6
CONV_W = 4
N_HEADS = 8
QK_NOPE, QK_ROPE, V_HEAD = 64, 32, 64
QK = QK_NOPE + QK_ROPE
HALF = QK_ROPE // 2
ROPE_THETA = 10000.0
TOP_K = 2
LRU_C = 8.0

RAW = 7
SPLIT = 3
CHUNK = 2048
FW = 256
MASKED = -1e30


def trunk(nc, x, positions, norm_mix, w_in, conv_w, conv_b, lru_wa, lru_ba, lru_wx, lru_bx,
          lru_lambda, q_norm, w_uq, kv_norm, w_ukv, w_out, norm_ffn, dense_w_gate, dense_w_up,
          dense_w_down, router_w, expert_w_gate, expert_w_up, expert_w_down, norm_final, out):
    DEPTH, D, IN_COLS = w_in.shape
    SEQ = x.shape[1]
    NB = SEQ // P
    KT = D // P
    LW = conv_w.shape[2]
    LT = LW // P
    QL, KVL = w_uq.shape[1], w_ukv.shape[1]
    CT = (QL + KVL) // P
    ZT = IN_COLS - 2 * LW
    E = expert_w_gate.shape[1]
    DENSE_UNITS = dense_w_gate.shape[2] // FW
    UNITS = expert_w_gate.shape[3] // FW
    SCALE = 1.0 / math.sqrt(QK)
    assert NB == 2 and DEPTH == 2 and KT == 8 and LT == 4 and UNITS == 7 and SEQ == 256

    MIX_CHUNKS = 12

    def ffn_order(units):
        order = []
        for s in range(units + 2):
            if s < units:
                order += [("gu", s, 0), ("gu", s, 1)]
            if s >= 2:
                order.append(("down", s - 2, 0))
        return order

    DENSE_ORDER = ffn_order(DENSE_UNITS)
    EXPERT_ORDER = ffn_order(UNITS)
    FIRST = {("mix", 0): 0, ("dense", 0): MIX_CHUNKS,
             ("mix", 1): MIX_CHUNKS + len(DENSE_ORDER)}
    EXPERT0 = FIRST["mix", 1] + MIX_CHUNKS
    PER_JOB = len(EXPERT_ORDER)
    assert PER_JOB % RAW == 0 and PER_JOB % SPLIT == 0
    DENSE_U = DENSE_UNITS * NB
    SLOTS = 3

    ctx = ExitStack()
    with ctx:
        def sb(name, shape, dt=F32):
            return ctx.enter_context(nc.sbuf_tensor(name, shape, dt))

        def sem(name):
            return ctx.enter_context(nc.semaphore(name))

        raw = sb("raw", [P, RAW, CHUNK])
        w_hi = sb("w_hi", [P, SPLIT, CHUNK], F32R)
        w_lo = sb("w_lo", [P, SPLIT, CHUNK], F32R)
        xs = sb("xs", [P, NB, D])
        xn = sb("xn", [P, NB, D])
        act_hi = sb("act_hi", [P, KT, SEQ], F32R)
        act_lo = sb("act_lo", [P, KT, SEQ], F32R)
        sm_hi = sb("sm_hi", [P, SLOTS, NB, FW], F32R)
        sm_lo = sb("sm_lo", [P, SLOTS, NB, FW], F32R)
        c_hi = sm_hi[:, :, 0, :]
        c_lo = sm_lo[:, :, 0, :]
        xl = sb("xl", [P, LT, CONV_W - 1 + SEQ])
        xc = sb("xc", [P, LT, SEQ])
        yg = sb("yg", [P, LT, SEQ])
        gg = sb("gg", [P, LT, SEQ])
        ta = sb("ta", [P, LT, SEQ])
        tb = sb("tb", [P, LT, SEQ])
        tr = sb("tr", [P, LT, SEQ])
        ts = sb("ts", [P, LT, SEQ])
        kcat = sb("kcat", [P, NB, N_HEADS, QK])
        vv = sb("vv", [P, NB, N_HEADS, V_HEAD])
        cn = tr[:, 0:CT, :].rearrange("p t n -> p (t n)").rearrange("p (b n) -> p b n", b=NB)
        qcat = xn[:, :, 0:N_HEADS * QK].rearrange("p b (h d) -> p b h d", h=N_HEADS)
        qkT = sb("qkT", [QK, 2, 2 * SEQ])
        pr = sb("pr", [P, 2, 3 * P])
        pT = sb("pT", [P, 2, 3 * P])
        rope_a = ts[:, 0, :].rearrange("p (h d) -> p h d", h=N_HEADS)
        rope_b = ts[:, 1, :].rearrange("p (h d) -> p h d", h=N_HEADS)
        kr = sb("kr", [P, NB, QK_ROPE])
        gate_bd = sb("gate_bd", [P, 2, LT, P])
        ident = sb("ident", [P, P])
        mask = sb("mask", [P, 3 * P])
        rows = yg[0:102, 3, 0:P]
        prm = sb("prm", [P, 102])
        lru_c = sb("lru_c", [P, 3, DEPTH * LT])
        pos_i = sb("pos_i", [P, NB], I32)
        pos_f = sb("pos_f", [P, NB])
        inv = sb("inv", [P, HALF])
        ang = yg[:, 0, 0:NB * HALF].rearrange("p (b n) -> p b n", b=NB)
        turn = yg[:, 1, 0:2 * NB * HALF].rearrange("p (w b n) -> p w b n", w=2, b=NB)
        trig_in = yg[:, 2, 0:2 * NB * HALF].rearrange("p (w b n) -> p w b n", w=2, b=NB)
        trig = sb("trig", [P, 2, NB, HALF])
        ssq = sb("ssq", [P, NB])
        mean = sb("mean", [P, NB])
        rstd = sb("rstd", [P, NB])
        zssq = sb("zssq", [P, 2, NB])
        zmean = sb("zmean", [P, 2, NB])
        zrstd = sb("zrstd", [P, 2, NB])
        mhalf = sb("mhalf", [P, 4])
        mx = sb("mx", [P, 2, 2])
        nmx = sb("nmx", [P, 2, 2])
        rs = sb("rs", [P, 2, 2])
        ri = sb("ri", [P, 2, 2])
        grow = xc[:, :, :].rearrange("p t n -> p (t n)")
        sg = yg[:, 0:2, :]
        hid = yg[:, 2:4, :]
        ysb = tr[:, :, :].rearrange("p t n -> p (t n)")
        sel_s = ta[:, 0, :].rearrange("p (b n) -> p b n", b=NB)
        sel_g = ta[:, 1, :].rearrange("p (b n) -> p b n", b=NB)
        sel_t = ta[:, 2, :].rearrange("p (b n) -> p b n", b=NB)
        before = gg[:, 0, 0:P]
        ones = gg[:, 0, P:2 * P]
        slot = gg[:, 1, 0:P]
        slot2 = gg[:, 1, P:2 * P]
        rw = gg[:, 3, 0:KT * E]
        rw_hi, rw_lo = (w[:, 0, 1, 0:KT * E] for w in (sm_hi, sm_lo))
        lg, top, topi, topf = (gg[:, 2, 16 * k:16 * k + 16].rearrange("p (b e) -> p b e", b=NB) for k in range(4))
        topi = topi.bitcast(U32)
        oh = gg[:, 2, 64:64 + 2 * NB * E].rearrange("p (k b e) -> p k b e", k=2, b=NB)
        pick, gates, place = (gg[:, 3, 64 + 16 * k:80 + 16 * k].rearrange("p (b e) -> p b e", b=NB) for k in range(3))
        i8 = sb("i8", [P, E])
        dif = sb("dif", [P, NB])
        tw = sb("tw", [P, 2, NB])
        cur = sb("cur", [P, 2, NB])
        jb = gg[0:1, 3, 128:128 + 4 * E].rearrange("p (k e) -> p k e", k=4)
        jf = sb("jf", [1, 4])
        jobs = sb("jobs", [1, 4], I32)

        bank = [ctx.enter_context(nc.psum_tensor(f"bank{i}", [P, 512], F32)) for i in range(8)]

        landed = [sem(f"landed{i}") for i in range(RAW)]
        hi_made, lo_made = sem("hi_made"), sem("lo_made")
        used = sem("used")
        x_in, rows_in, pos_in, rw_in, wout_s = sem("x_in"), sem("rows_in"), sem("pos_in"), sem("rw_in"), sem("stored")
        bd_in, grow_in = sem("bd_in"), sem("grow_in")
        bd_zero, consts = sem("bd_zero"), sem("consts")
        prm_t, prm_r = sem("prm_t"), sem("prm_r")
        lam_e, lru_r = sem("lam_e"), sem("lru_r")
        angle_r, trig_r = sem("angle_r"), sem("trig_r")
        ss_r, rstd_r, xn_a, xn_v = sem("ss_r"), sem("rstd_r"), sem("xn_a"), sem("xn_v")
        nT, nT_hi, nT_lo = sem("nT"), sem("nT_hi"), sem("nT_lo")
        xl_r, yg_r = sem("xl_r"), sem("yg_r")
        zss_r, zrstd_r, cn_r, kr_r, kr_c = sem("zss_r"), sem("zrstd_r"), sem("cn_r"), sem("kr_r"), sem("kr_c")
        cT, cT_hi, cT_lo = sem("cT"), sem("cT_hi"), sem("cT_lo")
        q_c, q_r, k_a, k_v = sem("q_c"), sem("q_r"), sem("k_a"), sem("k_v")
        xc_r, gate_p, gate_t = sem("xc_r"), sem("gate_p"), sem("gate_t")
        sq_r, gin_r, gth_r, gg_r, iw_r = sem("sq_r"), sem("gin_r"), sem("gth_r"), sem("gg_r"), sem("iw_r")
        lru_o, lru_hi, lru_lo = sem("lru_o"), sem("lru_hi"), sem("lru_lo")
        qkT_p, qkT_r, s_p, s_r, p_r, pn_r, pT_p, pT_r, o_p, o_hi, o_lo = (
            sem("qkT_p"), sem("qkT_r"), sem("s_p"), sem("s_r"), sem("p_r"), sem("pn_r"), sem("pT_p"),
            sem("pT_r"), sem("o_p"), sem("o_hi"), sem("o_lo"))
        mix_r = sem("mix_r")
        gu_p, sg_r, hid_r, hT_p, hT_hi, hT_lo = (
            sem("gu_p"), sem("sg_r"), sem("hid_r"), sem("hT_p"), sem("hT_hi"), sem("hT_lo"))
        y_r = sem("y_r")
        rw_h, rw_r, lg_p, lg_r, tw_r, pick_r, place_p, jobs_r, xg_r = (
            sem("rw_h"), sem("rw_r"), sem("lg_p"), sem("lg_r"), sem("tw_r"), sem("pick_r"),
            sem("place_p"), sem("jobs_r"), sem("xg_r"))
        cur_r = sem("cur_r")
        sel_r, xg_p, xg_hi, xg_lo, sT_p, sT_r, ye_r, sc_p, sc_r = (
            sem("sel_r"), sem("xg_p"), sem("xg_hi"), sem("xg_lo"), sem("sT_p"), sem("sT_r"),
            sem("ye_r"), sem("sc_p"), sem("sc_r"))
        out_r = sem("out_r")
        a_ch, v_ch, g_ch = sem("scalar_step"), sem("vector_step"), sem("pool_step")

        def stepper(eng, s):
            n = [0]

            def step(*ins):
                n[0] += 1
                ins[-1].then_inc(s, 1)
                eng.wait_ge(s, n[0])
            return step

        def raw_slot(first, c):
            return (first + c) % RAW

        def raw_turn(first, c, i=0):
            return (first + c) // RAW + 1 + i * (PER_JOB // RAW)

        def split_slot(first, c):
            return (first + c) % SPLIT

        def nth(first, c, i=0):
            return first + c + i * PER_JOB

        def by_tile(w):
            return w.rearrange("(k p) n -> p k n", p=P)

        def mix_sources(l):
            win, wout = by_tile(w_in[l]), by_tile(w_out[l])
            for c0, wd in ((0, LW), (LW, LW), (2 * LW, ZT)):
                for k in (0, 4):
                    yield wd, 4, win[:, k:k + 4, c0:c0 + wd]
            yield N_HEADS * QK, QL // P, by_tile(w_uq[l])
            yield w_ukv.shape[2], KVL // P, by_tile(w_ukv[l])
            for k in range(0, KT, 2):
                yield D, 2, wout[:, k:k + 2, :]

        def load_ffn(eng, order, first, gate, up, down, i=0):
            g, u = by_tile(gate), by_tile(up)
            d = down.rearrange("(s p j) n -> s p (j n)", p=P, j=2)
            for c, (kind, s, k) in enumerate(order):
                r = raw[:, raw_slot(first, c), :]
                eng.wait_ge(lo_made, nth(first, c, i) - RAW + 1)
                if kind == "gu":
                    dst = r.rearrange("p (k w n) -> p k w n", k=4, w=2)
                    for w, src in enumerate((g, u)):
                        eng.dma_start(dst[:, :, w, :], src[:, 4 * k:4 * k + 4, s * FW:(s + 1) * FW]
                                      ).then_inc(landed[raw_slot(first, c)], 16)
                else:
                    for j in range(2):
                        h = slice(j * CHUNK // 2, (j + 1) * CHUNK // 2)
                        eng.dma_start(r[:, h], d[s][:, h]).then_inc(landed[raw_slot(first, c)], 16)

        def ffn(ops, units, chunk, ahead):
            finish, turned = ops
            c = ahead
            for s in range(units + 1):
                if s >= 1:
                    finish(s - 1)
                if s >= 2:
                    chunk(c)
                    c += 1
                if s + 1 < units:
                    chunk(c)
                    c += 1
                if s >= 1:
                    turned(s - 1)
                if s + 1 < units:
                    chunk(c)
                    c += 1
            chunk(c)

        def act_unit_ops(act, nb, u0, gu_done):
            def finish(s):
                for b in range(nb):
                    if b < nb - 1:
                        act.wait_ge(gu_p, s + 1)
                    else:
                        act.wait_ge(used, gu_done(s))
                    o = b if nb == 2 else s % 2
                    act.activation(sg[:, o, :], bank[4 + o][:, 0:FW], ACT.Silu).then_inc(sg_r, 1)

            def turned(s):
                for b in range(nb):
                    act.wait_ge(hT_p, u0 + nb * s + b + 1)
                    o = b if nb == 2 else s % 2
                    act.activation(sm_hi[:, s % SLOTS, b, :], bank[6 + o][:, 0:FW], ACT.Copy).then_inc(hT_hi, 1)
            return finish, turned

        def vec_unit_ops(dve, nb, u0):
            def finish(s):
                for b in range(nb):
                    dve.wait_ge(sg_r, u0 + nb * s + b + 1)
                    o = b if nb == 2 else s % 2
                    dve.tensor_tensor(hid[:, o, :], sg[:, o, :], bank[4 + o][:, FW:2 * FW], ALU.mult).then_inc(hid_r, 1)

            def turned(s):
                for b in range(nb):
                    dve.wait_ge(hT_hi, u0 + nb * s + b + 1)
                    o = b if nb == 2 else s % 2
                    dve.tensor_tensor(sm_lo[:, s % SLOTS, b, :], bank[6 + o][:, 0:FW],
                                      sm_hi[:, s % SLOTS, b, :].bitcast(F32), ALU.subtract).then_inc(hT_lo, 1)
            return finish, turned

        block = ctx.enter_context(nc.Block())

        @block.sync
        def _(sp):
            for b in range(NB):
                sp.dma_start(xs[:, b, :], x[0, b * P:(b + 1) * P, :]).then_inc(x_in, 16)
            r0 = 0
            for v in (norm_mix.rearrange("l (k p) -> (l k) p", p=P),
                      norm_ffn.rearrange("l (k p) -> (l k) p", p=P),
                      conv_w.rearrange("l j (t p) -> (l j t) p", p=P),
                      conv_b.rearrange("l (t p) -> (l t) p", p=P),
                      lru_ba.rearrange("l (t q) c -> (l t) (q c)", q=2),
                      lru_bx.rearrange("l (t q) c -> (l t) (q c)", q=2),
                      lru_lambda.rearrange("l (t p) -> (l t) p", p=P),
                      q_norm.rearrange("l (k p) -> (l k) p", p=P),
                      kv_norm.rearrange("l (k p) -> (l k) p", p=P)):
                sp.dma_start(rows[r0:r0 + v.shape[0], :], v).then_inc(rows_in, 16)
                r0 += v.shape[0]
            sp.dma_start(pos_i[:, :], positions.rearrange("o (b p) -> p (o b)", p=P),
                         allow_slow_non_contiguous=True).then_inc(pos_in, 16)

            def load_mix(l):
                first = FIRST["mix", l]
                for c, (wd, k, src) in enumerate(mix_sources(l)):
                    if first + c >= RAW:
                        sp.wait_ge(lo_made, first + c - RAW + 1)
                    s = raw_slot(first, c)
                    dst = raw[:, s, 0:k * wd].rearrange("p (k n) -> p k n", k=k)
                    for j in range(2):
                        ks, ns = ((slice(j * k // 2, (j + 1) * k // 2), slice(0, wd)) if k > 1 else
                                  (slice(0, 1), slice(j * wd // 2, (j + 1) * wd // 2)))
                        sp.dma_start(dst[:, ks, ns], src[:, ks, ns]).then_inc(landed[s], 16)

            def load_gates(l):
                for w, src in enumerate((lru_wa, lru_wx)):
                    for q in range(2):
                        sp.dma_start(gate_bd[64 * q:64 * q + 64, w, :, 64 * q:64 * q + 64],
                                     src[l].rearrange("(t q) c d -> q c t d", q=2)[q]).then_inc(bd_in, 16)

            sp.wait_ge(bd_zero, 1)
            load_gates(0)
            load_mix(0)
            sp.wait_ge(gate_p, 1)
            load_gates(1)
            load_ffn(sp, DENSE_ORDER, FIRST["dense", 0], dense_w_gate[0], dense_w_up[0], dense_w_down[0])
            load_mix(1)

            def job(i, e):
                load_ffn(sp, EXPERT_ORDER, EXPERT0, *(w[0, bass.ds(e, 1)].rearrange("o a b -> (o a) b")
                                                      for w in (expert_w_gate, expert_w_up, expert_w_down)), i=i)

            with sp.Fori(0, E) as i:
                job(i, i)
            sp.wait_ge(jobs_r, 1)
            more = sp.value_load(jobs[0:1, 0:1], min_val=0, max_val=3)
            with sp.If(more > 0):
                with sp.Fori(E, E + more) as i:
                    e = sp.value_load(jobs[0:1, bass.ds(i - (E - 1), 1)], min_val=0, max_val=E - 1)
                    job(i, e)
            for b in range(NB):
                sp.wait_ge(out_r, b + 1)
                sp.dma_start(out[0, b * P:(b + 1) * P, :], xn[:, b, :]).then_inc(wout_s, 16)
            sp.wait_ge(wout_s, 16 * NB)

        @block.gpsimd
        def _(pool):
            step = stepper(pool, g_ch)
            pool.memset(gate_bd[:], 0.0).then_inc(bd_zero, 1)
            pool.memset(mhalf[:], -0.5)
            for j in range(HALF):
                pool.memset(inv[:, j:j + 1], float(np.float32(1.0) / np.float32(ROPE_THETA) ** np.float32(j / HALF)))
            pool.memset(xl[:, :, 0:CONV_W - 1], 0.0)
            step(pool.memset(ident[:], 0.0))
            pool.affine_select(out=ident[:], in_=ident[:], compare_op=ALU.not_equal, fill=1.0, base=0,
                               pattern=[[-1, P]], channel_multiplier=1)
            step(pool.memset(mask[:], 0.0))
            for c in (0, 2 * P):
                pool.affine_select(out=mask[:, c:c + P], in_=mask[:, c:c + P], compare_op=ALU.is_ge,
                                   fill=MASKED, base=0, pattern=[[-1, P]], channel_multiplier=1)
            pool.iota(i8[:], pattern=[[1, E]], base=0, channel_multiplier=0,
                      allow_small_or_imprecise_dtypes=True).then_inc(consts, 1)

            def rms(k):
                pool.wait_ge(ss_r, k + 1)
                step(pool.tensor_scalar(mean[:], ssq[:], 1.0 / D, EPS, ALU.mult, ALU.add))
                pool.tensor_tensor(rstd[:], mean[:], mhalf[:, 0:NB], ALU.pow).then_inc(rstd_r, 1)

            for l in range(DEPTH):
                rms(2 * l)
                pool.wait_ge(zss_r, l + 1)
                for w, n in enumerate((QL, KVL)):
                    ins = pool.tensor_scalar(zmean[:, w, :], zssq[:, w, :], 1.0 / n, EPS, ALU.mult, ALU.add)
                step(ins)
                pool.tensor_tensor(zrstd[:].rearrange("p w b -> p (w b)"), zmean[:].rearrange("p w b -> p (w b)"),
                                   mhalf[:], ALU.pow).then_inc(zrstd_r, 1)
                pool.wait_ge(yg_r, l + 1)
                step(pool.tensor_scalar(gg[:], gg[:], 0.044715, 1.0, ALU.mult, ALU.add))
                pool.tensor_tensor(gg[:], gg[:], yg[:], ALU.mult).then_inc(gin_r, 1)
                pool.wait_ge(kr_r, l + 1)
                for b in range(NB):
                    ins = pool.tensor_copy(kcat[:, b, :, QK_NOPE:], kr[:, b, :].unsqueeze(1).to_broadcast([P, N_HEADS, QK_ROPE]))
                ins.then_inc(kr_c, 1)
                pool.wait_ge(gth_r, l + 1)
                step(pool.tensor_scalar(gg[:], gg[:], 1.0, 1.0, ALU.mult, ALU.add))
                pool.tensor_tensor(gg[:], gg[:], yg[:], ALU.mult).then_inc(gg_r, 1)
                pool.wait_ge(gate_t, l + 1)
                pool.wait_ge(xc_r, l + 1)
                step(pool.tensor_scalar(tb[:], tb[:], 1.0, 1.0, ALU.mult, ALU.add))
                pool.tensor_tensor(tb[:], tb[:], xc[:], ALU.mult).then_inc(iw_r, 1)
                rms(2 * l + 1)
            pool.wait_ge(lru_o, DEPTH)
            pool.dma_start(rw.rearrange("p (k e) -> p k e", k=KT), router_w[0].rearrange("(k p) e -> p k e", p=P)).then_inc(rw_in, 16)
            pool.dma_start(grow, norm_ffn[1].partition_broadcast(P)).then_inc(grow_in, 16)
            step(pool.memset(before, 1.0))
            pool.affine_select(out=before, in_=before, compare_op=ALU.is_gt, fill=0.0, base=0,
                               pattern=[[1, P]], channel_multiplier=-1)
            pool.memset(ones, 1.0)
            pool.iota(slot, pattern=[[1, P]], base=0, channel_multiplier=0, allow_small_or_imprecise_dtypes=True)
            pool.iota(slot2, pattern=[[1, P]], base=P, channel_multiplier=0,
                      allow_small_or_imprecise_dtypes=True).then_inc(consts, 1)
            pool.wait_ge(xg_r, 1)
            pool.dma_start(grow, norm_final.partition_broadcast(P)).then_inc(grow_in, 16)
            rms(2 * DEPTH)

        @block.scalar
        def _(act):
            step = stepper(act, a_ch)

            def hi(first, c, width=CHUNK, i=0):
                act.wait_ge(landed[raw_slot(first, c)], 32 * raw_turn(first, c, i))
                if isinstance(i, int) and i == 0 and first + c < SPLIT:
                    pass
                else:
                    act.wait_ge(used, nth(first, c, i) - SPLIT + 1)
                act.activation(w_hi[:, split_slot(first, c), 0:width], raw[:, raw_slot(first, c), 0:width],
                               ACT.Copy).then_inc(hi_made, 1)

            def norm(k):
                for b in range(NB):
                    ins = act.activation(xn[:, b, :], xs[:, b, :], ACT.Square, accum_out=ssq[:, b:b + 1])
                ins.then_inc(ss_r, 1)
                act.wait_ge(rstd_r, k + 1)
                act.activation(xn[:, 0, :], xs[:, 0, :], ACT.Copy, scale=rstd[:, 0:1]).then_inc(xn_a, 1)

            def norm_split(k, gain0):
                for j in range(4):
                    act.wait_ge(nT, 4 * k + j + 1)
                    for t in range(2):
                        kt = 2 * j + t
                        ins = act.activation(act_hi[:, kt, :], bank[4 * (k % 2) + j][:, t * SEQ:(t + 1) * SEQ], ACT.Copy,
                                             scale=prm[:, gain0 + kt:gain0 + kt + 1])
                    ins.then_inc(nT_hi, 1)

            act.wait_ge(prm_r, 1)
            act.activation(lru_c[:, 0, :], prm[:, 88:96], ACT.Exp, scale=-1.0).then_inc(lam_e, 1)
            act.wait_ge(lam_e, 1)
            act.activation(lru_c[:, 0, :], lru_c[:, 0, :], ACT.Ln, bias=1.0).then_inc(lam_e, 1)
            act.wait_ge(angle_r, 1)
            act.activation(trig[:], trig_in, ACT.Sin).then_inc(trig_r, 1)
            act.wait_ge(x_in, 16 * NB)

            for l in range(DEPTH):
                first = FIRST["mix", l]
                if l:
                    act.wait_ge(y_r, 1)
                norm(2 * l)
                for c in range(SPLIT):
                    hi(first, c)
                norm_split(2 * l, l * KT)
                hi(first, 3)
                act.wait_ge(used, first + 2)
                for j in range(2):
                    ins = act.activation(xl[:, 2 * j:2 * j + 2, CONV_W - 1:],
                                         bank[4 + j][:].rearrange("p (t n) -> p t n", t=2), ACT.Copy)
                ins.then_inc(xl_r, 1)
                hi(first, 4, 4 * ZT)
                act.wait_ge(used, first + 4)
                for j in range(2):
                    act.activation(yg[:, 2 * j:2 * j + 2, :], bank[6 + j][:].rearrange("p (t n) -> p t n", t=2), ACT.Copy)
                    ins = act.activation(gg[:, 2 * j:2 * j + 2, :], bank[6 + j][:].rearrange("p (t n) -> p t n", t=2), ACT.Square)
                ins.then_inc(yg_r, 1)
                hi(first, 5, 4 * ZT)
                hi(first, 6, QL // P * N_HEADS * QK)
                act.wait_ge(used, first + 6)
                for b in range(NB):
                    act.activation(cn[:, b, 0:QL], bank[b][:, 0:QL], ACT.Square, accum_out=zssq[:, 0, b:b + 1])
                    ins = act.activation(cn[:, b, QL:], bank[b][:, QL:QL + KVL], ACT.Square, accum_out=zssq[:, 1, b:b + 1])
                ins.then_inc(zss_r, 1)
                hi(first, 7, KVL // P * w_ukv.shape[2])
                act.wait_ge(cT, l + 1)
                for t in range(CT):
                    g = 96 + 2 * l + t if t < QL // P else 100 + l
                    ins = act.activation(c_hi[:, t, :], bank[2 + t // 2][:, (t % 2) * SEQ:(t % 2 + 1) * SEQ], ACT.Copy,
                                         scale=prm[:, g:g + 1])
                ins.then_inc(cT_hi, 1)
                act.wait_ge(used, first + 7)
                for b in range(NB):
                    for j in range(2):
                        ins = act.activation(qcat[:, b, 4 * j:4 * j + 4, :],
                                             bank[2 + 2 * b + j][:, 0:4 * QK].rearrange("p (h d) -> p h d", h=4), ACT.Copy)
                    ins.then_inc(q_c, 1)
                act.wait_ge(used, first + 8)
                for b in range(NB):
                    src = bank[6 - 6 * b][:].rearrange("p (h d) -> p h d", h=4)
                    act.activation(kcat[:, b, 0:4, 0:QK_NOPE], src[:, :, 0:QK_NOPE], ACT.Copy)
                    ins = act.activation(vv[:, b, 0:4, :], src[:, :, QK_NOPE:], ACT.Copy)
                ins.then_inc(k_a, 1)
                act.wait_ge(gate_p, l + 1)
                act.wait_ge(lru_r, 1)
                for t in range(LT):
                    c = l * LT + t
                    act.activation(ta[:, t, :], bank[2 + t // 2][:, (t % 2) * SEQ:(t % 2 + 1) * SEQ], ACT.Tanh,
                                   scale=0.5, bias=lru_c[:, 1, c:c + 1])
                    ins = act.activation(tb[:, t, :], bank[4 + t // 2][:, (t % 2) * SEQ:(t % 2 + 1) * SEQ], ACT.Tanh,
                                         scale=0.5, bias=lru_c[:, 2, c:c + 1])
                ins.then_inc(gate_t, 1)
                act.wait_ge(gate_t, l + 1)
                for t in range(LT):
                    c = l * LT + t
                    ins = act.activation(ta[:, t, :], ta[:, t, :], ACT.Tanh, scale=lru_c[:, 0, c:c + 1],
                                         bias=lru_c[:, 0, c:c + 1])
                step(ins)
                act.wait_ge(gin_r, l + 1)
                act.activation(gg[:], gg[:], ACT.Tanh, scale=math.sqrt(2.0 / math.pi)).then_inc(gth_r, 1)
                act.wait_ge(q_r, l + 1)
                act.activation(ts[:], ta[:], ACT.Sqrt, scale=-1.0).then_inc(sq_r, 1)

                def qk_turn(h):
                    n = N_HEADS * l + h
                    act.wait_ge(qkT_p, n + 1)
                    if n >= 2:
                        act.wait_ge(s_p, n - 1)
                    act.activation(qkT[:, h % 2, :], bank[h % 2][0:QK, :], ACT.Copy).then_inc(qkT_r, 1)

                def exps(h):
                    n = N_HEADS * l + h
                    act.wait_ge(s_r, n + 1)
                    for j, (c0, c1) in enumerate(((0, P), (P, 3 * P))):
                        ins = act.activation(pr[:, h % 2, c0:c1], pr[:, h % 2, c0:c1], ACT.Exp, scale=SCALE,
                                             bias=nmx[:, h % 2, j:j + 1], accum_out=rs[:, h % 2, j:j + 1])
                    ins.then_inc(p_r, 1)

                def p_turn(h):
                    n = N_HEADS * l + h
                    act.wait_ge(pT_p, n + 1)
                    if n >= 2:
                        act.wait_ge(o_p, n - 1)
                    act.activation(pT[:, h % 2, :], bank[4 + h % 2][:, 0:3 * P], ACT.Copy).then_inc(pT_r, 1)

                def o_split(g):
                    act.wait_ge(o_p, N_HEADS * l + 4 * g + 4)
                    act.activation(act_hi[:, LT + 2 * g:LT + 2 * g + 2, :],
                                   bank[6 + g][:].rearrange("p (t n) -> p t n", t=2), ACT.Copy).then_inc(o_hi, 1)

                for i in range(N_HEADS + 3):
                    if i < N_HEADS:
                        qk_turn(i)
                    if 1 <= i <= N_HEADS:
                        exps(i - 1)
                    if 2 <= i <= N_HEADS + 1:
                        p_turn(i - 2)
                    if i == 3:
                        hi(first, 8)
                        hi(first, 9)
                    if i == 7:
                        o_split(0)
                act.wait_ge(lru_o, l + 1)
                act.activation(act_hi[:, 0:LT, :], ts[:], ACT.Copy).then_inc(lru_hi, 1)
                hi(first, 10)
                o_split(1)
                hi(first, 11)
                act.wait_ge(mix_r, l + 1)
                norm(2 * l + 1)
                if l == 0:
                    f0 = FIRST["dense", 0]
                    hi(f0, 0)
                    hi(f0, 1)
                    norm_split(1, 16)
                    ffn(act_unit_ops(act, NB, 0, lambda s: nth(f0, DENSE_ORDER.index(("gu", s, 1))) + 1), DENSE_UNITS, lambda c: hi(f0, c), 2)
                else:
                    act.wait_ge(rw_in, 16)
                    act.activation(rw_hi, rw, ACT.Copy).then_inc(rw_h, 1)
                    norm_split(3, 24)
                    act.wait_ge(lg_r, 1)
                    act.activation(tw[:, 0, :], dif[:], ACT.Tanh, scale=0.5).then_inc(tw_r, 1)

            def job(i):
                hi(EXPERT0, 0, i=i)
                hi(EXPERT0, 1, i=i)
                act.wait_ge(xg_p, i + 1)
                for j in range(2):
                    ins = act.activation(act_hi[:, 4 * j:4 * j + 4, 0:P],
                                         bank[j][:].rearrange("p (k n) -> p k n", k=4), ACT.Copy)
                ins.then_inc(xg_hi, 1)
                act.wait_ge(sT_p, i + 1)
                act.activation(sel_t, bank[7][:, 0:NB * P].rearrange("p (b n) -> p b n", b=NB), ACT.Copy).then_inc(sT_r, 1)
                ffn(act_unit_ops(act, 1, DENSE_U + UNITS * i, lambda s: nth(EXPERT0, EXPERT_ORDER.index(("gu", s, 1)), i) + 1), UNITS, lambda c: hi(EXPERT0, c, i=i), 2)
                act.wait_ge(used, nth(EXPERT0, PER_JOB, i))
                for j in range(2):
                    ins = act.activation(ysb[:, 512 * j:512 * j + 512], bank[2 + j][:], ACT.Copy)
                ins.then_inc(ye_r, 1)

            with act.Fori(0, E) as i:
                job(i)
            act.wait_ge(jobs_r, 1)
            more = act.value_load(jobs[0:1, 0:1], min_val=0, max_val=3)
            with act.If(more > 0):
                with act.Fori(E, E + more) as i:
                    job(i)
            act.wait_ge(sc_r, (E + more) * 4)
            norm(2 * DEPTH)

        @block.vector
        def _(dve):
            step = stepper(dve, v_ch)

            def lo(first, c, width=CHUNK, i=0):
                s = split_slot(first, c)
                dve.wait_ge(hi_made, nth(first, c, i) + 1)
                dve.tensor_tensor(w_lo[:, s, 0:width], raw[:, raw_slot(first, c), 0:width],
                                  w_hi[:, s, 0:width].bitcast(F32), ALU.subtract).then_inc(lo_made, 1)

            def norm(k):
                dve.wait_ge(rstd_r, k + 1)
                dve.tensor_scalar(xn[:, 1, :], xs[:, 1, :], rstd[:, 1:2], None, ALU.mult).then_inc(xn_v, 1)

            def norm_split(k, gain0):
                for j in range(4):
                    dve.wait_ge(nT_hi, 4 * k + j + 1)
                    for t in range(2):
                        kt = 2 * j + t
                        ins = dve.scalar_tensor_tensor(out=act_lo[:, kt, :], in0=bank[4 * (k % 2) + j][:, t * SEQ:(t + 1) * SEQ],
                                                       scalar=prm[:, gain0 + kt:gain0 + kt + 1],
                                                       in1=act_hi[:, kt, :].bitcast(F32), op0=ALU.mult, op1=ALU.subtract)
                    ins.then_inc(nT_lo, 1)

            dve.wait_ge(prm_t, 1)
            dve.tensor_copy(prm[:], bank[0][:, 0:102]).then_inc(prm_r, 1)
            dve.wait_ge(pos_in, 16)
            step(dve.tensor_copy(pos_f[:], pos_i[:]))
            dve.wait_ge(consts, 1)
            for b in range(NB):
                ins = dve.tensor_scalar(ang[:, b, :], inv[:], pos_f[:, b:b + 1], None, ALU.mult)
            step(ins)
            rnd = 1.5 * 2.0 ** 23
            for w in range(2):
                ins = dve.tensor_scalar(turn[:, w], ang, 1.0 / (2 * math.pi), 0.25 * w, ALU.mult, ALU.add)
            step(ins)
            step(dve.tensor_scalar(turn, turn, rnd, -rnd, ALU.add, ALU.add))
            c1 = 6.28125
            c2 = float(np.float32(2 * math.pi - c1))
            for w in range(2):
                ins = dve.scalar_tensor_tensor(out=trig_in[:, w], in0=turn[:, w], scalar=-c1, in1=ang, op0=ALU.mult, op1=ALU.add)
            step(ins)
            step(dve.scalar_tensor_tensor(out=trig_in, in0=turn, scalar=-c2, in1=trig_in, op0=ALU.mult, op1=ALU.add))
            step(dve.tensor_scalar(trig_in[:, 1], trig_in[:, 1], math.pi / 2, None, ALU.add))
            lim = 3.1415925
            dve.tensor_scalar(trig_in, trig_in, lim, -lim, ALU.min, ALU.max).then_inc(angle_r, 1)
            dve.wait_ge(prm_r, 1)
            dve.tensor_scalar(lru_c[:, 1:3, :], prm[:, 72:88].rearrange("p (w c) -> p w c", w=2), 0.5, None, ALU.mult)
            dve.wait_ge(lam_e, 2)
            step(dve.tensor_scalar(lru_c[:, 0, :], lru_c[:, 0, :], -LRU_C / 4, None, ALU.mult))
            dve.tensor_copy(dif[:], pos_f[:]).then_inc(lru_r, 1)
            dve.wait_ge(trig_r, 1)

            def rope(dst, src, b, heads):
                sin = trig[:, 0, b, :].unsqueeze(1).to_broadcast([P, heads, HALF])
                cos = trig[:, 1, b, :].unsqueeze(1).to_broadcast([P, heads, HALF])
                ra, rb = rope_a[:, 0:heads, :], rope_b[:, 0:heads, :]
                for j in range(2):
                    hs = slice(HALF * j, HALF * j + HALF)
                    dve.tensor_tensor(ra[:, :, hs], src[:, :, hs], cos, ALU.mult)
                    ins = dve.tensor_tensor(rb[:, :, hs], src[:, :, hs], sin, ALU.mult)
                step(ins)
                dve.tensor_tensor(dst[:, :, 0:HALF], ra[:, :, 0:HALF], rb[:, :, HALF:], ALU.subtract)
                return dve.tensor_tensor(dst[:, :, HALF:], ra[:, :, HALF:], rb[:, :, 0:HALF], ALU.add)

            for l in range(DEPTH):
                first = FIRST["mix", l]
                norm(2 * l)
                for c in range(SPLIT):
                    lo(first, c)
                norm_split(2 * l, l * KT)
                lo(first, 3)
                dve.wait_ge(xl_r, l + 1)
                for j in reversed(range(CONV_W)):
                    for t in range(LT):
                        w = 32 + (l * CONV_W + j) * LT + t
                        src = xl[:, t, j:j + SEQ]
                        if j == CONV_W - 1:
                            cb = 64 + l * LT + t
                            ins = dve.tensor_scalar(xc[:, t, :], src, prm[:, w:w + 1], prm[:, cb:cb + 1], ALU.mult, ALU.add)
                        else:
                            ins = dve.scalar_tensor_tensor(out=xc[:, t, :], in0=src, scalar=prm[:, w:w + 1], in1=xc[:, t, :],
                                                           op0=ALU.mult, op1=ALU.add)
                    if j:
                        step(ins)
                    else:
                        ins.then_inc(xc_r, 1)
                    if j == 2:
                        lo(first, 4, 4 * ZT)
                    if j == 1:
                        lo(first, 5, 4 * ZT)
                lo(first, 6, QL // P * N_HEADS * QK)
                dve.wait_ge(zrstd_r, l + 1)
                for b in range(NB):
                    dve.tensor_scalar(cn[:, b, 0:QL], bank[b][:, 0:QL], zrstd[:, 0, b:b + 1], None, ALU.mult)
                    ins = dve.tensor_scalar(cn[:, b, QL:], bank[b][:, QL:QL + KVL], zrstd[:, 1, b:b + 1], None, ALU.mult)
                ins.then_inc(cn_r, 1)
                for b in range(NB):
                    ins = rope(kr[:, b, :].unsqueeze(1), bank[b][:, QL + KVL:ZT].unsqueeze(1), b, 1)
                    if b == 0:
                        step(ins)
                ins.then_inc(kr_r, 1)
                dve.wait_ge(cT_hi, l + 1)
                for t in range(CT):
                    g = 96 + 2 * l + t if t < QL // P else 100 + l
                    ins = dve.scalar_tensor_tensor(out=c_lo[:, t, :], in0=bank[2 + t // 2][:, (t % 2) * SEQ:(t % 2 + 1) * SEQ],
                                                   scalar=prm[:, g:g + 1], in1=c_hi[:, t, :].bitcast(F32),
                                                   op0=ALU.mult, op1=ALU.subtract)
                ins.then_inc(cT_lo, 1)
                lo(first, 7, KVL // P * w_ukv.shape[2])
                dve.wait_ge(kr_r, l + 1)
                for b in range(NB):
                    dve.wait_ge(q_c, NB * l + b + 1)
                    r = qcat[:, b, :, QK_NOPE:]
                    ins = rope(r, r, b, N_HEADS)
                    if b == 0:
                        step(ins)
                ins.then_inc(q_r, 1)
                dve.wait_ge(used, first + 8)
                for b in range(NB):
                    src = bank[7 - 6 * b][:].rearrange("p (h d) -> p h d", h=4)
                    dve.tensor_copy(kcat[:, b, 4:8, 0:QK_NOPE], src[:, :, 0:QK_NOPE])
                    ins = dve.tensor_copy(vv[:, b, 4:8, :], src[:, :, QK_NOPE:])
                ins.then_inc(k_v, 1)

                def mask_max(h):
                    n = N_HEADS * l + h
                    dve.wait_ge(s_p, n + 1)
                    if n >= 2:
                        dve.wait_ge(pT_p, n - 1)
                    for j, (c0, c1) in enumerate(((0, P), (P, 3 * P))):
                        ins = dve.tensor_tensor_reduce(pr[:, h % 2, c0:c1], bank[2 + h % 2][:, c0:c1], mask[:, c0:c1], 1.0, -3e38,
                                                       ALU.add, ALU.max, mx[:, h % 2, j:j + 1])
                    step(ins)
                    dve.tensor_scalar(nmx[:, h % 2, :], mx[:, h % 2, :], -SCALE, None, ALU.mult).then_inc(s_r, 1)

                def normalise(h):
                    n = N_HEADS * l + h
                    dve.wait_ge(p_r, n + 1)
                    step(dve.reciprocal(ri[:, h % 2, :], rs[:, h % 2, :]))
                    for j, (c0, c1) in enumerate(((0, P), (P, 3 * P))):
                        ins = dve.tensor_scalar(pr[:, h % 2, c0:c1], pr[:, h % 2, c0:c1], ri[:, h % 2, j:j + 1], None, ALU.mult)
                    ins.then_inc(pn_r, 1)

                def o_split(g):
                    dve.wait_ge(o_hi, 2 * l + g + 1)
                    a = slice(LT + 2 * g, LT + 2 * g + 2)
                    dve.tensor_tensor(act_lo[:, a, :], bank[6 + g][:].rearrange("p (t n) -> p t n", t=2),
                                      act_hi[:, a, :].bitcast(F32), ALU.subtract).then_inc(o_lo, 1)

                def lru_part(i):
                    if i == 0:
                        dve.wait_ge(sq_r, l + 1)
                        step(dve.tensor_scalar(tr[:], ta[:], -1.0, 1.0, ALU.mult, ALU.add))
                    elif 1 <= i <= 4:
                        t = i - 1
                        ins = dve.reciprocal(tr[:, t, :], tr[:, t, :])
                        step(ins)
                        dve.scalar_tensor_tensor(out=ta[:, t, :], in0=ta[:, t, :], scalar=1.0, in1=tr[:, t, :], op0=ALU.add, op1=ALU.mult)
                        ins = dve.tensor_tensor(ts[:, t, :], ts[:, t, :], tr[:, t, :], ALU.mult)
                        step(ins)
                        if t == LT - 1:
                            step(dve.memset(ts[:, :, 0:1], 0.5))
                            dve.wait_ge(iw_r, l + 1)
                    elif i == 5:
                        step(dve.tensor_tensor(tb[:], tb[:], ts[:], ALU.mult))
                    elif i == 6:
                        for t in range(LT):
                            ins = dve.tensor_tensor_scan(ts[:, t, :], ta[:, t, :], tb[:, t, :], 0.0, ALU.mult, ALU.add)
                        step(ins)
                        dve.wait_ge(gg_r, l + 1)
                        dve.scalar_tensor_tensor(out=ts[:], in0=ts[:], scalar=0.5, in1=gg[:], op0=ALU.mult, op1=ALU.mult).then_inc(lru_o, 1)

                for i in range(N_HEADS + 3):
                    if 1 <= i <= N_HEADS:
                        mask_max(i - 1)
                    if 1 <= i <= 7:
                        lru_part(i - 1)
                    if 1 <= i <= N_HEADS:
                        normalise(i - 1)
                    if i == 3:
                        lo(first, 8)
                        lo(first, 9)
                    if i == 7:
                        o_split(0)
                dve.wait_ge(lru_hi, l + 1)
                dve.tensor_tensor(act_lo[:, 0:LT, :], ts[:], act_hi[:, 0:LT, :].bitcast(F32), ALU.subtract).then_inc(lru_lo, 1)
                lo(first, 10)
                o_split(1)
                lo(first, 11)
                dve.wait_ge(used, first + MIX_CHUNKS)
                for b in range(NB):
                    for j in range(2):
                        ins = dve.tensor_tensor(xs[:, b, 512 * j:512 * j + 512], xs[:, b, 512 * j:512 * j + 512], bank[2 * b + j][:], ALU.add)
                ins.then_inc(mix_r, 1)
                norm(2 * l + 1)
                if l == 0:
                    f0 = FIRST["dense", 0]
                    lo(f0, 0)
                    lo(f0, 1)
                    norm_split(1, 16)
                    ffn(vec_unit_ops(dve, NB, 0), DENSE_UNITS, lambda c: lo(f0, c), 2)
                    dve.wait_ge(used, FIRST["mix", 1])
                    for b in range(NB):
                        for j in range(2):
                            ins = dve.tensor_tensor(xs[:, b, 512 * j:512 * j + 512], xs[:, b, 512 * j:512 * j + 512], bank[2 * b + j][:], ALU.add)
                    ins.then_inc(y_r, 1)

            dve.wait_ge(rw_h, 1)
            dve.tensor_tensor(rw_lo, rw, rw_hi.bitcast(F32), ALU.subtract).then_inc(rw_r, 1)
            norm_split(3, 24)
            dve.wait_ge(lg_p, 1)
            step(dve.tensor_copy(lg, bank[0][:, 0:NB * E].rearrange("p (b e) -> p b e", b=NB)))
            for b in range(NB):
                ins = dve.max(top[:, b, :], lg[:, b, :])
            step(ins)
            dve.tensor_tensor(dif[:].unsqueeze(2), top[:, :, 0:1], top[:, :, 1:2], ALU.subtract).then_inc(lg_r, 1)
            for b in range(NB):
                ins = dve.max_index(topi[:, b, :], top[:, b, :], lg[:, b, :])
            step(ins)
            step(dve.tensor_copy(topf, topi))
            for b in range(NB):
                for k in range(TOP_K):
                    ins = dve.tensor_scalar(oh[:, k, b, :], i8[:], topf[:, b, k:k + 1], None, ALU.is_equal)
            step(ins)
            dve.tensor_tensor(pick, oh[:, 0], oh[:, 1], ALU.add).then_inc(pick_r, 1)
            dve.wait_ge(tw_r, 1)
            dve.tensor_scalar(tw[:, 1, :], tw[:, 0, :], -0.5, 0.5, ALU.mult, ALU.add).then_inc(tw_r, 1)
            dve.wait_ge(tw_r, 2)
            step(dve.tensor_scalar(tw[:, 0, :], tw[:, 0, :], 0.5, 0.5, ALU.mult, ALU.add))
            for b in range(NB):
                ins = dve.tensor_scalar(gates[:, b, :], oh[:, 0, b, :], tw[:, 0, b:b + 1], None, ALU.mult)
            step(ins)
            for b in range(NB):
                ins = dve.scalar_tensor_tensor(out=gates[:, b, :], in0=oh[:, 1, b, :], scalar=tw[:, 1, b:b + 1], in1=gates[:, b, :],
                                               op0=ALU.mult, op1=ALU.add)
            step(ins)
            dve.wait_ge(place_p, 1)
            step(dve.scalar_tensor_tensor(out=place, in0=bank[1][:, 0:NB * E].rearrange("p (b e) -> p b e", b=NB), scalar=1.0,
                                          in1=pick, op0=ALU.add, op1=ALU.mult))
            step(dve.tensor_scalar(place, place, -1.0, None, ALU.add))
            over, upto, idx, hit = (jb[:, k, :] for k in range(4))
            step(dve.tensor_scalar(over, bank[1][0:1, NB * E:(NB + 1) * E], P + 0.5, None, ALU.is_gt))
            step(dve.tensor_tensor_scan(upto, over, over, 0.0, ALU.add, ALU.max))
            step(dve.memset(jf[:], 0.0))
            step(dve.tensor_copy(jf[:, 0:1], upto[:, E - 1:E]))
            for j in range(3):
                step(dve.tensor_scalar(idx, upto, float(j + 1), None, ALU.is_equal))
                step(dve.tensor_tensor(idx, idx, over, ALU.mult))
                step(dve.tensor_tensor(hit, idx, i8[0:1, :], ALU.mult))
                step(dve.tensor_reduce(jf[:, j + 1:j + 2], hit, AX, ALU.add))
            dve.tensor_copy(jobs[:], jf[:]).then_inc(jobs_r, 1)
            dve.wait_ge(grow_in, 16)
            for b in range(NB):
                ins = dve.tensor_tensor(xn[:, b, :], xn[:, b, :], grow, ALU.mult)
            ins.then_inc(xg_r, 1)

            def job(i, e, slots):
                for b in range(NB):
                    dve.tensor_copy(cur[:, 0, b:b + 1], place[:, b, bass.ds(e, 1)])
                    ins = dve.tensor_copy(cur[:, 1, b:b + 1], gates[:, b, bass.ds(e, 1)])
                ins.then_inc(cur_r, 1)
                dve.wait_ge(cur_r, i + 1)
                for b in range(NB):
                    dve.tensor_scalar(sel_s[:, b, :], slots, cur[:, 0, b:b + 1], None, ALU.is_equal)
                    ins = dve.tensor_scalar(sel_g[:, b, :], slots, cur[:, 0, b:b + 1], cur[:, 1, b:b + 1], ALU.is_equal, ALU.mult)
                ins.then_inc(sel_r, 1)
                lo(EXPERT0, 0, i=i)
                lo(EXPERT0, 1, i=i)
                dve.wait_ge(xg_hi, i + 1)
                for j in range(2):
                    a = slice(4 * j, 4 * j + 4)
                    ins = dve.tensor_tensor(act_lo[:, a, 0:P], bank[j][:].rearrange("p (k n) -> p k n", k=4),
                                            act_hi[:, a, 0:P].bitcast(F32), ALU.subtract)
                ins.then_inc(xg_lo, 1)
                ffn(vec_unit_ops(dve, 1, DENSE_U + UNITS * i), UNITS, lambda c: lo(EXPERT0, c, i=i), 2)
                for b in range(NB):
                    for j in range(2):
                        dve.wait_ge(sc_p, 4 * i + 2 * b + j + 1)
                        dve.tensor_tensor(xs[:, b, 512 * j:512 * j + 512], xs[:, b, 512 * j:512 * j + 512], bank[j][:],
                                          ALU.add).then_inc(sc_r, 1)

            dve.wait_ge(consts, 2)
            with dve.Fori(0, E) as i:
                job(i, i, slot)
            more = dve.value_load(jobs[0:1, 0:1], min_val=0, max_val=3)
            with dve.If(more > 0):
                with dve.Fori(E, E + more) as i:
                    e = dve.value_load(jobs[0:1, bass.ds(i - (E - 1), 1)], min_val=0, max_val=E - 1)
                    job(i, e, slot2)
            norm(2 * DEPTH)
            dve.wait_ge(grow_in, 32)
            dve.wait_ge(xn_v, 2 * DEPTH + 1)
            dve.wait_ge(xn_a, 2 * DEPTH + 1)
            for b in range(NB):
                dve.tensor_tensor(xn[:, b, :], xn[:, b, :], grow, ALU.mult).then_inc(out_r, 1)

        @block.tensor
        def _(pe):
            def chunk(first, c, i=0):
                pe.wait_ge(lo_made, nth(first, c, i) + 1)
                return split_slot(first, c)

            def three(o, a_h, a_l, b_h, b_l, start, stop, **k):
                pe.matmul(o, a_l, b_h, start=start, stop=False, **k)
                pe.matmul(o, a_h, b_l, start=False, stop=False, **k)
                return pe.matmul(o, a_h, b_h, start=False, stop=stop, **k)

            def ffn_products(nb, units, order, first, u0, i):
                y0 = 0 if nb == 2 else 2

                def gate_up(s):
                    for b in range(nb):
                        if nb == 2 and s:
                            pe.wait_ge(hid_r, u0 + nb * (s - 1) + b + 1)
                        if nb == 1 and s != 1:
                            pe.wait_ge(hid_r, u0 + max(s - 1, 0))
                    for k in range(2):
                        c = order.index(("gu", s, k))
                        sl = chunk(first, c, i)
                        for b in range(nb):
                            o = bank[4 + (b if nb == 2 else s % 2)]
                            m = slice(b * P, (b + 1) * P)
                            for kk in range(4):
                                kt = 4 * k + kk
                                n = slice(kk * 2 * FW, (kk + 1) * 2 * FW)
                                ins = three(o[:], act_hi[:, kt, m], act_lo[:, kt, m], w_hi[:, sl, n], w_lo[:, sl, n],
                                            start=(kt == 0), stop=(kt == KT - 1))
                            if b == nb - 1:
                                ins.then_inc(used, 1)
                            elif k == 1:
                                ins.then_inc(gu_p, 1)

                def turn(s):
                    for b in range(nb):
                        u = u0 + nb * s + b
                        o = b if nb == 2 else s % 2
                        pe.wait_ge(hid_r, u + 1)
                        if nb == 2 and s:
                            pe.wait_ge(hT_lo, u - nb + 1)
                        if nb == 1 and s != 1:
                            pe.wait_ge(hT_lo, u0 + max(s - 1, 0))
                        h = hid[:, o, :].rearrange("p (n j) -> p j n", j=2)
                        for j in range(2):
                            ins = pe.transpose(bank[6 + o][:, j * P:(j + 1) * P], h[:, j, :], ident[:])
                        ins.then_inc(hT_p, 1)

                def down(s):
                    sl = chunk(first, order.index(("down", s, 0)), i)
                    for b in range(nb):
                        pe.wait_ge(hT_lo, u0 + nb * s + b + 1)
                        for j in range(2):
                            m = slice(j * P, (j + 1) * P)
                            for n in range(2):
                                w = slice(j * D + 512 * n, j * D + 512 * (n + 1))
                                ins = three(bank[y0 + 2 * b + n][:], sm_hi[:, s % SLOTS, b, m], sm_lo[:, s % SLOTS, b, m],
                                            w_hi[:, sl, w], w_lo[:, sl, w], start=(s == 0 and j == 0),
                                            stop=(s == units - 1 and j == 1))
                    ins.then_inc(used, 1)

                for s in range(units + 2):
                    if s < units:
                        gate_up(s)
                    if 1 <= s <= units:
                        turn(s - 1)
                    if s >= 2:
                        down(s - 2)

            def norm_turn(k):
                pe.wait_ge(xn_a, k + 1)
                pe.wait_ge(xn_v, k + 1)
                for kt in range(KT):
                    for b in range(NB):
                        c = (kt % 2) * SEQ + b * P
                        ins = pe.transpose(bank[4 * (k % 2) + kt // 2][:, c:c + P], xn[:, b, kt * P:(kt + 1) * P], ident[:])
                    if kt % 2:
                        ins.then_inc(nT, 1)

            pe.wait_ge(consts, 1)
            pe.wait_ge(rows_in, 16 * 9)
            pe.transpose(bank[0][:, 0:102], rows, ident[0:102, 0:102]).then_inc(prm_t, 1)
            pe.wait_ge(prm_r, 1)

            for l in range(DEPTH):
                first = FIRST["mix", l]
                norm_turn(2 * l)
                pe.wait_ge(nT_lo, 8 * l + 4)
                for w in range(2):
                    for k in range(2):
                        c = 2 * w + k
                        s = chunk(first, c)
                        wh = w_hi[:, s, :].rearrange("p (k n) -> p k n", k=4)
                        wl = w_lo[:, s, :].rearrange("p (k n) -> p k n", k=4)
                        for kk in range(4):
                            kt = 4 * k + kk
                            for t in range(LT):
                                o = bank[4 + 2 * w + t // 2][:, (t % 2) * SEQ:(t % 2 + 1) * SEQ]
                                m = slice(t * P, (t + 1) * P)
                                ins = three(o, wh[:, kk, m], wl[:, kk, m], act_hi[:, kt, :], act_lo[:, kt, :],
                                            start=(kt == 0 and t % 2 == 0), stop=(kt == KT - 1), skip_group_check=True)
                        ins.then_inc(used, 1)
                for k in range(2):
                    s = chunk(first, 4 + k)
                    wh = w_hi[:, s, 0:4 * ZT].rearrange("p (k n) -> p k n", k=4)
                    wl = w_lo[:, s, 0:4 * ZT].rearrange("p (k n) -> p k n", k=4)
                    for kk in range(4):
                        kt = 4 * k + kk
                        for b in range(NB):
                            m = slice(b * P, (b + 1) * P)
                            ins = three(bank[b][:, 0:ZT], act_hi[:, kt, m], act_lo[:, kt, m], wh[:, kk, :], wl[:, kk, :],
                                        start=(kt == 0), stop=(kt == KT - 1))
                    ins.then_inc(used, 1)
                pe.wait_ge(cn_r, l + 1)
                for t in range(CT):
                    for b in range(NB):
                        c = (t % 2) * SEQ + b * P
                        ins = pe.transpose(bank[2 + t // 2][:, c:c + P], cn[:, b, t * P:(t + 1) * P], ident[:])
                ins.then_inc(cT, 1)
                pe.wait_ge(cT_lo, l + 1)
                pe.wait_ge(xl_r, l + 1)
                QT = QL // P
                s = chunk(first, 6)
                wh = w_hi[:, s, 0:QT * N_HEADS * QK].rearrange("p (k n) -> p k n", k=QT)
                wl = w_lo[:, s, 0:QT * N_HEADS * QK].rearrange("p (k n) -> p k n", k=QT)
                for b in range(NB):
                    m = slice(b * P, (b + 1) * P)
                    for j in range(2):
                        n = slice(j * 4 * QK, (j + 1) * 4 * QK)
                        for kt in range(QT):
                            ins = three(bank[2 + 2 * b + j][:, 0:4 * QK], c_hi[:, kt, m], c_lo[:, kt, m], wh[:, kt, n], wl[:, kt, n],
                                        start=(kt == 0), stop=(kt == QT - 1))
                ins.then_inc(used, 1)
                pe.wait_ge(yg_r, l + 1)
                pe.wait_ge(kr_r, l + 1)
                s = chunk(first, 7)
                for b in range(NB):
                    m = slice(b * P, (b + 1) * P)
                    for j in range(2):
                        n = slice(j * 512, (j + 1) * 512)
                        ins = three(bank[6 - 6 * b + j][:], c_hi[:, QT, m], c_lo[:, QT, m], w_hi[:, s, n], w_lo[:, s, n],
                                    start=True, stop=True)
                ins.then_inc(used, 1)
                pe.wait_ge(xc_r, l + 1)
                pe.wait_ge(bd_in, 64 * (l + 1))
                pe.wait_ge(q_c, NB * (l + 1))
                for w in range(2):
                    for t in range(LT):
                        ins = pe.matmul(bank[2 + 2 * w + t // 2][:, (t % 2) * SEQ:(t % 2 + 1) * SEQ], gate_bd[:, w, t, :],
                                        xc[:, t, :], start=True, stop=True)
                ins.then_inc(gate_p, 1)

                def qk_turn(h):
                    n = N_HEADS * l + h
                    if n >= 2:
                        pe.wait_ge(qkT_r, n - 1)
                    for b in range(NB):
                        pe.transpose(bank[h % 2][0:QK, b * P:(b + 1) * P], qcat[:, b, h, :], ident[:])
                    for b in range(NB):
                        ins = pe.transpose(bank[h % 2][0:QK, SEQ + b * P:SEQ + (b + 1) * P], kcat[:, b, h, :], ident[:])
                    ins.then_inc(qkT_p, 1)

                def scores(h):
                    n = N_HEADS * l + h
                    pe.wait_ge(qkT_r, n + 1)
                    if n >= 2:
                        pe.wait_ge(s_r, n - 1)
                    t = qkT[:, h % 2, :]
                    pe.matmul(bank[2 + h % 2][:, 0:P], t[:, 0:P], t[:, SEQ:SEQ + P], start=True, stop=True)
                    pe.matmul(bank[2 + h % 2][:, P:3 * P], t[:, P:2 * P], t[:, SEQ:2 * SEQ], start=True, stop=True).then_inc(s_p, 1)

                def p_turn(h):
                    n = N_HEADS * l + h
                    pe.wait_ge(pn_r, n + 1)
                    if n >= 2:
                        pe.wait_ge(pT_r, n - 1)
                    for src, dst in ((0, 0), (P, P), (2 * P, 2 * P)):
                        ins = pe.transpose(bank[4 + h % 2][:, dst:dst + P], pr[:, h % 2, src:src + P], ident[:])
                    ins.then_inc(pT_p, 1)

                def values(h):
                    n = N_HEADS * l + h
                    pe.wait_ge(pT_r, n + 1)
                    r = slice((h % 2) * V_HEAD, (h % 2 + 1) * V_HEAD)
                    c = (h // 2 % 2) * SEQ
                    o = bank[6 + h // 4]
                    pe.matmul(o[r, c:c + SEQ], vv[:, 0, h, :], pT[:, h % 2, 0:SEQ], start=True, stop=False)
                    pe.matmul(o[r, c + P:c + SEQ], vv[:, 1, h, :], pT[:, h % 2, SEQ:], start=False, stop=True).then_inc(o_p, 1)

                pe.wait_ge(q_r, l + 1)
                pe.wait_ge(k_a, l + 1)
                pe.wait_ge(k_v, l + 1)
                pe.wait_ge(kr_c, l + 1)
                pe.wait_ge(gate_t, l + 1)
                for i in range(N_HEADS + 3):
                    if i < N_HEADS:
                        qk_turn(i)
                    if 1 <= i <= N_HEADS:
                        scores(i - 1)
                    if 2 <= i <= N_HEADS + 1:
                        p_turn(i - 2)
                    if i >= 3:
                        values(i - 3)
                pe.wait_ge(lru_lo, l + 1)
                pe.wait_ge(s_r, N_HEADS * (l + 1))
                for c in range(4):
                    if c >= 2:
                        pe.wait_ge(o_lo, 2 * l + c - 1)
                    s = chunk(first, 8 + c)
                    for kk in range(2):
                        kt = 2 * c + kk
                        for b in range(NB):
                            for j in range(2):
                                m, n = slice(b * P, (b + 1) * P), slice(kk * D + 512 * j, kk * D + 512 * (j + 1))
                                ins = three(bank[2 * b + j][:], act_hi[:, kt, m], act_lo[:, kt, m], w_hi[:, s, n], w_lo[:, s, n],
                                            start=(kt == 0), stop=(kt == KT - 1))
                    ins.then_inc(used, 1)
                norm_turn(2 * l + 1)
                pe.wait_ge(nT_lo, 8 * l + 8)
                if l == 0:
                    ffn_products(NB, DENSE_UNITS, DENSE_ORDER, FIRST["dense", 0], 0, 0)

            pe.wait_ge(rw_r, 1)
            for b in range(NB):
                m = slice(b * P, (b + 1) * P)
                for kt in range(KT):
                    ins = three(bank[0][:, b * E:(b + 1) * E], act_hi[:, kt, m], act_lo[:, kt, m], rw_hi[:, kt * E:(kt + 1) * E], rw_lo[:, kt * E:(kt + 1) * E],
                                start=(kt == 0), stop=(kt == KT - 1))
            ins.then_inc(lg_p, 1)
            pe.wait_ge(pick_r, 1)
            pe.wait_ge(consts, 2)
            pe.matmul(bank[1][:, 0:E], before, pick[:, 0, :], start=True, stop=True)
            pe.matmul(bank[1][:, E:2 * E], before, pick[:, 1, :], start=True, stop=False)
            pe.matmul(bank[1][:, E:2 * E], ones, pick[:, 0, :], start=False, stop=True)
            for b in range(NB):
                ins = pe.matmul(bank[1][:, 2 * E:3 * E], ones, pick[:, b, :], start=(b == 0), stop=(b == NB - 1))
            ins.then_inc(place_p, 1)
            pe.wait_ge(xg_r, 1)

            def job(i):
                pe.wait_ge(sel_r, i + 1)
                for kt in range(KT):
                    for b in range(NB):
                        ins = pe.matmul(bank[kt // 4][:, (kt % 4) * P:(kt % 4 + 1) * P], xn[:, b, kt * P:(kt + 1) * P],
                                        sel_s[:, b, :], start=(b == 0), stop=(b == NB - 1))
                ins.then_inc(xg_p, 1)
                for b in range(NB):
                    ins = pe.transpose(bank[7][:, b * P:(b + 1) * P], sel_g[:, b, :], ident[:])
                ins.then_inc(sT_p, 1)
                pe.wait_ge(xg_lo, i + 1)
                pe.wait_ge(sT_r, i + 1)
                ffn_products(1, UNITS, EXPERT_ORDER, EXPERT0, DENSE_U + UNITS * i, i)
                pe.wait_ge(ye_r, i + 1)
                for b in range(NB):
                    for j in range(2):
                        if b:
                            pe.wait_ge(sc_r, 4 * i + j + 1)
                        pe.matmul(bank[j][:], sel_t[:, b, :], ysb[:, 512 * j:512 * (j + 1)], start=True, stop=True).then_inc(sc_p, 1)

            with pe.Fori(0, E) as i:
                job(i)
            pe.wait_ge(jobs_r, 1)
            more = pe.value_load(jobs[0:1, 0:1], min_val=0, max_val=3)
            with pe.If(more > 0):
                with pe.Fori(E, E + more) as i:
                    job(i)


_INS = ['x', 'positions', 'norm_mix', 'w_in', 'conv_w', 'conv_b', 'lru_wa', 'lru_ba', 'lru_wx', 'lru_bx',
        'lru_lambda', 'q_norm', 'w_uq', 'kv_norm', 'w_ukv', 'w_out', 'norm_ffn', 'dense_w_gate',
        'dense_w_up', 'dense_w_down', 'router_w', 'expert_w_gate', 'expert_w_up', 'expert_w_down',
        'norm_final']


def kernel(**inputs):
    import concourse.bacc as _bacc
    from concourse.bass_utils import run_bass_kernel_spmd as _run

    nc = _bacc.Bacc("TRN2", target_bir_lowering=False, num_devices=1)
    arrays, args = {}, []
    for name in _INS:
        a = np.ascontiguousarray(inputs[name])
        arrays[f"in_{name}"] = a
        args.append(nc.dram_tensor(f"in_{name}", a.shape, mybir.dt.from_np(a.dtype), kind="ExternalInput").ap())
    out = nc.dram_tensor("out_x", inputs["x"].shape, F32, kind="ExternalOutput").ap()
    trunk(nc, *args, out)
    return _run(nc, [arrays], core_ids=[0]).results[0]["out_x"]
```

```python
import math
from contextlib import ExitStack

import numpy as np
import concourse.bass as bass
from concourse import mybir

P = 128
BF16 = mybir.dt.bfloat16
F32, F32R, I32, U32 = mybir.dt.float32, mybir.dt.float32r, mybir.dt.int32, mybir.dt.uint32
ALU = mybir.AluOpType
ACT = mybir.ActivationFunctionType
AX = mybir.AxisListType.X

EPS = 1e-6
CONV_W = 4
N_HEADS = 8
QK_NOPE, QK_ROPE, V_HEAD = 64, 32, 64
QK = QK_NOPE + QK_ROPE
HALF = QK_ROPE // 2
ROPE_THETA = 10000.0
TOP_K = 2
LRU_C = 8.0

RAW = 7
SPLIT = 3
CHUNK = 2048
FW = 256
MASKED = -1e30


def trunk(nc, x, positions, norm_mix, w_in, conv_w, conv_b, lru_wa, lru_ba, lru_wx, lru_bx,
          lru_lambda, q_norm, w_uq, kv_norm, w_ukv, w_out, norm_ffn, dense_w_gate, dense_w_up,
          dense_w_down, router_w, expert_w_gate, expert_w_up, expert_w_down, norm_final, out):
    DEPTH, D, IN_COLS = w_in.shape
    SEQ = x.shape[1]
    NB = SEQ // P
    KT = D // P
    LW = conv_w.shape[2]
    LT = LW // P
    QL, KVL = w_uq.shape[1], w_ukv.shape[1]
    CT = (QL + KVL) // P
    ZT = IN_COLS - 2 * LW
    E = expert_w_gate.shape[1]
    DENSE_UNITS = dense_w_gate.shape[2] // FW
    UNITS = expert_w_gate.shape[3] // FW
    SCALE = 1.0 / math.sqrt(QK)
    MORE = (NB * P * TOP_K) // (P + 1)
    JOBS = E + MORE
    assert NB == 2 and DEPTH == 2 and KT == 8 and LT == 4 and UNITS == 7 and SEQ == 256

    MIX_CHUNKS = 12

    def ffn_order(units):
        order = []
        for s in range(units + 2):
            if s < units:
                order += [("gu", s, 0), ("gu", s, 1)]
            if s >= 2:
                order.append(("down", s - 2, 0))
        return order

    DENSE_ORDER = ffn_order(DENSE_UNITS)
    EXPERT_ORDER = ffn_order(UNITS)
    FIRST = {("mix", 0): 0, ("dense", 0): MIX_CHUNKS,
             ("mix", 1): MIX_CHUNKS + len(DENSE_ORDER)}
    EXPERT0 = FIRST["mix", 1] + MIX_CHUNKS
    PER_JOB = len(EXPERT_ORDER)
    assert PER_JOB % RAW == 0 and PER_JOB % SPLIT == 0
    DENSE_U = DENSE_UNITS * NB
    SLOTS = 3

    ctx = ExitStack()
    with ctx:
        def sb(name, shape, dt=F32):
            return ctx.enter_context(nc.sbuf_tensor(name, shape, dt))

        def sem(name):
            return ctx.enter_context(nc.semaphore(name))

        raw = sb("raw", [P, RAW, CHUNK])
        w_hi = sb("w_hi", [P, SPLIT, CHUNK], F32R)
        w_lo = sb("w_lo", [P, SPLIT, CHUNK], F32R)
        xs = sb("xs", [P, NB, D])
        xn = sb("xn", [P, NB, D])
        act_hi = sb("act_hi", [P, KT, SEQ], F32R)
        act_lo = sb("act_lo", [P, KT, SEQ], F32R)
        sm_hi = sb("sm_hi", [P, SLOTS, NB, FW], F32R)
        sm_lo = sb("sm_lo", [P, SLOTS, NB, FW], F32R)
        c_hi = sm_hi[:, :, 0, :]
        c_lo = sm_lo[:, :, 0, :]
        xc = sb("xc", [P, LT, SEQ])
        yg = sb("yg", [P, LT, SEQ])
        gg = sb("gg", [P, LT, SEQ])
        mixer_base = nc.sbuf_base
        xl = sb("xl", [P, LT, CONV_W - 1 + SEQ])
        ta = sb("ta", [P, LT, SEQ])
        tb = sb("tb", [P, LT, SEQ])
        tr = sb("tr", [P, LT, SEQ])
        ts = sb("ts", [P, LT, SEQ])
        kcat = sb("kcat", [P, NB, N_HEADS, QK])
        vv = sb("vv", [P, NB, N_HEADS, V_HEAD])
        cn = tr[:, 0:CT, :].rearrange("p t n -> p (t n)").rearrange("p (b n) -> p b n", b=NB)
        qcat = xn[:, :, 0:N_HEADS * QK].rearrange("p b (h d) -> p b h d", h=N_HEADS)
        qkT = sb("qkT", [QK, 2, 2 * SEQ])
        pr = sb("pr", [P, 2, 3 * P])
        pT = sb("pT", [P, 2, 3 * P])
        rope_a, rope_b = (pr[:, k, 0:N_HEADS * QK_ROPE].rearrange("p (h d) -> p h d", h=N_HEADS) for k in range(2))
        kr = sb("kr", [P, NB, QK_ROPE])
        gate_bd = sb("gate_bd", [P, 2, LT, P])
        mixer_end = nc.sbuf_base
        ident = sb("ident", [P, P])
        mask = sb("mask", [P, 3 * P])
        rows = yg[0:102, 3, 0:P]
        prm = sb("prm", [P, 102])
        lru_c = sb("lru_c", [P, 4, DEPTH * LT])
        pos_i = sb("pos_i", [P, NB], I32)
        pos_f = sb("pos_f", [P, NB])
        inv = sb("inv", [P, HALF])
        ang = yg[:, 0, 0:NB * HALF].rearrange("p (b n) -> p b n", b=NB)
        turn = yg[:, 1, 0:2 * NB * HALF].rearrange("p (w b n) -> p w b n", w=2, b=NB)
        trig_in = yg[:, 2, 0:2 * NB * HALF].rearrange("p (w b n) -> p w b n", w=2, b=NB)
        trig = sb("trig", [P, 2, NB, HALF])
        ssq = sb("ssq", [P, NB])
        mean = sb("mean", [P, NB])
        rstd = sb("rstd", [P, NB])
        zssq = sb("zssq", [P, 2, NB])
        zmean = sb("zmean", [P, 2, NB])
        zrstd = sb("zrstd", [P, 2, NB])
        mhalf = sb("mhalf", [P, 4])
        mx = sb("mx", [P, 2, 2])
        nmx = sb("nmx", [P, 2, 2])
        rs = sb("rs", [P, 2, 2])
        ri = sb("ri", [P, 2, 2])
        grow = xc[:, :, :].rearrange("p t n -> p (t n)")
        sg = yg[:, 0:2, :]
        hid = yg[:, 2:4, :]
        expert_at = [mixer_base]

        def over(name, shape, dt=F32R):
            at = (expert_at[0] + 31) // 32 * 32
            expert_at[0] = at + (2 if dt == BF16 else 4) * int(np.prod(shape[1:]))
            assert expert_at[0] <= mixer_end
            return nc.alloc_sbuf_tensor_at(name, shape, dt, offset=at)

        y_hi, y_lo = over("y_hi", [P, D]), over("y_lo", [P, D])
        sel_t = over("sel_t", [P, NB, P])
        xg = [over(f"xg{k}", [P, NB, D], BF16) for k in range(3)]
        sel = over("sel", [P, NB, P], BF16)
        xgain = over("xgain", [P, NB, D], F32)
        wide = over("wide", [P, 2, MORE, NB, E], F32)
        lgT = nc.alloc_sbuf_tensor_at("lgT", [E, SEQ], F32, offset=(expert_at[0] + 31) // 32 * 32)
        expert_at[0] = (expert_at[0] + 31) // 32 * 32 + 4 * SEQ
        cur = over("cur", [P, 2, NB], F32)
        ident_b = over("ident_b", [P, P], BF16)
        before = gg[:, 0, 0:P]
        ones = gg[:, 0, P:2 * P]
        slot = gg[:, 1, 0:P]
        rw = gg[:, 3, 0:KT * E]
        rw_hi, rw_lo = (w[:, 0, 1, 0:KT * E] for w in (sm_hi, sm_lo))
        lg, top, topi, topf = (gg[:, 2, 16 * k:16 * k + 16].rearrange("p (b e) -> p b e", b=NB) for k in range(4))
        topi = topi.bitcast(U32)
        oh = gg[:, 2, 64:64 + 2 * NB * E].rearrange("p (k b e) -> p k b e", k=2, b=NB)
        pick = gg[:, 3, 64:80].rearrange("p (b e) -> p b e", b=NB)
        gates, place = (gg[:, 3, 80 + NB * JOBS * k:80 + NB * JOBS * (k + 1)].rearrange("p (b e) -> p b e", b=NB) for k in range(2))
        i8 = sb("i8", [P, E])
        dif = sb("dif", [P, NB])
        tw = sb("tw", [P, 2, NB])
        jb = gg[:, 3, 160:160 + 8 * E].rearrange("p (k e) -> p k e", k=8)
        jf = sb("jf", [1, 4])
        jobs = sb("jobs", [1, 4], I32)

        bank = [ctx.enter_context(nc.psum_tensor(f"bank{i}", [P, 512], F32)) for i in range(8)]

        landed = [sem(f"landed{i}") for i in range(RAW)]
        hi_made, lo_made = sem("hi_made"), sem("lo_made")
        used = sem("used")
        x_in = [sem(f"x_in{b}") for b in range(NB)]
        rows_in, pos_in, rw_in, wout_s = sem("rows_in"), sem("pos_in"), sem("rw_in"), sem("stored")
        bd_in, grow_in = sem("bd_in"), sem("grow_in")
        bd_zero, consts = sem("bd_zero"), sem("consts")
        prm_t, prm_r = sem("prm_t"), sem("prm_r")
        lam_e, lru_r = sem("lam_e"), sem("lru_r")
        angle_r, trig_r = sem("angle_r"), sem("trig_r")
        ss_r, rstd_r, xn_a, xn_v = sem("ss_r"), sem("rstd_r"), sem("xn_a"), sem("xn_v")
        nT, nT_hi, nT_lo = sem("nT"), sem("nT_hi"), sem("nT_lo")
        xl_r, yg_r = sem("xl_r"), sem("yg_r")
        zss_r, zrstd_r, cn_r, kr_r, kr_c = sem("zss_r"), sem("zrstd_r"), sem("cn_r"), sem("kr_r"), sem("kr_c")
        cT, cT_hi, cT_lo = sem("cT"), sem("cT_hi"), sem("cT_lo")
        q_c, q_r, k_r, v_r = sem("q_c"), sem("q_r"), sem("k_r"), sem("v_r")
        xc_r, gate_p, gate_t = sem("xc_r"), sem("gate_p"), sem("gate_t")
        decay_r, a_r = sem("decay_r"), sem("a_r")
        sq_r, gin_r, gth_r, gg_r, iw_r = sem("sq_r"), sem("gin_r"), sem("gth_r"), sem("gg_r"), sem("iw_r")
        lru_o, lru_lo = sem("lru_o"), sem("lru_lo")
        qkT_p, qkT_r, s_p, s_r, p_r, pn_r, pT_p, pT_r, o_p, o_hi, o_lo = (
            sem("qkT_p"), sem("qkT_r"), sem("s_p"), sem("s_r"), sem("p_r"), sem("pn_r"), sem("pT_p"),
            sem("pT_r"), sem("o_p"), sem("o_hi"), sem("o_lo"))
        mix_r, first_rows = sem("mix_r"), sem("first_rows")
        gu_p, sg_r, hid_r, hT_p, hT_hi, hT_lo = (
            sem("gu_p"), sem("sg_r"), sem("hid_r"), sem("hT_p"), sem("hT_hi"), sem("hT_lo"))
        y_r = sem("y_r")
        rw_h, rw_r, lg_p, lg_r, tw_r, pick_r, place_p, jobs_r, xg_r, lgT_r = (
            sem("rw_h"), sem("rw_r"), sem("lg_p"), sem("lg_r"), sem("tw_r"), sem("pick_r"),
            sem("place_p"), sem("jobs_r"), sem("xg_r"), sem("lgT_r"))
        sel_r, xT_p, xT_hi, xT_lo, sT_p, sT_r, yg_hi, yg_lo, sc_p, sc_r, xg_a, xg_v, cur_r, gate_r = (
            sem("sel_r"), sem("xT_p"), sem("xT_hi"), sem("xT_lo"), sem("sT_p"), sem("sT_r"),
            sem("yg_hi"), sem("yg_lo"), sem("sc_p"), sem("sc_r"), sem("xg_a"), sem("xg_v"), sem("cur_r"), sem("gate_r"))
        out_r = sem("out_r")
        a_ch, v_ch, g_ch = sem("scalar_step"), sem("vector_step"), sem("pool_step")

        def stepper(eng, s):
            n = [0]

            def step(*ins):
                n[0] += 1
                ins[-1].then_inc(s, 1)
                eng.wait_ge(s, n[0])
            return step

        def raw_slot(first, c):
            return (first + c) % RAW

        def raw_turn(first, c, i=0):
            return (first + c) // RAW + 1 + i * (PER_JOB // RAW)

        def split_slot(first, c):
            return (first + c) % SPLIT

        def nth(first, c, i=0):
            return first + c + i * PER_JOB

        def by_tile(w):
            return w.rearrange("(k p) n -> p k n", p=P)

        def mix_sources(l):
            win, wout = by_tile(w_in[l]), by_tile(w_out[l])
            for c0, wd, k in ((2 * LW, ZT, 0), (2 * LW, ZT, 4), (0, LW, 0), (0, LW, 4), (LW, LW, 0)):
                yield wd, 4, win[:, k:k + 4, c0:c0 + wd]
            yield N_HEADS * QK, QL // P, by_tile(w_uq[l])
            yield LW, 4, win[:, 4:8, LW:2 * LW]
            yield w_ukv.shape[2], KVL // P, by_tile(w_ukv[l])
            for k in range(0, KT, 2):
                yield D, 2, wout[:, k:k + 2, :]

        def load_ffn(eng, order, first, gate, up, down, i=0):
            g, u = by_tile(gate), by_tile(up)
            d = down.rearrange("(s p j) n -> s p (j n)", p=P, j=2)
            for c, (kind, s, k) in enumerate(order):
                r = raw[:, raw_slot(first, c), :]
                eng.wait_ge(lo_made, nth(first, c, i) - RAW + 1)
                if kind == "gu":
                    dst = r.rearrange("p (k w n) -> p k w n", k=4, w=2)
                    for w, src in enumerate((g, u)):
                        eng.dma_start(dst[:, :, w, :], src[:, 4 * k:4 * k + 4, s * FW:(s + 1) * FW]
                                      ).then_inc(landed[raw_slot(first, c)], 16)
                else:
                    for j in range(2):
                        h = slice(j * CHUNK // 2, (j + 1) * CHUNK // 2)
                        eng.dma_start(r[:, h], d[s][:, h]).then_inc(landed[raw_slot(first, c)], 16)

        def ffn(ops, units, chunk):
            finish, turned = ops
            c = 2
            for s in range(units + 1):
                if s >= 2:
                    chunk(c)
                    c += 1
                if s + 1 < units:
                    chunk(c)
                    c += 1
                if s < 2:
                    chunk(c)
                    c += 1
                if s >= 1:
                    turned(s - 1)
                if s < units:
                    finish(s)
                if s >= 2 and s + 1 < units:
                    chunk(c)
                    c += 1
            chunk(c)

        def job_start(ops, chunk, outputs, scattered):
            finish, turned = ops
            chunk(1)
            outputs()
            chunk(2)
            chunk(3)
            finish(0)
            chunk(4)
            chunk(5)
            turned(0)
            finish(1)
            chunk(6)
            scattered()

        def job_rest(ops, chunk, matrix, gathered, next_chunk):
            finish, turned = ops
            chunk(7)
            turned(1)
            chunk(8)
            for s in range(3, UNITS):
                finish(s - 1)
                chunk(3 * s)
                chunk(3 * s + 1)
                turned(s - 1)
                if s == UNITS - 1:
                    finish(s)
                if s == 4:
                    matrix()
                chunk(3 * s + 2)
            next_chunk()
            turned(UNITS - 1)
            gathered()

        def act_unit_ops(act, nb, u0, gu_done):
            def finish(s):
                for b in range(nb):
                    if b < nb - 1:
                        act.wait_ge(gu_p, s + 1)
                    else:
                        act.wait_ge(used, gu_done(s))
                    o = b if nb == 2 else s % 2
                    act.activation(sg[:, o, :], bank[4 + o][:, 0:FW], ACT.Silu).then_inc(sg_r, 1)

            def turned(s):
                for b in range(nb):
                    act.wait_ge(hT_p, u0 + nb * s + b + 1)
                    o = b if nb == 2 else s % 2
                    act.activation(sm_hi[:, s % SLOTS, b, :], bank[6 + o][:, 0:FW], ACT.Copy).then_inc(hT_hi, 1)
            return finish, turned

        def vec_unit_ops(dve, nb, u0):
            def finish(s):
                for b in range(nb):
                    dve.wait_ge(sg_r, u0 + nb * s + b + 1)
                    o = b if nb == 2 else s % 2
                    dve.tensor_tensor(hid[:, o, :], sg[:, o, :], bank[4 + o][:, FW:2 * FW], ALU.mult).then_inc(hid_r, 1)

            def turned(s):
                for b in range(nb):
                    dve.wait_ge(hT_hi, u0 + nb * s + b + 1)
                    o = b if nb == 2 else s % 2
                    dve.tensor_tensor(sm_lo[:, s % SLOTS, b, :], bank[6 + o][:, 0:FW],
                                      sm_hi[:, s % SLOTS, b, :].bitcast(F32), ALU.subtract).then_inc(hT_lo, 1)
            return finish, turned

        block = ctx.enter_context(nc.Block())

        @block.sync
        def _(sp):
            for b in range(NB):
                sp.dma_start(xs[:, b, :], x[0, b * P:(b + 1) * P, :]).then_inc(x_in[b], 16)
            def load_mix(l, c0, c1):
                first = FIRST["mix", l]
                for c, (wd, k, src) in tuple(enumerate(mix_sources(l)))[c0:c1]:
                    if first + c >= RAW:
                        sp.wait_ge(lo_made, first + c - RAW + 1)
                    s = raw_slot(first, c)
                    dst = raw[:, s, 0:k * wd].rearrange("p (k n) -> p k n", k=k)
                    for j in range(2):
                        ks, ns = ((slice(j * k // 2, (j + 1) * k // 2), slice(0, wd)) if k > 1 else
                                  (slice(0, 1), slice(j * wd // 2, (j + 1) * wd // 2)))
                        sp.dma_start(dst[:, ks, ns], src[:, ks, ns]).then_inc(landed[s], 16)

            def load_gates(l):
                for w, src in enumerate((lru_wa, lru_wx)):
                    for q in range(2):
                        sp.dma_start(gate_bd[64 * q:64 * q + 64, w, :, 64 * q:64 * q + 64],
                                     src[l].rearrange("(t q) c d -> q c t d", q=2)[q]).then_inc(bd_in, 16)

            load_mix(0, 0, 1)
            r0 = 0
            for v in (norm_mix.rearrange("l (k p) -> (l k) p", p=P),
                      norm_ffn.rearrange("l (k p) -> (l k) p", p=P),
                      conv_w.rearrange("l j (t p) -> (l j t) p", p=P),
                      conv_b.rearrange("l (t p) -> (l t) p", p=P),
                      lru_ba.rearrange("l (t q) c -> (l t) (q c)", q=2),
                      lru_bx.rearrange("l (t q) c -> (l t) (q c)", q=2),
                      lru_lambda.rearrange("l (t p) -> (l t) p", p=P),
                      q_norm.rearrange("l (k p) -> (l k) p", p=P),
                      kv_norm.rearrange("l (k p) -> (l k) p", p=P)):
                sp.dma_start(rows[r0:r0 + v.shape[0], :], v).then_inc(rows_in, 16)
                r0 += v.shape[0]
            sp.dma_start(pos_i[:, :], positions.rearrange("o (b p) -> p (o b)", p=P),
                         allow_slow_non_contiguous=True).then_inc(pos_in, 16)
            load_mix(0, 1, 4)
            sp.wait_ge(bd_zero, 1)
            load_gates(0)
            load_mix(0, 4, MIX_CHUNKS)
            sp.wait_ge(gate_p, 2)
            load_gates(1)
            load_ffn(sp, DENSE_ORDER, FIRST["dense", 0], dense_w_gate[0], dense_w_up[0], dense_w_down[0])
            load_mix(1, 0, MIX_CHUNKS)

            def job(i, e):
                load_ffn(sp, EXPERT_ORDER, EXPERT0, *(w[0, bass.ds(e, 1)].rearrange("o a b -> (o a) b")
                                                      for w in (expert_w_gate, expert_w_up, expert_w_down)), i=i)

            with sp.Fori(0, E) as i:
                job(i, i)
            sp.wait_ge(jobs_r, 1)
            last = sp.value_load(jobs[0:1, 0:1], min_val=E - 1, max_val=E - 1 + MORE)
            with sp.If(last > E - 1):
                with sp.Fori(E, last + 1) as i:
                    e = sp.value_load(jobs[0:1, bass.ds(i - (E - 1), 1)], min_val=0, max_val=E - 1)
                    job(i, e)
            for b in range(NB):
                sp.wait_ge(out_r, b + 1)
                sp.dma_start(out[0, b * P:(b + 1) * P, :], xn[:, b, :]).then_inc(wout_s, 16)
            sp.wait_ge(wout_s, 16 * NB)

        @block.gpsimd
        def _(pool):
            step = stepper(pool, g_ch)
            pool.memset(gate_bd[:], 0.0).then_inc(bd_zero, 1)
            pool.memset(mhalf[:], -0.5)
            for j in range(HALF):
                pool.memset(inv[:, j:j + 1], float(np.float32(1.0) / np.float32(ROPE_THETA) ** np.float32(j / HALF)))
            pool.memset(xl[:, :, 0:CONV_W - 1], 0.0)
            step(pool.memset(ident[:], 0.0))
            pool.affine_select(out=ident[:], in_=ident[:], compare_op=ALU.not_equal, fill=1.0, base=0,
                               pattern=[[-1, P]], channel_multiplier=1)
            step(pool.memset(mask[:], 0.0))
            for c in (0, 2 * P):
                pool.affine_select(out=mask[:, c:c + P], in_=mask[:, c:c + P], compare_op=ALU.is_ge,
                                   fill=MASKED, base=0, pattern=[[-1, P]], channel_multiplier=1)
            pool.iota(i8[:], pattern=[[1, E]], base=0, channel_multiplier=0,
                      allow_small_or_imprecise_dtypes=True).then_inc(consts, 1)

            def rms(k):
                for b in range(NB):
                    pool.wait_ge(ss_r, NB * k + b + 1)
                    step(pool.tensor_scalar(mean[:, b:b + 1], ssq[:, b:b + 1], 1.0 / D, EPS, ALU.mult, ALU.add))
                    pool.tensor_tensor(rstd[:, b:b + 1], mean[:, b:b + 1], mhalf[:, 0:1], ALU.pow).then_inc(rstd_r, 1)

            for l in range(DEPTH):
                rms(2 * l)
                pool.wait_ge(zss_r, l + 1)
                for w, n in enumerate((QL, KVL)):
                    ins = pool.tensor_scalar(zmean[:, w, :], zssq[:, w, :], 1.0 / n, EPS, ALU.mult, ALU.add)
                step(ins)
                pool.tensor_tensor(zrstd[:].rearrange("p w b -> p (w b)"), zmean[:].rearrange("p w b -> p (w b)"),
                                   mhalf[:], ALU.pow).then_inc(zrstd_r, 1)
                pool.wait_ge(kr_r, l + 1)
                for b in range(NB):
                    ins = pool.tensor_copy(kcat[:, b, :, QK_NOPE:], kr[:, b, :].unsqueeze(1).to_broadcast([P, N_HEADS, QK_ROPE]))
                ins.then_inc(kr_c, 1)
                pool.wait_ge(yg_r, l + 1)
                step(pool.tensor_scalar(gg[:], gg[:], 0.044715, 1.0, ALU.mult, ALU.add))
                pool.tensor_tensor(gg[:], gg[:], yg[:], ALU.mult).then_inc(gin_r, 1)
                pool.wait_ge(gate_t, l + 1)
                pool.wait_ge(xc_r, l + 1)
                step(pool.tensor_scalar(tb[:], tb[:], 1.0, 1.0, ALU.mult, ALU.add))
                pool.tensor_tensor(tb[:], tb[:], xc[:], ALU.mult).then_inc(iw_r, 1)
                pool.wait_ge(gth_r, l + 1)
                step(pool.tensor_scalar(gg[:], gg[:], 1.0, 1.0, ALU.mult, ALU.add))
                pool.tensor_tensor(gg[:], gg[:], yg[:], ALU.mult).then_inc(gg_r, 1)
                pool.wait_ge(lru_o, l + 1)
                step(pool.tensor_copy(act_hi[:, 0:LT, :], ts[:]))
                pool.tensor_tensor(act_lo[:, 0:LT, :], ts[:], act_hi[:, 0:LT, :].bitcast(F32), ALU.subtract).then_inc(lru_lo, 1)
                if l == DEPTH - 1:
                    pool.dma_start(rw.rearrange("p (k e) -> p k e", k=KT), router_w[0].rearrange("(k p) e -> p k e", p=P)).then_inc(rw_in, 16)
                    pool.dma_start(grow, norm_ffn[1].partition_broadcast(P)).then_inc(grow_in, 16)
                    step(pool.memset(before, 1.0))
                    pool.affine_select(out=before, in_=before, compare_op=ALU.is_gt, fill=0.0, base=0,
                                       pattern=[[1, P]], channel_multiplier=-1)
                    pool.memset(ones, 1.0)
                    pool.iota(slot, pattern=[[1, P]], base=0, channel_multiplier=0,
                              allow_small_or_imprecise_dtypes=True).then_inc(consts, 1)
                rms(2 * l + 1)
            pool.wait_ge(grow_in, 16)
            for b, normed in enumerate((xn_a, xn_v)):
                pool.wait_ge(normed, 2 * DEPTH)
                if b == 0:
                    pool.tensor_copy(ident_b[:], ident[:])
                pool.tensor_tensor(xgain[:, b, :], xn[:, b, :], grow, ALU.mult).then_inc(xg_r, 1)
            pool.wait_ge(xg_r, NB)
            pool.dma_start(grow, norm_final.partition_broadcast(P)).then_inc(grow_in, 16)
            rms(2 * DEPTH)

        @block.scalar
        def _(act):
            step = stepper(act, a_ch)

            def hi(first, c, width=CHUNK, i=0):
                act.wait_ge(landed[raw_slot(first, c)], 32 * raw_turn(first, c, i))
                if isinstance(i, int) and i == 0 and first + c < SPLIT:
                    pass
                else:
                    act.wait_ge(used, nth(first, c, i) - SPLIT + 1)
                act.activation(w_hi[:, split_slot(first, c), 0:width], raw[:, raw_slot(first, c), 0:width],
                               ACT.Copy).then_inc(hi_made, 1)

            def squares(ready):
                for b in range(NB):
                    act.wait_ge(*ready(b))
                    act.activation(xn[:, b, :], xs[:, b, :], ACT.Square, accum_out=ssq[:, b:b + 1]).then_inc(ss_r, 1)

            def norm(k, ready):
                squares(ready)
                act.wait_ge(rstd_r, NB * k + 1)
                act.activation(xn[:, 0, :], xs[:, 0, :], ACT.Copy, scale=rstd[:, 0:1]).then_inc(xn_a, 1)

            def norm_split(k, gain0):
                for j in range(4):
                    act.wait_ge(nT, 4 * k + j + 1)
                    for t in range(2):
                        kt = 2 * j + t
                        ins = act.activation(act_hi[:, kt, :], bank[4 * (k % 2) + j][:, t * SEQ:(t + 1) * SEQ], ACT.Copy,
                                             scale=prm[:, gain0 + kt:gain0 + kt + 1])
                    ins.then_inc(nT_hi, 1)

            for l in range(DEPTH):
                first = FIRST["mix", l]
                if l:
                    hi(first, 0, 4 * ZT)
                    hi(first, 1, 4 * ZT)
                    norm(2 * l, lambda b: (y_r, b + 1))
                else:
                    norm(0, lambda b: (x_in[b], 16))
                    hi(first, 0, 4 * ZT)
                    act.wait_ge(prm_r, 1)
                norm_split(2 * l, l * KT)
                if l == 0:
                    hi(first, 1, 4 * ZT)
                    act.activation(lru_c[:, 0, :], prm[:, 88:96], ACT.Exp, scale=-1.0).then_inc(lam_e, 1)
                    act.wait_ge(lam_e, 1)
                    act.activation(lru_c[:, 0, :], lru_c[:, 0, :], ACT.Ln, bias=1.0).then_inc(lam_e, 1)
                    act.wait_ge(angle_r, 1)
                    act.activation(trig[:], trig_in, ACT.Sin).then_inc(trig_r, 1)
                hi(first, 2)
                hi(first, 3)
                act.wait_ge(used, first + 2)
                for b in range(NB):
                    act.activation(cn[:, b, 0:QL], bank[b][:, 0:QL], ACT.Square, accum_out=zssq[:, 0, b:b + 1])
                    ins = act.activation(cn[:, b, QL:], bank[b][:, QL:QL + KVL], ACT.Square, accum_out=zssq[:, 1, b:b + 1])
                ins.then_inc(zss_r, 1)
                hi(first, 4)
                act.wait_ge(used, first + 4)
                for j in range(2):
                    ins = act.activation(xl[:, 2 * j:2 * j + 2, CONV_W - 1:],
                                         bank[4 + j][:].rearrange("p (t n) -> p t n", t=2), ACT.Copy)
                ins.then_inc(xl_r, 1)
                act.wait_ge(cT, l + 1)
                for t in range(CT):
                    g = 96 + 2 * l + t if t < QL // P else 100 + l
                    ins = act.activation(c_hi[:, t, :], bank[2 + t // 2][:, (t % 2) * SEQ:(t % 2 + 1) * SEQ], ACT.Copy,
                                         scale=prm[:, g:g + 1])
                ins.then_inc(cT_hi, 1)
                hi(first, 5, QL // P * N_HEADS * QK)
                hi(first, 6)
                hi(first, 7, KVL // P * w_ukv.shape[2])
                hi(first, 8)
                act.wait_ge(gate_p, 2 * l + 1)
                act.wait_ge(lru_r, 1)
                for t in range(LT):
                    c = l * LT + t
                    ins = act.activation(ta[:, t, :], bank[t // 2][:, (t % 2) * SEQ:(t % 2 + 1) * SEQ], ACT.Tanh,
                                         scale=0.5, bias=lru_c[:, 1, c:c + 1])
                step(ins)
                for t in range(LT):
                    c = l * LT + t
                    ins = act.activation(tr[:, t, :], ta[:, t, :], ACT.Tanh, scale=lru_c[:, 0, c:c + 1],
                                         bias=lru_c[:, 0, c:c + 1])
                ins.then_inc(decay_r, 1)
                act.wait_ge(used, first + 7)
                for j in range(2):
                    act.activation(yg[:, 2 * j:2 * j + 2, :], bank[6 + j][:].rearrange("p (t n) -> p t n", t=2), ACT.Copy)
                    ins = act.activation(gg[:, 2 * j:2 * j + 2, :], bank[6 + j][:].rearrange("p (t n) -> p t n", t=2), ACT.Square)
                ins.then_inc(yg_r, 1)
                act.wait_ge(gate_p, 2 * l + 2)
                for t in range(LT):
                    c = l * LT + t
                    ins = act.activation(tb[:, t, :], bank[2 + t // 2][:, (t % 2) * SEQ:(t % 2 + 1) * SEQ], ACT.Tanh,
                                         scale=0.5, bias=lru_c[:, 2, c:c + 1])
                ins.then_inc(gate_t, 1)
                act.wait_ge(decay_r, l + 1)
                act.activation(ts[:], tr[:], ACT.Sqrt, scale=-1.0).then_inc(sq_r, 1)

                def gelu():
                    act.wait_ge(gin_r, l + 1)
                    act.activation(gg[:], gg[:], ACT.Tanh, scale=math.sqrt(2.0 / math.pi)).then_inc(gth_r, 1)

                def recurrence():
                    for t in range(LT):
                        c = l * LT + t
                        ins = act.activation(ta[:, t, :], ta[:, t, :], ACT.Exp, scale=lru_c[:, 3, c:c + 1],
                                             bias=lru_c[:, 3, c:c + 1])
                    ins.then_inc(a_r, 1)

                def qk_turn(h):
                    n = N_HEADS * l + h
                    act.wait_ge(qkT_p, n + 1)
                    if n >= 2:
                        act.wait_ge(s_p, n - 1)
                    act.activation(qkT[:, h % 2, :], bank[h % 2][0:QK, :], ACT.Copy).then_inc(qkT_r, 1)

                def exps(h):
                    n = N_HEADS * l + h
                    act.wait_ge(s_r, n + 1)
                    for j, (c0, c1) in enumerate(((0, P), (P, 3 * P))):
                        ins = act.activation(pr[:, h % 2, c0:c1], pr[:, h % 2, c0:c1], ACT.Exp, scale=SCALE,
                                             bias=nmx[:, h % 2, j:j + 1], accum_out=rs[:, h % 2, j:j + 1])
                    ins.then_inc(p_r, 1)

                def p_turn(h):
                    n = N_HEADS * l + h
                    act.wait_ge(pT_p, n + 1)
                    if n >= 2:
                        act.wait_ge(o_p, n - 1)
                    act.activation(pT[:, h % 2, :], bank[4 + h % 2][:, 0:3 * P], ACT.Copy).then_inc(pT_r, 1)

                def o_split(g):
                    act.wait_ge(o_p, N_HEADS * l + 4 * g + 4)
                    act.activation(act_hi[:, LT + 2 * g:LT + 2 * g + 2, :],
                                   bank[6 + g][:].rearrange("p (t n) -> p t n", t=2), ACT.Copy).then_inc(o_hi, 1)

                for i in range(N_HEADS + 3):
                    if i < N_HEADS:
                        qk_turn(i)
                    if 1 <= i <= N_HEADS:
                        exps(i - 1)
                    if i == 1:
                        recurrence()
                        gelu()
                    if 2 <= i <= N_HEADS + 1:
                        p_turn(i - 2)
                    if i == 4:
                        hi(first, 9)
                    if i == 7:
                        o_split(0)
                hi(first, 10)
                o_split(1)
                hi(first, 11)
                f0 = EXPERT0 if l else FIRST["dense", 0]
                hi(f0, 0)
                hi(f0, 1)
                norm(2 * l + 1, lambda b: (mix_r, NB * l + b + 1))
                if l == 0:
                    norm_split(1, 16)
                    ffn(act_unit_ops(act, NB, 0, lambda s: nth(f0, DENSE_ORDER.index(("gu", s, 1))) + 1), DENSE_UNITS, lambda c: hi(f0, c))
                else:
                    act.wait_ge(rw_in, 16)
                    act.activation(rw_hi, rw, ACT.Copy).then_inc(rw_h, 1)
                    norm_split(3, 24)
                    hi(EXPERT0, 2)
                    act.wait_ge(lg_r, 1)
                    act.activation(tw[:, 0, :], dif[:], ACT.Tanh, scale=0.5).then_inc(tw_r, 1)
                    for k in range(2):
                        for b in range(NB):
                            if k:
                                act.wait_ge(xg_v, b + 1)
                            else:
                                act.wait_ge(xg_r, b + 1)
                            act.activation(xg[k][:, b, :], xgain[:, b, :], ACT.Copy).then_inc(xg_a, 1)

            def unit_ops(j):
                return act_unit_ops(act, 1, DENSE_U + UNITS * j,
                                    lambda s: nth(EXPERT0, EXPERT_ORDER.index(("gu", s, 1)), j) + 1)

            def gathered(j):
                act.wait_ge(xT_p, j + 1)
                for k in range(2):
                    ins = act.activation(act_hi[:, 4 * k:4 * k + 4, 0:P],
                                         bank[k][:].rearrange("p (k n) -> p k n", k=4), ACT.Copy)
                ins.then_inc(xT_hi, 1)

            def outputs(i):
                act.wait_ge(used, nth(EXPERT0, PER_JOB, i))
                for k in range(2):
                    ins = act.activation(y_hi[:, 512 * k:512 * k + 512], bank[2 + k][:], ACT.Copy)
                ins.then_inc(yg_hi, 1)

            def matrix(j):
                act.wait_ge(sT_p, j + 1)
                if not isinstance(j, int):
                    act.wait_ge(sc_p, j)
                act.activation(sel_t[:], bank[7][:, 0:NB * P].rearrange("p (b n) -> p b n", b=NB),
                               ACT.Copy).then_inc(sT_r, 1)

            def job(i, more):
                job_rest(unit_ops(i), lambda c: hi(EXPERT0, c, i=i), lambda: None,
                         lambda: gathered(i + 1) if more else None,
                         lambda: hi(EXPERT0, 0, i=i + 1) if more else None)
                if more:
                    job_start(unit_ops(i + 1), lambda c: hi(EXPERT0, c, i=i + 1), lambda: outputs(i), lambda: matrix(i + 1))

            gathered(0)
            job_start(unit_ops(0), lambda c: hi(EXPERT0, c) if c > 2 else None, lambda: None, lambda: matrix(0))
            act.wait_ge(jobs_r, 1)
            last = act.value_load(jobs[0:1, 0:1], min_val=E - 1, max_val=E - 1 + MORE)
            with act.Fori(0, last) as i:
                job(i, True)
            job(last, False)
            outputs(last)
            squares(lambda b: (sc_r, last * NB + b + 2))

        @block.vector
        def _(dve):
            step = stepper(dve, v_ch)

            def lo(first, c, width=CHUNK, i=0):
                s = split_slot(first, c)
                dve.wait_ge(hi_made, nth(first, c, i) + 1)
                dve.tensor_tensor(w_lo[:, s, 0:width], raw[:, raw_slot(first, c), 0:width],
                                  w_hi[:, s, 0:width].bitcast(F32), ALU.subtract).then_inc(lo_made, 1)

            def norm(k):
                dve.wait_ge(rstd_r, NB * k + 2)
                dve.tensor_scalar(xn[:, 1, :], xs[:, 1, :], rstd[:, 1:2], None, ALU.mult).then_inc(xn_v, 1)

            def norm_split(k, gain0):
                for j in range(4):
                    dve.wait_ge(nT_hi, 4 * k + j + 1)
                    for t in range(2):
                        kt = 2 * j + t
                        ins = dve.scalar_tensor_tensor(out=act_lo[:, kt, :], in0=bank[4 * (k % 2) + j][:, t * SEQ:(t + 1) * SEQ],
                                                       scalar=prm[:, gain0 + kt:gain0 + kt + 1],
                                                       in1=act_hi[:, kt, :].bitcast(F32), op0=ALU.mult, op1=ALU.subtract)
                    ins.then_inc(nT_lo, 1)

            dve.wait_ge(prm_t, 1)
            dve.tensor_copy(prm[:], bank[0][:, 0:102]).then_inc(prm_r, 1)
            def rope(dst, src, b, heads):
                sin = trig[:, 0, b, :].unsqueeze(1).to_broadcast([P, heads, HALF])
                cos = trig[:, 1, b, :].unsqueeze(1).to_broadcast([P, heads, HALF])
                ra, rb = rope_a[:, 0:heads, :], rope_b[:, 0:heads, :]
                for j in range(2):
                    hs = slice(HALF * j, HALF * j + HALF)
                    dve.tensor_tensor(ra[:, :, hs], src[:, :, hs], cos, ALU.mult)
                    ins = dve.tensor_tensor(rb[:, :, hs], src[:, :, hs], sin, ALU.mult)
                step(ins)
                dve.tensor_tensor(dst[:, :, 0:HALF], ra[:, :, 0:HALF], rb[:, :, HALF:], ALU.subtract)
                return dve.tensor_tensor(dst[:, :, HALF:], ra[:, :, HALF:], rb[:, :, 0:HALF], ALU.add)

            for l in range(DEPTH):
                first = FIRST["mix", l]
                norm(2 * l)
                if l == 0:
                    dve.wait_ge(pos_in, 16)
                    step(dve.tensor_copy(pos_f[:], pos_i[:]))
                    dve.wait_ge(consts, 1)
                    for b in range(NB):
                        ins = dve.tensor_scalar(ang[:, b, :], inv[:], pos_f[:, b:b + 1], None, ALU.mult)
                    step(ins)
                    rnd = 1.5 * 2.0 ** 23
                    for w in range(2):
                        ins = dve.tensor_scalar(turn[:, w], ang, 1.0 / (2 * math.pi), 0.25 * w, ALU.mult, ALU.add)
                    step(ins)
                    step(dve.tensor_scalar(turn, turn, rnd, -rnd, ALU.add, ALU.add))
                    c1 = 6.28125
                    c2 = float(np.float32(2 * math.pi - c1))
                    for w in range(2):
                        ins = dve.scalar_tensor_tensor(out=trig_in[:, w], in0=turn[:, w], scalar=-c1, in1=ang, op0=ALU.mult, op1=ALU.add)
                    step(ins)
                    step(dve.scalar_tensor_tensor(out=trig_in, in0=turn, scalar=-c2, in1=trig_in, op0=ALU.mult, op1=ALU.add))
                    step(dve.tensor_scalar(trig_in[:, 1], trig_in[:, 1], math.pi / 2, None, ALU.add))
                    lim = 3.1415925
                    dve.tensor_scalar(trig_in, trig_in, lim, -lim, ALU.min, ALU.max).then_inc(angle_r, 1)
                    lo(first, 0, 4 * ZT)
                norm_split(2 * l, l * KT)
                if l == 0:
                    lo(first, 1, 4 * ZT)
                    dve.wait_ge(prm_r, 1)
                    dve.tensor_scalar(lru_c[:, 1:3, :], prm[:, 72:88].rearrange("p (w c) -> p w c", w=2), 0.5, None, ALU.mult)
                    dve.wait_ge(lam_e, 2)
                    dve.tensor_scalar(lru_c[:, 3, :], lru_c[:, 0, :], -LRU_C / 2, None, ALU.mult)
                    step(dve.tensor_scalar(lru_c[:, 0, :], lru_c[:, 0, :], -LRU_C / 4, None, ALU.mult))
                    dve.tensor_copy(dif[:], pos_f[:]).then_inc(lru_r, 1)
                    dve.wait_ge(trig_r, 1)
                lo(first, 2)
                lo(first, 3)
                dve.wait_ge(zrstd_r, l + 1)
                for b in range(NB):
                    dve.tensor_scalar(cn[:, b, 0:QL], bank[b][:, 0:QL], zrstd[:, 0, b:b + 1], None, ALU.mult)
                    ins = dve.tensor_scalar(cn[:, b, QL:], bank[b][:, QL:QL + KVL], zrstd[:, 1, b:b + 1], None, ALU.mult)
                ins.then_inc(cn_r, 1)
                for b in range(NB):
                    ins = rope(kr[:, b, :].unsqueeze(1), bank[b][:, QL + KVL:ZT].unsqueeze(1), b, 1)
                    if b == 0:
                        step(ins)
                ins.then_inc(kr_r, 1)
                lo(first, 4)

                def conv(j):
                    for t in range(LT):
                        w = 32 + (l * CONV_W + j) * LT + t
                        src = xl[:, t, j:j + SEQ]
                        if j == CONV_W - 1:
                            cb = 64 + l * LT + t
                            ins = dve.tensor_scalar(xc[:, t, :], src, prm[:, w:w + 1], prm[:, cb:cb + 1], ALU.mult, ALU.add)
                        else:
                            ins = dve.scalar_tensor_tensor(out=xc[:, t, :], in0=src, scalar=prm[:, w:w + 1], in1=xc[:, t, :],
                                                           op0=ALU.mult, op1=ALU.add)
                    if j:
                        step(ins)
                    else:
                        ins.then_inc(xc_r, 1)

                dve.wait_ge(xl_r, l + 1)
                conv(3)
                conv(2)
                dve.wait_ge(cT_hi, l + 1)
                for t in range(CT):
                    g = 96 + 2 * l + t if t < QL // P else 100 + l
                    ins = dve.scalar_tensor_tensor(out=c_lo[:, t, :], in0=bank[2 + t // 2][:, (t % 2) * SEQ:(t % 2 + 1) * SEQ],
                                                   scalar=prm[:, g:g + 1], in1=c_hi[:, t, :].bitcast(F32),
                                                   op0=ALU.mult, op1=ALU.subtract)
                ins.then_inc(cT_lo, 1)
                lo(first, 5, QL // P * N_HEADS * QK)
                conv(1)
                conv(0)
                lo(first, 6)
                lo(first, 7, KVL // P * w_ukv.shape[2])

                def lru_part(i):
                    if i == 0:
                        dve.wait_ge(sq_r, l + 1)
                        dve.wait_ge(a_r, l + 1)
                        step(dve.scalar_tensor_tensor(out=ts[:], in0=ta[:], scalar=1.0, in1=ts[:], op0=ALU.add, op1=ALU.mult))
                        step(dve.memset(ts[:, :, 0:1], 1.0))
                    elif i == 1:
                        dve.wait_ge(iw_r, l + 1)
                        step(dve.tensor_tensor(tb[:], tb[:], ts[:], ALU.mult))
                    elif i == 2:
                        for t in range(LT):
                            ins = dve.tensor_tensor_scan(ts[:, t, :], ta[:, t, :], tb[:, t, :], 0.0, ALU.mult, ALU.add)
                        step(ins)
                        dve.wait_ge(gg_r, l + 1)
                        dve.scalar_tensor_tensor(out=ts[:], in0=ts[:], scalar=0.25, in1=gg[:], op0=ALU.mult, op1=ALU.mult).then_inc(lru_o, 1)

                dve.wait_ge(used, first + 6)
                for b in range(NB):
                    for j in range(2):
                        ins = dve.tensor_copy(qcat[:, b, 4 * j:4 * j + 4, :],
                                              bank[2 + 2 * b + j][:, 0:4 * QK].rearrange("p (h d) -> p h d", h=4))
                ins.then_inc(q_c, 1)
                dve.wait_ge(q_c, l + 1)
                for b in range(NB):
                    rq = qcat[:, b, :, QK_NOPE:]
                    ins = rope(rq, rq, b, N_HEADS)
                    if b == 0:
                        step(ins)
                ins.then_inc(q_r, 1)
                lo(first, 8)
                dve.wait_ge(used, first + 8)
                for part, made in ((0, k_r), (1, v_r)):
                    for b in range(NB):
                        for j in range(2):
                            src = bank[4 + 2 * j + b][:].rearrange("p (h d) -> p h d", h=4)
                            hs = slice(4 * j, 4 * j + 4)
                            if part == 0:
                                ins = dve.tensor_copy(kcat[:, b, hs, 0:QK_NOPE], src[:, :, 0:QK_NOPE])
                            else:
                                ins = dve.tensor_copy(vv[:, b, hs, :], src[:, :, QK_NOPE:])
                    ins.then_inc(made, 1)

                def mask_max(h):
                    n = N_HEADS * l + h
                    dve.wait_ge(s_p, n + 1)
                    if n >= 2:
                        dve.wait_ge(pT_p, n - 1)
                    for j, (c0, c1) in enumerate(((0, P), (P, 3 * P))):
                        ins = dve.tensor_tensor_reduce(pr[:, h % 2, c0:c1], bank[2 + h % 2][:, c0:c1], mask[:, c0:c1], 1.0, -3e38,
                                                       ALU.add, ALU.max, mx[:, h % 2, j:j + 1])
                    step(ins)
                    dve.tensor_scalar(nmx[:, h % 2, :], mx[:, h % 2, :], -SCALE, None, ALU.mult).then_inc(s_r, 1)

                def normalise(h):
                    n = N_HEADS * l + h
                    dve.wait_ge(p_r, n + 1)
                    step(dve.reciprocal(ri[:, h % 2, :], rs[:, h % 2, :]))
                    for j, (c0, c1) in enumerate(((0, P), (P, 3 * P))):
                        ins = dve.tensor_scalar(pr[:, h % 2, c0:c1], pr[:, h % 2, c0:c1], ri[:, h % 2, j:j + 1], None, ALU.mult)
                    ins.then_inc(pn_r, 1)

                def o_split(g):
                    dve.wait_ge(o_hi, 2 * l + g + 1)
                    a = slice(LT + 2 * g, LT + 2 * g + 2)
                    dve.tensor_tensor(act_lo[:, a, :], bank[6 + g][:].rearrange("p (t n) -> p t n", t=2),
                                      act_hi[:, a, :].bitcast(F32), ALU.subtract).then_inc(o_lo, 1)

                for i in range(N_HEADS + 3):
                    if 2 <= i <= N_HEADS + 1:
                        normalise(i - 2)
                    if 1 <= i <= N_HEADS:
                        mask_max(i - 1)
                    if 2 <= i <= 4:
                        lru_part(i - 2)
                    if i == 5:
                        lo(first, 9)
                    if i == 7:
                        o_split(0)
                lo(first, 10)
                o_split(1)
                lo(first, 11)
                f0 = EXPERT0 if l else FIRST["dense", 0]
                lo(f0, 0)
                lo(f0, 1)
                dve.wait_ge(first_rows, 2 * l + 1)
                for b in range(NB):
                    if b:
                        dve.wait_ge(used, first + MIX_CHUNKS)
                    for j in range(2):
                        ins = dve.tensor_tensor(xs[:, b, 512 * j:512 * j + 512], xs[:, b, 512 * j:512 * j + 512], bank[2 * b + j][:], ALU.add)
                    ins.then_inc(mix_r, 1)
                norm(2 * l + 1)
                if l == 0:
                    norm_split(1, 16)
                    ffn(vec_unit_ops(dve, NB, 0), DENSE_UNITS, lambda c: lo(f0, c))
                    lo(FIRST["mix", 1], 0, 4 * ZT)
                    lo(FIRST["mix", 1], 1, 4 * ZT)
                    dve.wait_ge(first_rows, 2)
                    for b in range(NB):
                        if b:
                            dve.wait_ge(used, FIRST["mix", 1])
                        for j in range(2):
                            ins = dve.tensor_tensor(xs[:, b, 512 * j:512 * j + 512], xs[:, b, 512 * j:512 * j + 512], bank[2 * b + j][:], ALU.add)
                        ins.then_inc(y_r, 1)

            dve.wait_ge(rw_h, 1)
            dve.tensor_tensor(rw_lo, rw, rw_hi.bitcast(F32), ALU.subtract).then_inc(rw_r, 1)
            norm_split(3, 24)
            dve.wait_ge(lg_p, 1)
            dve.tensor_copy(lgT[:], bank[0][0:E, 0:SEQ]).then_inc(lgT_r, 1)
            dve.wait_ge(lg_p, 2)
            step(dve.tensor_copy(lg, bank[1][:, 0:NB * E].rearrange("p (b e) -> p b e", b=NB)))
            for b in range(NB):
                ins = dve.max(top[:, b, :], lg[:, b, :])
            step(ins)
            dve.tensor_tensor(dif[:].unsqueeze(2), top[:, :, 0:1], top[:, :, 1:2], ALU.subtract).then_inc(lg_r, 1)
            for b in range(NB):
                ins = dve.max_index(topi[:, b, :], top[:, b, :], lg[:, b, :])
            step(ins)
            step(dve.tensor_copy(topf, topi))
            for b in range(NB):
                for k in range(TOP_K):
                    ins = dve.tensor_scalar(oh[:, k, b, :], i8[:], topf[:, b, k:k + 1], None, ALU.is_equal)
            step(ins)
            dve.tensor_tensor(pick, oh[:, 0], oh[:, 1], ALU.add).then_inc(pick_r, 1)
            for b in range(NB):
                dve.wait_ge(xg_a, b + 1)
                dve.tensor_tensor(xgain[:, b, :], xgain[:, b, :], xg[0][:, b, :], ALU.subtract).then_inc(xg_v, 1)
            dve.wait_ge(tw_r, 1)
            dve.tensor_scalar(tw[:, 1, :], tw[:, 0, :], -0.5, 0.5, ALU.mult, ALU.add).then_inc(tw_r, 1)
            dve.wait_ge(tw_r, 2)
            step(dve.tensor_scalar(tw[:, 0, :], tw[:, 0, :], 0.5, 0.5, ALU.mult, ALU.add))
            for b in range(NB):
                ins = dve.tensor_scalar(gates[:, b, 0:E], oh[:, 0, b, :], tw[:, 0, b:b + 1], None, ALU.mult)
            step(ins)
            for b in range(NB):
                ins = dve.scalar_tensor_tensor(out=gates[:, b, 0:E], in0=oh[:, 1, b, :], scalar=tw[:, 1, b:b + 1], in1=gates[:, b, 0:E],
                                               op0=ALU.mult, op1=ALU.add)
            step(ins)
            dve.wait_ge(place_p, 1)
            over, upto = (jb[:, k, :] for k in range(2))
            dve.tensor_scalar(over, bank[1][:, NB * E:(NB + 1) * E], P + 0.5, None, ALU.is_gt).then_inc(sc_r, 1)
            step(dve.scalar_tensor_tensor(out=place[:, :, 0:E], in0=bank[1][:, 0:NB * E].rearrange("p (b e) -> p b e", b=NB),
                                          scalar=1.0, in1=pick, op0=ALU.add, op1=ALU.mult))
            step(dve.tensor_scalar(place[:, :, 0:E], place[:, :, 0:E], -1.0, None, ALU.add))

            def matrix(j):
                if not isinstance(j, int):
                    dve.wait_ge(sT_p, j)
                for b in range(NB):
                    ins = dve.tensor_copy(cur[:, 0, b:b + 1], place[:, b, bass.ds(j, 1)])
                ins.then_inc(cur_r, 1)
                dve.wait_ge(cur_r, j + 1)
                for b in range(NB):
                    ins = dve.tensor_scalar(sel[:, b, :], slot, cur[:, 0, b:b + 1], None, ALU.is_equal)
                ins.then_inc(sel_r, 1)

            dve.wait_ge(consts, 2)
            matrix(0)
            for b in range(NB):
                dve.wait_ge(xg_a, NB + b + 1)
                dve.tensor_tensor(xg[2][:, b, :], xgain[:, b, :], xg[1][:, b, :], ALU.subtract).then_inc(xg_v, 1)
            lo(EXPERT0, 2)
            hit = [jb[:, 2 + j, :] for j in range(MORE)]
            step(dve.tensor_tensor_scan(upto, over, over, 0.0, ALU.add, ALU.max))
            for j in range(MORE):
                ins = dve.scalar_tensor_tensor(out=hit[j], in0=upto, scalar=float(j + 1), in1=over, op0=ALU.is_equal, op1=ALU.mult)
            step(ins)
            dve.tensor_scalar(jf[:, 0:1], upto[0:1, E - 1:E], float(E - 1), None, ALU.add)
            for j in range(MORE):
                ins = dve.tensor_tensor(jb[0:1, 5 + j, :], hit[j][0:1], i8[0:1, :], ALU.mult)
            step(ins)
            step(dve.tensor_reduce(jf[:, 1:1 + MORE], jb[0:1, 5:5 + MORE, :], AX, ALU.add))
            dve.tensor_copy(jobs[:], jf[:]).then_inc(jobs_r, 1)
            for j in range(MORE):
                for b in range(NB):
                    dve.scalar_tensor_tensor(out=wide[:, 0, j, b, :], in0=place[:, b, 0:E], scalar=1.0 - P, in1=hit[j], op0=ALU.add, op1=ALU.mult)
                    ins = dve.tensor_tensor(wide[:, 1, j, b, :], gates[:, b, 0:E], hit[j], ALU.mult)
            step(ins)
            for j in range(MORE):
                dve.tensor_reduce(place[:, :, E + j], wide[:, 0, j], AX, ALU.add)
                ins = dve.tensor_reduce(gates[:, :, E + j], wide[:, 1, j], AX, ALU.add)
            step(ins)
            step(dve.tensor_scalar(place[:, :, E:E + MORE], place[:, :, E:E + MORE], -1.0, None, ALU.add))

            def gathered(j):
                dve.wait_ge(xT_hi, j + 1)
                for k in range(2):
                    a = slice(4 * k, 4 * k + 4)
                    ins = dve.tensor_tensor(act_lo[:, a, 0:P], bank[k][:].rearrange("p (k n) -> p k n", k=4),
                                            act_hi[:, a, 0:P].bitcast(F32), ALU.subtract)
                ins.then_inc(xT_lo, 1)

            def outputs(i):
                dve.wait_ge(yg_hi, i + 1)
                for k in range(2):
                    w = slice(512 * k, 512 * k + 512)
                    ins = dve.tensor_tensor(y_lo[:, w], bank[2 + k][:], y_hi[:, w].bitcast(F32), ALU.subtract)
                ins.then_inc(yg_lo, 1)

            def add(i):
                for b in range(NB):
                    ins = dve.tensor_copy(cur[:, 1, b:b + 1], gates[:, b, bass.ds(i, 1)])
                ins.then_inc(gate_r, 1)
                dve.wait_ge(gate_r, i + 1)
                dve.wait_ge(sc_p, i + 1)
                for b in range(NB):
                    for j in range(2):
                        w = slice(512 * j, 512 * j + 512)
                        ins = dve.scalar_tensor_tensor(out=xs[:, b, w], in0=bank[2 * b + j][:], scalar=cur[:, 1, b:b + 1],
                                                       in1=xs[:, b, w], op0=ALU.mult, op1=ALU.add)
                    ins.then_inc(sc_r, 1)

            def job(i, more):
                job_rest(vec_unit_ops(dve, 1, DENSE_U + UNITS * i), lambda c: lo(EXPERT0, c, i=i),
                         lambda: matrix(i + 1) if more else None, lambda: gathered(i + 1) if more else None,
                         lambda: lo(EXPERT0, 0, i=i + 1) if more else None)
                if more:
                    job_start(vec_unit_ops(dve, 1, DENSE_U + UNITS * (i + 1)), lambda c: lo(EXPERT0, c, i=i + 1),
                              lambda: outputs(i), lambda: add(i))

            gathered(0)
            job_start(vec_unit_ops(dve, 1, DENSE_U), lambda c: lo(EXPERT0, c) if c > 2 else None, lambda: None, lambda: None)
            last = dve.value_load(jobs[0:1, 0:1], min_val=E - 1, max_val=E - 1 + MORE)
            with dve.Fori(0, last) as i:
                job(i, True)
            job(last, False)
            outputs(last)
            add(last)
            dve.wait_ge(grow_in, 32)
            for b in range(NB):
                dve.wait_ge(rstd_r, NB * 2 * DEPTH + b + 1)
                dve.scalar_tensor_tensor(out=xn[:, b, :], in0=xs[:, b, :], scalar=rstd[:, b:b + 1], in1=grow,
                                         op0=ALU.mult, op1=ALU.mult).then_inc(out_r, 1)

        @block.tensor
        def _(pe):
            def chunk(first, c, i=0):
                pe.wait_ge(lo_made, nth(first, c, i) + 1)
                return split_slot(first, c)

            def three(o, a_h, a_l, b_h, b_l, start, stop, **k):
                pe.matmul(o, a_l, b_h, start=start, stop=False, **k)
                pe.matmul(o, a_h, b_l, start=False, stop=False, **k)
                return pe.matmul(o, a_h, b_h, start=False, stop=stop, **k)

            def ffn_products(nb, units, order, first, u0, i):
                y0 = 0 if nb == 2 else 2

                def gate_up(s):
                    for b in range(nb):
                        if nb == 2 and s:
                            pe.wait_ge(hid_r, u0 + nb * (s - 1) + b + 1)
                        if nb == 1 and s != 1:
                            pe.wait_ge(hid_r, u0 + max(s - 1, 0))
                    for k in range(2):
                        c = order.index(("gu", s, k))
                        sl = chunk(first, c, i)
                        if nb == 2 and s == 0:
                            pe.wait_ge(nT_lo, 4 + 2 * k + 2)
                        for b in range(nb):
                            o = bank[4 + (b if nb == 2 else s % 2)]
                            m = slice(b * P, (b + 1) * P)
                            for kk in range(4):
                                kt = 4 * k + kk
                                n = slice(kk * 2 * FW, (kk + 1) * 2 * FW)
                                ins = three(o[:], act_hi[:, kt, m], act_lo[:, kt, m], w_hi[:, sl, n], w_lo[:, sl, n],
                                            start=(kt == 0), stop=(kt == KT - 1))
                            if b == nb - 1:
                                ins.then_inc(used, 1)
                            elif k == 1:
                                ins.then_inc(gu_p, 1)

                def turn(s):
                    for b in range(nb):
                        u = u0 + nb * s + b
                        o = b if nb == 2 else s % 2
                        pe.wait_ge(hid_r, u + 1)
                        if nb == 2 and s:
                            pe.wait_ge(hT_lo, u - nb + 1)
                        if nb == 1 and s != 1:
                            pe.wait_ge(hT_lo, u0 + max(s - 1, 0))
                        h = hid[:, o, :].rearrange("p (n j) -> p j n", j=2)
                        for j in range(2):
                            ins = pe.transpose(bank[6 + o][:, j * P:(j + 1) * P], h[:, j, :], ident[:])
                        ins.then_inc(hT_p, 1)

                def down(s):
                    sl = chunk(first, order.index(("down", s, 0)), i)
                    for b in range(nb):
                        pe.wait_ge(hT_lo, u0 + nb * s + b + 1)
                        for j in range(2):
                            m = slice(j * P, (j + 1) * P)
                            for n in range(2):
                                w = slice(j * D + 512 * n, j * D + 512 * (n + 1))
                                ins = three(bank[y0 + 2 * b + n][:], sm_hi[:, s % SLOTS, b, m], sm_lo[:, s % SLOTS, b, m],
                                            w_hi[:, sl, w], w_lo[:, sl, w], start=(s == 0 and j == 0),
                                            stop=(s == units - 1 and j == 1))
                        if nb == 2 and b == 0 and s == units - 1:
                            ins.then_inc(first_rows, 1)
                    ins.then_inc(used, 1)

                return gate_up, turn, down

            def norm_turn(k):
                for b, normed in enumerate((xn_a, xn_v)):
                    pe.wait_ge(normed, k + 1)
                    for kt in range(KT):
                        c = (kt % 2) * SEQ + b * P
                        ins = pe.transpose(bank[4 * (k % 2) + kt // 2][:, c:c + P], xn[:, b, kt * P:(kt + 1) * P], ident[:])
                        if b and kt % 2:
                            ins.then_inc(nT, 1)

            pe.wait_ge(consts, 1)
            pe.wait_ge(rows_in, 16 * 9)
            pe.transpose(bank[0][:, 0:102], rows, ident[0:102, 0:102]).then_inc(prm_t, 1)
            pe.wait_ge(prm_r, 1)

            for l in range(DEPTH):
                first = FIRST["mix", l]
                norm_turn(2 * l)
                for k in range(2):
                    s = chunk(first, k)
                    pe.wait_ge(nT_lo, 8 * l + 2 * k + 2)
                    wh = w_hi[:, s, 0:4 * ZT].rearrange("p (k n) -> p k n", k=4)
                    wl = w_lo[:, s, 0:4 * ZT].rearrange("p (k n) -> p k n", k=4)
                    for kk in range(4):
                        kt = 4 * k + kk
                        for b in range(NB):
                            m = slice(b * P, (b + 1) * P)
                            ins = three(bank[b][:, 0:ZT], act_hi[:, kt, m], act_lo[:, kt, m], wh[:, kk, :], wl[:, kk, :],
                                        start=(kt == 0), stop=(kt == KT - 1))
                    ins.then_inc(used, 1)

                def wide_product(chunks, banks):
                    for c, k in chunks:
                        s = chunk(first, c)
                        wh = w_hi[:, s, :].rearrange("p (k n) -> p k n", k=4)
                        wl = w_lo[:, s, :].rearrange("p (k n) -> p k n", k=4)
                        for kk in range(4):
                            kt = 4 * k + kk
                            for t in range(LT):
                                o = bank[banks + t // 2][:, (t % 2) * SEQ:(t % 2 + 1) * SEQ]
                                m = slice(t * P, (t + 1) * P)
                                ins = three(o, wh[:, kk, m], wl[:, kk, m], act_hi[:, kt, :], act_lo[:, kt, :],
                                            start=(kt == 0 and t % 2 == 0), stop=(kt == KT - 1), skip_group_check=True)
                        ins.then_inc(used, 1)

                pe.wait_ge(nT_lo, 8 * l + 4)
                wide_product(((2, 0), (3, 1)), 4)
                pe.wait_ge(cn_r, l + 1)
                for t in range(CT):
                    for b in range(NB):
                        c = (t % 2) * SEQ + b * P
                        ins = pe.transpose(bank[2 + t // 2][:, c:c + P], cn[:, b, t * P:(t + 1) * P], ident[:])
                ins.then_inc(cT, 1)
                wide_product(((4, 0),), 6)
                pe.wait_ge(cT_lo, l + 1)
                pe.wait_ge(xl_r, l + 1)
                QT = QL // P
                s = chunk(first, 5)
                wh = w_hi[:, s, 0:QT * N_HEADS * QK].rearrange("p (k n) -> p k n", k=QT)
                wl = w_lo[:, s, 0:QT * N_HEADS * QK].rearrange("p (k n) -> p k n", k=QT)
                for b in range(NB):
                    m = slice(b * P, (b + 1) * P)
                    for j in range(2):
                        n = slice(j * 4 * QK, (j + 1) * 4 * QK)
                        for kt in range(QT):
                            ins = three(bank[2 + 2 * b + j][:, 0:4 * QK], c_hi[:, kt, m], c_lo[:, kt, m], wh[:, kt, n], wl[:, kt, n],
                                        start=(kt == 0), stop=(kt == QT - 1))
                ins.then_inc(used, 1)

                def gate_product(w):
                    for t in range(LT):
                        ins = pe.matmul(bank[2 * w + t // 2][:, (t % 2) * SEQ:(t % 2 + 1) * SEQ], gate_bd[:, w, t, :],
                                        xc[:, t, :], start=True, stop=True)
                    ins.then_inc(gate_p, 1)

                pe.wait_ge(xc_r, l + 1)
                pe.wait_ge(bd_in, 64 * (l + 1))
                pe.wait_ge(kr_r, l + 1)
                gate_product(0)
                wide_product(((6, 1),), 6)
                pe.wait_ge(q_c, l + 1)
                gate_product(1)
                pe.wait_ge(yg_r, l + 1)
                s = chunk(first, 7)
                for b in range(NB):
                    m = slice(b * P, (b + 1) * P)
                    for j in range(2):
                        n = slice(j * 512, (j + 1) * 512)
                        ins = three(bank[4 + 2 * j + b][:], c_hi[:, QT, m], c_lo[:, QT, m], w_hi[:, s, n], w_lo[:, s, n],
                                    start=True, stop=True)
                ins.then_inc(used, 1)

                def qk_turn(h):
                    n = N_HEADS * l + h
                    if n >= 2:
                        pe.wait_ge(qkT_r, n - 1)
                    for b in range(NB):
                        pe.transpose(bank[h % 2][0:QK, b * P:(b + 1) * P], qcat[:, b, h, :], ident[:])
                    for b in range(NB):
                        ins = pe.transpose(bank[h % 2][0:QK, SEQ + b * P:SEQ + (b + 1) * P], kcat[:, b, h, :], ident[:])
                    ins.then_inc(qkT_p, 1)

                def scores(h):
                    n = N_HEADS * l + h
                    pe.wait_ge(qkT_r, n + 1)
                    if n >= 2:
                        pe.wait_ge(s_r, n - 1)
                    t = qkT[:, h % 2, :]
                    pe.matmul(bank[2 + h % 2][:, 0:P], t[:, 0:P], t[:, SEQ:SEQ + P], start=True, stop=True)
                    pe.matmul(bank[2 + h % 2][:, P:3 * P], t[:, P:2 * P], t[:, SEQ:2 * SEQ], start=True, stop=True).then_inc(s_p, 1)

                def p_turn(h):
                    n = N_HEADS * l + h
                    pe.wait_ge(pn_r, n + 1)
                    if n >= 2:
                        pe.wait_ge(pT_r, n - 1)
                    for src, dst in ((0, 0), (P, P), (2 * P, 2 * P)):
                        ins = pe.transpose(bank[4 + h % 2][:, dst:dst + P], pr[:, h % 2, src:src + P], ident[:])
                    ins.then_inc(pT_p, 1)

                def values(h):
                    n = N_HEADS * l + h
                    pe.wait_ge(pT_r, n + 1)
                    r = slice((h % 2) * V_HEAD, (h % 2 + 1) * V_HEAD)
                    c = (h // 2 % 2) * SEQ
                    o = bank[6 + h // 4]
                    pe.matmul(o[r, c:c + SEQ], vv[:, 0, h, :], pT[:, h % 2, 0:SEQ], start=True, stop=False)
                    pe.matmul(o[r, c + P:c + SEQ], vv[:, 1, h, :], pT[:, h % 2, SEQ:], start=False, stop=True).then_inc(o_p, 1)

                pe.wait_ge(q_r, l + 1)
                pe.wait_ge(decay_r, l + 1)
                pe.wait_ge(k_r, l + 1)
                pe.wait_ge(kr_c, l + 1)

                def out_product(c):
                    s = chunk(first, 8 + c)
                    for b in range(NB):
                        for kk in range(2):
                            kt = 2 * c + kk
                            for j in range(2):
                                m, n = slice(b * P, (b + 1) * P), slice(kk * D + 512 * j, kk * D + 512 * (j + 1))
                                ins = three(bank[2 * b + j][:], act_hi[:, kt, m], act_lo[:, kt, m], w_hi[:, s, n], w_lo[:, s, n],
                                            start=(kt == 0), stop=(kt == KT - 1))
                        if b == 0 and c == 3:
                            ins.then_inc(first_rows, 1)
                    ins.then_inc(used, 1)

                for i in range(N_HEADS + 3):
                    if i == 1:
                        pe.wait_ge(gate_t, l + 1)
                    if i == 2:
                        pe.wait_ge(v_r, l + 1)
                    if i < N_HEADS:
                        qk_turn(i)
                    if 1 <= i <= N_HEADS:
                        scores(i - 1)
                    if 2 <= i <= N_HEADS + 1:
                        p_turn(i - 2)
                    if i >= 3:
                        values(i - 3)
                    if i == N_HEADS:
                        pe.wait_ge(lru_lo, l + 1)
                        pe.wait_ge(s_r, N_HEADS * (l + 1))
                        out_product(0)
                    if i == N_HEADS + 1:
                        out_product(1)
                for c in (2, 3):
                    pe.wait_ge(o_lo, 2 * l + c - 1)
                    out_product(c)
                norm_turn(2 * l + 1)
                if l == 0:
                    gate_up, turn, down = ffn_products(NB, DENSE_UNITS, DENSE_ORDER, FIRST["dense", 0], 0, 0)
                    for s in range(DENSE_UNITS + 2):
                        if s < DENSE_UNITS:
                            gate_up(s)
                        if 1 <= s <= DENSE_UNITS:
                            turn(s - 1)
                        if s >= 2:
                            down(s - 2)

            pe.wait_ge(rw_r, 1)
            for kt in range(KT):
                if kt % 2 == 0:
                    pe.wait_ge(nT_lo, 4 * 3 + kt // 2 + 1)
                n = slice(kt * E, (kt + 1) * E)
                ins = three(bank[0][0:E, 0:SEQ], rw_hi[:, n], rw_lo[:, n], act_hi[:, kt, :], act_lo[:, kt, :],
                            start=(kt == 0), stop=(kt == KT - 1))
            ins.then_inc(lg_p, 1)
            pe.wait_ge(lgT_r, 1)
            for b in range(NB):
                ins = pe.transpose(bank[1][:, b * E:(b + 1) * E], lgT[:, b * P:(b + 1) * P], ident[0:E, 0:E])
            ins.then_inc(lg_p, 1)
            pe.wait_ge(pick_r, 1)
            pe.wait_ge(consts, 2)
            pe.matmul(bank[1][:, 0:E], before, pick[:, 0, :], start=True, stop=True)
            pe.matmul(bank[1][:, E:2 * E], before, pick[:, 1, :], start=True, stop=False)
            pe.matmul(bank[1][:, E:2 * E], ones, pick[:, 0, :], start=False, stop=True)
            for b in range(NB):
                ins = pe.matmul(bank[1][:, 2 * E:3 * E], ones, pick[:, b, :], start=(b == 0), stop=(b == NB - 1))
            ins.then_inc(place_p, 1)
            def products(j):
                return ffn_products(1, UNITS, EXPERT_ORDER, EXPERT0, DENSE_U + UNITS * j, j)

            def gather(j):
                pe.wait_ge(sel_r, j + 1)
                for kt in range(KT):
                    f = slice(kt * P, (kt + 1) * P)
                    for b in range(NB):
                        for k in (2, 1, 0):
                            ins = pe.matmul(bank[kt // 4][:, (kt % 4) * P:(kt % 4 + 1) * P], xg[k][:, b, f], sel[:, b, :],
                                            start=(b == 0 and k == 2), stop=(b == NB - 1 and k == 0))
                ins.then_inc(xT_p, 1)

            def scatter(i):
                pe.wait_ge(yg_lo, i + 1)
                for b in (1, 0):
                    for j in range(2):
                        w = slice(512 * j, 512 * (j + 1))
                        pe.matmul(bank[2 * b + j][:], sel_t[:, b, :], y_lo[:, w], start=True, stop=False)
                        ins = pe.matmul(bank[2 * b + j][:], sel_t[:, b, :], y_hi[:, w], start=False, stop=True)
                ins.then_inc(sc_p, 1)

            def job_begin(j):
                gate_up, turn, down = products(j)
                pe.wait_ge(xT_lo, j + 1)
                gate_up(0)
                gate_up(1)
                for b in range(NB):
                    ins = pe.matmul(bank[7][:, b * P:(b + 1) * P], sel[:, b, :], ident_b[:], start=True, stop=True)
                ins.then_inc(sT_p, 1)
                turn(0)

            def job(i, more):
                gate_up, turn, down = products(i)
                for s in range(2, UNITS):
                    gate_up(s)
                    if s == 2:
                        pe.wait_ge(sT_r, i + 1)
                    turn(s - 1)
                    if s == 2:
                        pe.wait_ge(sc_r, NB * i + 1)
                    down(s - 2)
                if more:
                    gather(i + 1)
                turn(UNITS - 1)
                down(UNITS - 2)
                down(UNITS - 1)
                if more:
                    job_begin(i + 1)
                scatter(i)

            pe.wait_ge(xg_v, 2 * NB)
            gather(0)
            job_begin(0)
            pe.wait_ge(jobs_r, 1)
            last = pe.value_load(jobs[0:1, 0:1], min_val=E - 1, max_val=E - 1 + MORE)
            with pe.Fori(0, last) as i:
                job(i, True)
            job(last, False)


_INS = ['x', 'positions', 'norm_mix', 'w_in', 'conv_w', 'conv_b', 'lru_wa', 'lru_ba', 'lru_wx', 'lru_bx',
        'lru_lambda', 'q_norm', 'w_uq', 'kv_norm', 'w_ukv', 'w_out', 'norm_ffn', 'dense_w_gate',
        'dense_w_up', 'dense_w_down', 'router_w', 'expert_w_gate', 'expert_w_up', 'expert_w_down',
        'norm_final']


def kernel(**inputs):
    import concourse.bacc as _bacc
    from concourse.bass_utils import run_bass_kernel_spmd as _run

    nc = _bacc.Bacc("TRN2", target_bir_lowering=False, num_devices=1)
    arrays, args = {}, []
    for name in _INS:
        a = np.ascontiguousarray(inputs[name])
        arrays[f"in_{name}"] = a
        args.append(nc.dram_tensor(f"in_{name}", a.shape, mybir.dt.from_np(a.dtype), kind="ExternalInput").ap())
    out = nc.dram_tensor("out_x", inputs["x"].shape, F32, kind="ExternalOutput").ap()
    trunk(nc, *args, out)
    return _run(nc, [arrays], core_ids=[0]).results[0]["out_x"]
```

```python
import math
from contextlib import ExitStack

import numpy as np
import concourse.bass as bass
from concourse import mybir

P = 128
BF16 = mybir.dt.bfloat16
F32, F32R, I32, U32 = mybir.dt.float32, mybir.dt.float32r, mybir.dt.int32, mybir.dt.uint32
ALU = mybir.AluOpType
ACT = mybir.ActivationFunctionType
AX = mybir.AxisListType.X

EPS = 1e-6
CONV_W = 4
N_HEADS = 8
QK_NOPE, QK_ROPE, V_HEAD = 64, 32, 64
QK = QK_NOPE + QK_ROPE
HALF = QK_ROPE // 2
ROPE_THETA = 10000.0
TOP_K = 2
LRU_C = 8.0

RAW = 7
SPLIT = 3
CHUNK = 2048
FW = 256
MASKED = -1e30


def trunk(nc, x, positions, norm_mix, w_in, conv_w, conv_b, lru_wa, lru_ba, lru_wx, lru_bx,
          lru_lambda, q_norm, w_uq, kv_norm, w_ukv, w_out, norm_ffn, dense_w_gate, dense_w_up,
          dense_w_down, router_w, expert_w_gate, expert_w_up, expert_w_down, norm_final, out):
    DEPTH, D, IN_COLS = w_in.shape
    SEQ = x.shape[1]
    NB = SEQ // P
    KT = D // P
    LW = conv_w.shape[2]
    LT = LW // P
    QL, KVL = w_uq.shape[1], w_ukv.shape[1]
    CT = (QL + KVL) // P
    ZT = IN_COLS - 2 * LW
    E = expert_w_gate.shape[1]
    DENSE_UNITS = dense_w_gate.shape[2] // FW
    UNITS = expert_w_gate.shape[3] // FW
    SCALE = 1.0 / math.sqrt(QK)
    MORE = (NB * P * TOP_K) // (P + 1)
    JOBS = E + MORE
    assert NB == 2 and DEPTH == 2 and KT == 8 and LT == 4 and UNITS == 7 and SEQ == 256

    MIX_CHUNKS = 12

    def ffn_order(units, lag):
        order = []
        for s in range(units + lag):
            if s < units:
                order += [("gu", s, 0), ("gu", s, 1)]
            if s >= lag:
                order.append(("down", s - lag, 0))
        return order

    DENSE_ORDER = ffn_order(DENSE_UNITS, 1)
    EXPERT_ORDER = ffn_order(UNITS, 2)
    FIRST = {("mix", 0): 0, ("dense", 0): MIX_CHUNKS,
             ("mix", 1): MIX_CHUNKS + len(DENSE_ORDER)}
    EXPERT0 = FIRST["mix", 1] + MIX_CHUNKS
    PER_JOB = len(EXPERT_ORDER)
    assert PER_JOB % RAW == 0 and PER_JOB % SPLIT == 0
    DENSE_U = DENSE_UNITS
    SLOTS = 3

    ctx = ExitStack()
    with ctx:
        def sb(name, shape, dt=F32):
            return ctx.enter_context(nc.sbuf_tensor(name, shape, dt))

        def sem(name):
            return ctx.enter_context(nc.semaphore(name))

        raw = sb("raw", [P, RAW, CHUNK])
        w_hi = sb("w_hi", [P, SPLIT, CHUNK], F32R)
        w_lo = sb("w_lo", [P, SPLIT, CHUNK], F32R)
        xs = sb("xs", [P, NB, D])
        xn = sb("xn", [P, NB, D])
        act_hi = sb("act_hi", [P, KT, SEQ], F32R)
        act_lo = sb("act_lo", [P, KT, SEQ], F32R)
        sm_hi = sb("sm_hi", [P, SLOTS, NB, FW], F32R)
        sm_lo = sb("sm_lo", [P, SLOTS, NB, FW], F32R)
        c_hi = sm_hi[:, :, 0, :]
        c_lo = sm_lo[:, :, 0, :]
        xc = sb("xc", [P, LT, SEQ])
        yg = sb("yg", [P, LT, SEQ])
        gg = sb("gg", [P, LT, SEQ])
        mixer_base = nc.sbuf_base
        xl = sb("xl", [P, LT, CONV_W - 1 + SEQ])
        ta = sb("ta", [P, LT, SEQ])
        tb = sb("tb", [P, LT, SEQ])
        tr = sb("tr", [P, LT, SEQ])
        ts = sb("ts", [P, LT, SEQ])
        kcat = sb("kcat", [P, NB, N_HEADS, QK])
        vv = sb("vv", [P, NB, N_HEADS, V_HEAD])
        cn = tr[:, 0:CT, :].rearrange("p t n -> p (t n)").rearrange("p (b n) -> p b n", b=NB)
        qcat = xn[:, :, 0:N_HEADS * QK].rearrange("p b (h d) -> p b h d", h=N_HEADS)
        qkT = sb("qkT", [QK, 2, 2 * SEQ])
        pr = sb("pr", [P, 2, 3 * P])
        pT = sb("pT", [P, 2, 3 * P])
        rope_a, rope_b = (pr[:, k, 0:N_HEADS * QK_ROPE].rearrange("p (h d) -> p h d", h=N_HEADS) for k in range(2))
        kr = sb("kr", [P, NB, QK_ROPE])
        gate_bd = sb("gate_bd", [P, 2, LT, P])
        mixer_end = nc.sbuf_base
        ident = sb("ident", [P, P])
        mask = sb("mask", [P, 3 * P])
        rows = yg[0:102, 3, 0:P]
        prm = sb("prm", [P, 102])
        lru_c = sb("lru_c", [P, 4, DEPTH * LT])
        pos_i = sb("pos_i", [P, NB], I32)
        pos_f = sb("pos_f", [P, NB])
        inv = sb("inv", [P, HALF])
        ang = yg[:, 0, 0:NB * HALF].rearrange("p (b n) -> p b n", b=NB)
        turn = yg[:, 1, 0:2 * NB * HALF].rearrange("p (w b n) -> p w b n", w=2, b=NB)
        trig_in = yg[:, 2, 0:2 * NB * HALF].rearrange("p (w b n) -> p w b n", w=2, b=NB)
        trig = sb("trig", [P, 2, NB, HALF])
        ssq = sb("ssq", [P, NB])
        mean = sb("mean", [P, NB])
        rstd = sb("rstd", [P, NB])
        zssq = sb("zssq", [P, 2, NB])
        zmean = sb("zmean", [P, 2, NB])
        zrstd = sb("zrstd", [P, 2, NB])
        mhalf = sb("mhalf", [P, 4])
        mx = sb("mx", [P, 2, 2])
        nmx = sb("nmx", [P, 2, 2])
        rs = sb("rs", [P, 2, 2])
        ri = sb("ri", [P, 2, 2])
        grow = xc[:, :, :].rearrange("p t n -> p (t n)")
        sg = yg[:, 0:2, :]
        hid = yg[:, 2:4, :]
        expert_at = [mixer_base]

        def over(name, shape, dt=F32R):
            at = (expert_at[0] + 31) // 32 * 32
            expert_at[0] = at + (2 if dt == BF16 else 4) * int(np.prod(shape[1:]))
            assert expert_at[0] <= mixer_end
            return nc.alloc_sbuf_tensor_at(name, shape, dt, offset=at)

        y_hi, y_lo = over("y_hi", [P, D]), over("y_lo", [P, D])
        sel_t = over("sel_t", [P, NB, P])
        xg = [over(f"xg{k}", [P, NB, D], BF16) for k in range(3)]
        sel = over("sel", [P, NB, P], BF16)
        xgain = over("xgain", [P, NB, D], F32)
        wide = over("wide", [P, 2, MORE, NB, E], F32)
        lgT = nc.alloc_sbuf_tensor_at("lgT", [E, SEQ], F32, offset=(expert_at[0] + 31) // 32 * 32)
        expert_at[0] = (expert_at[0] + 31) // 32 * 32 + 4 * SEQ
        cur = over("cur", [P, 2, NB], F32)
        ident_b = over("ident_b", [P, P], BF16)
        before = gg[:, 0, 0:P]
        ones = gg[:, 0, P:2 * P]
        slot = gg[:, 1, 0:P]
        rw = gg[:, 3, 0:KT * E]
        rw_hi, rw_lo = (w[:, 0, 1, 0:KT * E] for w in (sm_hi, sm_lo))
        lg, top, topi, topf = (gg[:, 2, 16 * k:16 * k + 16].rearrange("p (b e) -> p b e", b=NB) for k in range(4))
        topi = topi.bitcast(U32)
        oh = gg[:, 2, 64:64 + 2 * NB * E].rearrange("p (k b e) -> p k b e", k=2, b=NB)
        pick = gg[:, 3, 64:80].rearrange("p (b e) -> p b e", b=NB)
        gates, place = (gg[:, 3, 80 + NB * JOBS * k:80 + NB * JOBS * (k + 1)].rearrange("p (b e) -> p b e", b=NB) for k in range(2))
        i8 = sb("i8", [P, E])
        dif = sb("dif", [P, NB])
        tw = sb("tw", [P, 2, NB])
        jb = gg[:, 3, 160:160 + 8 * E].rearrange("p (k e) -> p k e", k=8)
        jf = sb("jf", [1, 4])
        jobs = sb("jobs", [1, 4], I32)

        bank = [ctx.enter_context(nc.psum_tensor(f"bank{i}", [P, 512], F32)) for i in range(8)]

        landed = [sem(f"landed{i}") for i in range(RAW)]
        hi_made, lo_made = sem("hi_made"), sem("lo_made")
        used = sem("used")
        x_in = [sem(f"x_in{b}") for b in range(NB)]
        rows_in, pos_in, rw_in, wout_s = sem("rows_in"), sem("pos_in"), sem("rw_in"), sem("stored")
        bd_in, grow_in = sem("bd_in"), sem("grow_in")
        bd_zero, consts = sem("bd_zero"), sem("consts")
        prm_t, prm_r = sem("prm_t"), sem("prm_r")
        lam_e, lru_r = sem("lam_e"), sem("lru_r")
        angle_r, trig_r = sem("angle_r"), sem("trig_r")
        ss_r, rstd_r, xn_v = sem("ss_r"), sem("rstd_r"), sem("xn_v")
        nT, nT_hi, nT_lo = sem("nT"), sem("nT_hi"), sem("nT_lo")
        xl_r, yg_r = sem("xl_r"), sem("yg_r")
        zss_r, zrstd_r, cn_r, kr_r, kr_c = sem("zss_r"), sem("zrstd_r"), sem("cn_r"), sem("kr_r"), sem("kr_c")
        cT, cT_hi, cT_lo = sem("cT"), sem("cT_hi"), sem("cT_lo")
        q_c, q_r, k_r, v_r = sem("q_c"), sem("q_r"), sem("k_r"), sem("v_r")
        xc_r, gate_p, gate_t = sem("xc_r"), sem("gate_p"), sem("gate_t")
        decay_r, a_r = sem("decay_r"), sem("a_r")
        sq_r, gin_r, gth_r, gg_r, iw_r = sem("sq_r"), sem("gin_r"), sem("gth_r"), sem("gg_r"), sem("iw_r")
        lru_o, lru_lo = sem("lru_o"), sem("lru_lo")
        qkT_p, qkT_r, s_p, s_r, p_r, pn_r, pT_p, pT_r, o_p, o_hi, o_lo = (
            sem("qkT_p"), sem("qkT_r"), sem("s_p"), sem("s_r"), sem("p_r"), sem("pn_r"), sem("pT_p"),
            sem("pT_r"), sem("o_p"), sem("o_hi"), sem("o_lo"))
        mix_r, first_rows = sem("mix_r"), sem("first_rows")
        sg_r, hid_r, hT_p, hT_hi, hT_lo = (
            sem("sg_r"), sem("hid_r"), sem("hT_p"), sem("hT_hi"), sem("hT_lo"))
        y_r = sem("y_r")
        rw_h, rw_r, lg_p, lg_r, tw_r, pick_r, place_p, jobs_r, xg_r, lgT_r = (
            sem("rw_h"), sem("rw_r"), sem("lg_p"), sem("lg_r"), sem("tw_r"), sem("pick_r"),
            sem("place_p"), sem("jobs_r"), sem("xg_r"), sem("lgT_r"))
        sel_r, xT_p, xT_hi, xT_lo, sT_p, sT_r, yg_hi, yg_lo, sc_p, sc_r, xg_a, xg_v, cur_r, gate_r = (
            sem("sel_r"), sem("xT_p"), sem("xT_hi"), sem("xT_lo"), sem("sT_p"), sem("sT_r"),
            sem("yg_hi"), sem("yg_lo"), sem("sc_p"), sem("sc_r"), sem("xg_a"), sem("xg_v"), sem("cur_r"), sem("gate_r"))
        out_r = sem("out_r")
        a_ch, v_ch, g_ch = sem("scalar_step"), sem("vector_step"), sem("pool_step")

        def stepper(eng, s):
            n = [0]

            def step(*ins):
                n[0] += 1
                ins[-1].then_inc(s, 1)
                eng.wait_ge(s, n[0])
            return step

        def raw_slot(first, c):
            return (first + c) % RAW

        def raw_turn(first, c, i=0):
            return (first + c) // RAW + 1 + i * (PER_JOB // RAW)

        def split_slot(first, c):
            return (first + c) % SPLIT

        def nth(first, c, i=0):
            return first + c + i * PER_JOB

        def by_tile(w):
            return w.rearrange("(k p) n -> p k n", p=P)

        def mix_sources(l):
            win, wout = by_tile(w_in[l]), by_tile(w_out[l])
            for c0, wd, k in ((2 * LW, ZT, 0), (2 * LW, ZT, 4), (0, LW, 0), (0, LW, 4), (LW, LW, 0)):
                yield wd, 4, win[:, k:k + 4, c0:c0 + wd]
            yield N_HEADS * QK, QL // P, by_tile(w_uq[l])
            yield LW, 4, win[:, 4:8, LW:2 * LW]
            yield w_ukv.shape[2], KVL // P, by_tile(w_ukv[l])
            for k in range(0, KT, 2):
                yield D, 2, wout[:, k:k + 2, :]

        def load_ffn(eng, order, first, gate, up, down, i=0, pairs=True):
            g, u = by_tile(gate), by_tile(up)
            d = down.rearrange("(s p j) n -> s j p n" if pairs else "(s j p) n -> s j p n", p=P, j=2)
            for c, (kind, s, k) in enumerate(order):
                r = raw[:, raw_slot(first, c), :]
                eng.wait_ge(lo_made, nth(first, c, i) - RAW + 1)
                if kind == "gu":
                    dst = r.rearrange("p (k w n) -> p k w n", k=4, w=2)
                    for w, src in enumerate((g, u)):
                        eng.dma_start(dst[:, :, w, :], src[:, 4 * k:4 * k + 4, s * FW:(s + 1) * FW]
                                      ).then_inc(landed[raw_slot(first, c)], 16)
                else:
                    for j in range(2):
                        h = slice(j * CHUNK // 2, (j + 1) * CHUNK // 2)
                        eng.dma_start(r[:, h], d[s, j]).then_inc(landed[raw_slot(first, c)], 16)

        def dense(ops, chunk):
            finish, split = ops
            c = 2
            for s in range(-1, DENSE_UNITS):
                if s >= 0:
                    finish(s)
                    split(s)
                    chunk(c)
                    c += 1
                if s + 2 < DENSE_UNITS:
                    chunk(c)
                    chunk(c + 1)
                    c += 2

        def job_start(ops, chunk, outputs, scattered, scattered_too):
            finish, turned = ops
            chunk(1)
            outputs()
            chunk(2)
            chunk(3)
            finish(0)
            chunk(4)
            chunk(5)
            turned(0)
            finish(1)
            scattered()
            chunk(6)
            scattered_too()

        def job_rest(ops, chunk, matrix, gathered, next_chunk):
            finish, turned = ops
            chunk(7)
            turned(1)
            chunk(8)
            for s in range(3, UNITS):
                finish(s - 1)
                chunk(3 * s)
                chunk(3 * s + 1)
                turned(s - 1)
                if s == UNITS - 1:
                    finish(s)
                if s == 4:
                    matrix()
                chunk(3 * s + 2)
            next_chunk()
            turned(UNITS - 1)
            gathered()

        def two(t):
            return t.rearrange("p j n -> p (j n)")

        def act_dense_ops(act, gu_done):
            def finish(s):
                act.wait_ge(used, gu_done(s))
                act.activation(two(sg), bank[4 + 2 * (s % 2)][:], ACT.Silu).then_inc(sg_r, 1)

            def split(s):
                act.wait_ge(hid_r, s + 1)
                act.activation(two(sm_hi[:, s % SLOTS]), two(hid), ACT.Copy).then_inc(hT_hi, 1)
            return finish, split

        def vec_dense_ops(dve):
            def finish(s):
                dve.wait_ge(sg_r, s + 1)
                if s:
                    dve.wait_ge(hT_lo, s)
                dve.tensor_tensor(two(hid), two(sg), bank[5 + 2 * (s % 2)][:], ALU.mult).then_inc(hid_r, 1)

            def split(s):
                dve.wait_ge(hT_hi, s + 1)
                dve.tensor_tensor(two(sm_lo[:, s % SLOTS]), two(hid), two(sm_hi[:, s % SLOTS]).bitcast(F32),
                                  ALU.subtract).then_inc(hT_lo, 1)
            return finish, split

        def act_unit_ops(act, u0, t0, gu_done):
            def finish(s):
                act.wait_ge(used, gu_done(s))
                act.activation(sg[:, s % 2, :], bank[4 + s % 2][:, 0:FW], ACT.Silu).then_inc(sg_r, 1)

            def turned(s):
                act.wait_ge(hT_p, t0 + s + 1)
                act.activation(sm_hi[:, s % SLOTS, 0, :], bank[6 + s % 2][:, 0:FW], ACT.Copy).then_inc(hT_hi, 1)
            return finish, turned

        def vec_unit_ops(dve, u0):
            def finish(s):
                dve.wait_ge(sg_r, u0 + s + 1)
                dve.tensor_tensor(hid[:, s % 2, :], sg[:, s % 2, :], bank[4 + s % 2][:, FW:2 * FW], ALU.mult).then_inc(hid_r, 1)

            def turned(s):
                dve.wait_ge(hT_hi, u0 + s + 1)
                dve.tensor_tensor(sm_lo[:, s % SLOTS, 0, :], bank[6 + s % 2][:, 0:FW],
                                  sm_hi[:, s % SLOTS, 0, :].bitcast(F32), ALU.subtract).then_inc(hT_lo, 1)
            return finish, turned

        block = ctx.enter_context(nc.Block())

        @block.sync
        def _(sp):
            for b in range(NB):
                sp.dma_start(xs[:, b, :], x[0, b * P:(b + 1) * P, :]).then_inc(x_in[b], 16)
            def load_mix(l, c0, c1):
                first = FIRST["mix", l]
                for c, (wd, k, src) in tuple(enumerate(mix_sources(l)))[c0:c1]:
                    if first + c >= RAW:
                        sp.wait_ge(lo_made, first + c - RAW + 1)
                    s = raw_slot(first, c)
                    dst = raw[:, s, 0:k * wd].rearrange("p (k n) -> p k n", k=k)
                    for j in range(2):
                        ks, ns = ((slice(j * k // 2, (j + 1) * k // 2), slice(0, wd)) if k > 1 else
                                  (slice(0, 1), slice(j * wd // 2, (j + 1) * wd // 2)))
                        sp.dma_start(dst[:, ks, ns], src[:, ks, ns]).then_inc(landed[s], 16)

            def load_gates(l):
                for w, src in enumerate((lru_wa, lru_wx)):
                    for q in range(2):
                        sp.dma_start(gate_bd[64 * q:64 * q + 64, w, :, 64 * q:64 * q + 64],
                                     src[l].rearrange("(t q) c d -> q c t d", q=2)[q]).then_inc(bd_in, 16)

            load_mix(0, 0, 1)
            r0 = 0
            for v in (norm_mix.rearrange("l (k p) -> (l k) p", p=P),
                      norm_ffn.rearrange("l (k p) -> (l k) p", p=P),
                      conv_w.rearrange("l j (t p) -> (l j t) p", p=P),
                      conv_b.rearrange("l (t p) -> (l t) p", p=P),
                      lru_ba.rearrange("l (t q) c -> (l t) (q c)", q=2),
                      lru_bx.rearrange("l (t q) c -> (l t) (q c)", q=2),
                      lru_lambda.rearrange("l (t p) -> (l t) p", p=P),
                      q_norm.rearrange("l (k p) -> (l k) p", p=P),
                      kv_norm.rearrange("l (k p) -> (l k) p", p=P)):
                sp.dma_start(rows[r0:r0 + v.shape[0], :], v).then_inc(rows_in, 16)
                r0 += v.shape[0]
            sp.dma_start(pos_i[:, :], positions.rearrange("o (b p) -> p (o b)", p=P),
                         allow_slow_non_contiguous=True).then_inc(pos_in, 16)
            load_mix(0, 1, 4)
            sp.wait_ge(bd_zero, 1)
            load_gates(0)
            load_mix(0, 4, MIX_CHUNKS)
            sp.wait_ge(gate_p, 2)
            load_gates(1)
            load_ffn(sp, DENSE_ORDER, FIRST["dense", 0], dense_w_gate[0], dense_w_up[0], dense_w_down[0],
                     pairs=False)
            load_mix(1, 0, MIX_CHUNKS)

            def job(i, e):
                load_ffn(sp, EXPERT_ORDER, EXPERT0, *(w[0, bass.ds(e, 1)].rearrange("o a b -> (o a) b")
                                                      for w in (expert_w_gate, expert_w_up, expert_w_down)), i=i)

            with sp.Fori(0, E) as i:
                job(i, i)
            sp.wait_ge(jobs_r, 1)
            last = sp.value_load(jobs[0:1, 0:1], min_val=E - 1, max_val=E - 1 + MORE)
            with sp.If(last > E - 1):
                with sp.Fori(E, last + 1) as i:
                    e = sp.value_load(jobs[0:1, bass.ds(i - (E - 1), 1)], min_val=0, max_val=E - 1)
                    job(i, e)
            for b in range(NB):
                sp.wait_ge(out_r, b + 1)
                sp.dma_start(out[0, b * P:(b + 1) * P, :], xn[:, b, :]).then_inc(wout_s, 16)
            sp.wait_ge(wout_s, 16 * NB)

        @block.gpsimd
        def _(pool):
            step = stepper(pool, g_ch)
            pool.memset(gate_bd[:], 0.0).then_inc(bd_zero, 1)
            pool.memset(mhalf[:], -0.5)
            for j in range(HALF):
                pool.memset(inv[:, j:j + 1], float(np.float32(1.0) / np.float32(ROPE_THETA) ** np.float32(j / HALF)))
            pool.memset(xl[:, :, 0:CONV_W - 1], 0.0)
            step(pool.memset(ident[:], 0.0))
            pool.affine_select(out=ident[:], in_=ident[:], compare_op=ALU.not_equal, fill=1.0, base=0,
                               pattern=[[-1, P]], channel_multiplier=1)
            step(pool.memset(mask[:], 0.0))
            for c in (0, 2 * P):
                pool.affine_select(out=mask[:, c:c + P], in_=mask[:, c:c + P], compare_op=ALU.is_ge,
                                   fill=MASKED, base=0, pattern=[[-1, P]], channel_multiplier=1)
            pool.iota(i8[:], pattern=[[1, E]], base=0, channel_multiplier=0,
                      allow_small_or_imprecise_dtypes=True).then_inc(consts, 1)

            def rms(k):
                for b in range(NB):
                    pool.wait_ge(ss_r, NB * k + b + 1)
                    step(pool.tensor_scalar(mean[:, b:b + 1], ssq[:, b:b + 1], 1.0 / D, EPS, ALU.mult, ALU.add))
                    pool.tensor_tensor(rstd[:, b:b + 1], mean[:, b:b + 1], mhalf[:, 0:1], ALU.pow).then_inc(rstd_r, 1)

            for l in range(DEPTH):
                rms(2 * l)
                pool.wait_ge(zss_r, l + 1)
                for w, n in enumerate((QL, KVL)):
                    ins = pool.tensor_scalar(zmean[:, w, :], zssq[:, w, :], 1.0 / n, EPS, ALU.mult, ALU.add)
                step(ins)
                pool.tensor_tensor(zrstd[:].rearrange("p w b -> p (w b)"), zmean[:].rearrange("p w b -> p (w b)"),
                                   mhalf[:], ALU.pow).then_inc(zrstd_r, 1)
                pool.wait_ge(kr_r, l + 1)
                for b in range(NB):
                    ins = pool.tensor_copy(kcat[:, b, :, QK_NOPE:], kr[:, b, :].unsqueeze(1).to_broadcast([P, N_HEADS, QK_ROPE]))
                ins.then_inc(kr_c, 1)
                pool.wait_ge(yg_r, l + 1)
                step(pool.tensor_tensor(gg[:], yg[:], yg[:], ALU.mult))
                step(pool.tensor_scalar(gg[:], gg[:], 0.044715, 1.0, ALU.mult, ALU.add))
                pool.tensor_tensor(gg[:], gg[:], yg[:], ALU.mult).then_inc(gin_r, 1)
                pool.wait_ge(gate_t, l + 1)
                pool.wait_ge(xc_r, l + 1)
                step(pool.tensor_scalar(tb[:], tb[:], 1.0, 1.0, ALU.mult, ALU.add))
                pool.tensor_tensor(tb[:], tb[:], xc[:], ALU.mult).then_inc(iw_r, 1)
                pool.wait_ge(gth_r, l + 1)
                step(pool.tensor_scalar(gg[:], gg[:], 1.0, 1.0, ALU.mult, ALU.add))
                pool.tensor_tensor(gg[:], gg[:], yg[:], ALU.mult).then_inc(gg_r, 1)
                pool.wait_ge(lru_o, l + 1)
                step(pool.tensor_copy(act_hi[:, 0:LT, :], ts[:]))
                pool.tensor_tensor(act_lo[:, 0:LT, :], ts[:], act_hi[:, 0:LT, :].bitcast(F32), ALU.subtract).then_inc(lru_lo, 1)
                if l == DEPTH - 1:
                    pool.dma_start(rw.rearrange("p (k e) -> p k e", k=KT), router_w[0].rearrange("(k p) e -> p k e", p=P)).then_inc(rw_in, 16)
                    pool.dma_start(grow, norm_ffn[1].partition_broadcast(P)).then_inc(grow_in, 16)
                    step(pool.memset(before, 1.0))
                    pool.affine_select(out=before, in_=before, compare_op=ALU.is_gt, fill=0.0, base=0,
                                       pattern=[[1, P]], channel_multiplier=-1)
                    pool.memset(ones, 1.0)
                    pool.iota(slot, pattern=[[1, P]], base=0, channel_multiplier=0,
                              allow_small_or_imprecise_dtypes=True).then_inc(consts, 1)
                rms(2 * l + 1)
            pool.wait_ge(grow_in, 16)
            for b in range(NB):
                pool.wait_ge(xn_v, NB * (2 * DEPTH - 1) + b + 1)
                if b == 0:
                    pool.tensor_copy(ident_b[:], ident[:])
                pool.tensor_tensor(xgain[:, b, :], xn[:, b, :], grow, ALU.mult).then_inc(xg_r, 1)
            pool.wait_ge(xg_r, NB)
            pool.dma_start(grow, norm_final.partition_broadcast(P)).then_inc(grow_in, 16)
            rms(2 * DEPTH)

        @block.scalar
        def _(act):
            step = stepper(act, a_ch)

            def hi(first, c, width=CHUNK, i=0):
                act.wait_ge(landed[raw_slot(first, c)], 32 * raw_turn(first, c, i))
                if isinstance(i, int) and i == 0 and first + c < SPLIT:
                    pass
                else:
                    act.wait_ge(used, nth(first, c, i) - SPLIT + 1)
                act.activation(w_hi[:, split_slot(first, c), 0:width], raw[:, raw_slot(first, c), 0:width],
                               ACT.Copy).then_inc(hi_made, 1)

            def squares(ready):
                for b in range(NB):
                    act.wait_ge(*ready(b))
                    act.activation(xn[:, b, :], xs[:, b, :], ACT.Square, accum_out=ssq[:, b:b + 1]).then_inc(ss_r, 1)

            def norm(k, ready):
                squares(ready)

            def norm_split(k, gain0):
                for j in range(4):
                    act.wait_ge(nT, 4 * k + j + 1)
                    for t in range(2):
                        kt = 2 * j + t
                        ins = act.activation(act_hi[:, kt, :], bank[4 - 4 * (k % 2) + j][:, t * SEQ:(t + 1) * SEQ], ACT.Copy,
                                             scale=prm[:, gain0 + kt:gain0 + kt + 1])
                    ins.then_inc(nT_hi, 1)

            for l in range(DEPTH):
                first = FIRST["mix", l]
                if l:
                    hi(first, 0, 4 * ZT)
                    hi(first, 1, 4 * ZT)
                    norm(2 * l, lambda b: (y_r, b + 1))
                else:
                    norm(0, lambda b: (x_in[b], 16))
                    hi(first, 0, 4 * ZT)
                    act.wait_ge(prm_r, 1)
                norm_split(2 * l, l * KT)
                if l == 0:
                    hi(first, 1, 4 * ZT)
                    act.activation(lru_c[:, 0, :], prm[:, 88:96], ACT.Exp, scale=-1.0).then_inc(lam_e, 1)
                    act.wait_ge(lam_e, 1)
                    act.activation(lru_c[:, 0, :], lru_c[:, 0, :], ACT.Ln, bias=1.0).then_inc(lam_e, 1)
                    act.wait_ge(angle_r, 1)
                    act.activation(trig[:], trig_in, ACT.Sin).then_inc(trig_r, 1)
                hi(first, 2)
                hi(first, 3)
                act.wait_ge(used, first + 2)
                for b in range(NB):
                    act.activation(cn[:, b, 0:QL], bank[b][:, 0:QL], ACT.Square, accum_out=zssq[:, 0, b:b + 1])
                    ins = act.activation(cn[:, b, QL:], bank[b][:, QL:QL + KVL], ACT.Square, accum_out=zssq[:, 1, b:b + 1])
                ins.then_inc(zss_r, 1)
                hi(first, 4)
                act.wait_ge(used, first + 4)
                for j in range(2):
                    ins = act.activation(xl[:, 2 * j:2 * j + 2, CONV_W - 1:],
                                         bank[4 + j][:].rearrange("p (t n) -> p t n", t=2), ACT.Copy)
                ins.then_inc(xl_r, 1)
                act.wait_ge(cT, l + 1)
                for t in range(CT):
                    g = 96 + 2 * l + t if t < QL // P else 100 + l
                    ins = act.activation(c_hi[:, t, :], bank[2 + t // 2][:, (t % 2) * SEQ:(t % 2 + 1) * SEQ], ACT.Copy,
                                         scale=prm[:, g:g + 1])
                ins.then_inc(cT_hi, 1)
                hi(first, 5, QL // P * N_HEADS * QK)
                hi(first, 6)
                hi(first, 7, KVL // P * w_ukv.shape[2])
                hi(first, 8)
                act.wait_ge(gate_p, 2 * l + 1)
                act.wait_ge(lru_r, 1)
                for t in range(LT):
                    c = l * LT + t
                    ins = act.activation(ta[:, t, :], bank[t // 2][:, (t % 2) * SEQ:(t % 2 + 1) * SEQ], ACT.Tanh,
                                         scale=0.5, bias=lru_c[:, 1, c:c + 1])
                step(ins)
                for t in range(LT):
                    c = l * LT + t
                    ins = act.activation(tr[:, t, :], ta[:, t, :], ACT.Tanh, scale=lru_c[:, 0, c:c + 1],
                                         bias=lru_c[:, 0, c:c + 1])
                ins.then_inc(decay_r, 1)
                act.wait_ge(used, first + 7)
                for j in range(2):
                    ins = act.activation(yg[:, 2 * j:2 * j + 2, :], bank[6 + j][:].rearrange("p (t n) -> p t n", t=2), ACT.Copy)
                ins.then_inc(yg_r, 1)
                act.wait_ge(gate_p, 2 * l + 2)
                for t in range(LT):
                    c = l * LT + t
                    ins = act.activation(tb[:, t, :], bank[2 + t // 2][:, (t % 2) * SEQ:(t % 2 + 1) * SEQ], ACT.Tanh,
                                         scale=0.5, bias=lru_c[:, 2, c:c + 1])
                ins.then_inc(gate_t, 1)
                act.wait_ge(decay_r, l + 1)
                act.activation(ts[:], tr[:], ACT.Sqrt, scale=-1.0).then_inc(sq_r, 1)

                def gelu():
                    act.wait_ge(gin_r, l + 1)
                    act.activation(gg[:], gg[:], ACT.Tanh, scale=math.sqrt(2.0 / math.pi)).then_inc(gth_r, 1)

                def recurrence():
                    for t in range(LT):
                        c = l * LT + t
                        ins = act.activation(ta[:, t, :], ta[:, t, :], ACT.Exp, scale=lru_c[:, 3, c:c + 1],
                                             bias=lru_c[:, 3, c:c + 1])
                    ins.then_inc(a_r, 1)

                def qk_turn(h):
                    n = N_HEADS * l + h
                    act.wait_ge(qkT_p, n + 1)
                    if n >= 2:
                        act.wait_ge(s_p, n - 1)
                    act.activation(qkT[:, h % 2, :], bank[h % 2][0:QK, :], ACT.Copy).then_inc(qkT_r, 1)

                def exps(h):
                    n = N_HEADS * l + h
                    act.wait_ge(s_r, n + 1)
                    for j, (c0, c1) in enumerate(((0, P), (P, 3 * P))):
                        ins = act.activation(pr[:, h % 2, c0:c1], pr[:, h % 2, c0:c1], ACT.Exp, scale=SCALE,
                                             bias=nmx[:, h % 2, j:j + 1], accum_out=rs[:, h % 2, j:j + 1])
                    ins.then_inc(p_r, 1)

                def p_turn(h):
                    n = N_HEADS * l + h
                    act.wait_ge(pT_p, n + 1)
                    if n >= 2:
                        act.wait_ge(o_p, n - 1)
                    act.activation(pT[:, h % 2, :], bank[4 + h % 2][:, 0:3 * P], ACT.Copy).then_inc(pT_r, 1)

                def o_split(g):
                    act.wait_ge(o_p, N_HEADS * l + 4 * g + 4)
                    act.activation(act_hi[:, LT + 2 * g:LT + 2 * g + 2, :],
                                   bank[6 + g][:].rearrange("p (t n) -> p t n", t=2), ACT.Copy).then_inc(o_hi, 1)

                for i in range(N_HEADS + 3):
                    if i < N_HEADS:
                        qk_turn(i)
                    if 1 <= i <= N_HEADS:
                        exps(i - 1)
                    if i == 1:
                        recurrence()
                        gelu()
                    if 2 <= i <= N_HEADS + 1:
                        p_turn(i - 2)
                    if i == 6:
                        hi(first, 9)
                    if i == 8:
                        o_split(0)
                hi(first, 10)
                o_split(1)
                hi(first, 11)
                f0 = EXPERT0 if l else FIRST["dense", 0]
                hi(f0, 0)
                hi(f0, 1)
                norm(2 * l + 1, lambda b: (mix_r, NB * l + b + 1))
                if l == 0:
                    norm_split(1, 16)
                    dense(act_dense_ops(act, lambda s: nth(f0, DENSE_ORDER.index(("gu", s, 1))) + 1), lambda c: hi(f0, c))
                else:
                    act.wait_ge(rw_in, 16)
                    act.activation(rw_hi, rw, ACT.Copy).then_inc(rw_h, 1)
                    norm_split(3, 24)
                    hi(EXPERT0, 2)
                    act.wait_ge(lg_r, 1)
                    act.activation(tw[:, 0, :], dif[:], ACT.Tanh, scale=0.5).then_inc(tw_r, 1)
                    for k in range(2):
                        for b in range(NB):
                            if k:
                                act.wait_ge(xg_v, b + 1)
                            else:
                                act.wait_ge(xg_r, b + 1)
                            act.activation(xg[k][:, b, :], xgain[:, b, :], ACT.Copy).then_inc(xg_a, 1)

            def unit_ops(j):
                return act_unit_ops(act, DENSE_U + UNITS * j, UNITS * j,
                                    lambda s: nth(EXPERT0, EXPERT_ORDER.index(("gu", s, 1)), j) + 1)

            def gathered(j):
                act.wait_ge(xT_p, j + 1)
                for k in range(2):
                    ins = act.activation(act_hi[:, 4 * k:4 * k + 4, 0:P],
                                         bank[k][:].rearrange("p (k n) -> p k n", k=4), ACT.Copy)
                ins.then_inc(xT_hi, 1)

            def outputs(i):
                act.wait_ge(used, nth(EXPERT0, PER_JOB, i))
                for k in range(2):
                    ins = act.activation(y_hi[:, 512 * k:512 * k + 512], bank[2 + k][:], ACT.Copy)
                ins.then_inc(yg_hi, 1)

            def matrix(j):
                act.wait_ge(sT_p, j + 1)
                if not isinstance(j, int):
                    act.wait_ge(sc_p, j)
                act.activation(sel_t[:], bank[7][:, 0:NB * P].rearrange("p (b n) -> p b n", b=NB),
                               ACT.Copy).then_inc(sT_r, 1)

            def job(i, more):
                job_rest(unit_ops(i), lambda c: hi(EXPERT0, c, i=i), lambda: None,
                         lambda: gathered(i + 1) if more else None,
                         lambda: hi(EXPERT0, 0, i=i + 1) if more else None)
                if more:
                    job_start(unit_ops(i + 1), lambda c: hi(EXPERT0, c, i=i + 1), lambda: outputs(i),
                              lambda: None, lambda: matrix(i + 1))

            gathered(0)
            job_start(unit_ops(0), lambda c: hi(EXPERT0, c) if c > 2 else None, lambda: None, lambda: None,
                      lambda: matrix(0))
            act.wait_ge(jobs_r, 1)
            last = act.value_load(jobs[0:1, 0:1], min_val=E - 1, max_val=E - 1 + MORE)
            with act.Fori(0, last) as i:
                job(i, True)
            job(last, False)
            outputs(last)
            squares(lambda b: (sc_r, last * NB + NB + b + 1))

        @block.vector
        def _(dve):
            step = stepper(dve, v_ch)

            def lo(first, c, width=CHUNK, i=0):
                s = split_slot(first, c)
                dve.wait_ge(hi_made, nth(first, c, i) + 1)
                dve.tensor_tensor(w_lo[:, s, 0:width], raw[:, raw_slot(first, c), 0:width],
                                  w_hi[:, s, 0:width].bitcast(F32), ALU.subtract).then_inc(lo_made, 1)

            def norm(k):
                for b in range(NB):
                    dve.wait_ge(rstd_r, NB * k + b + 1)
                    dve.tensor_scalar(xn[:, b, :], xs[:, b, :], rstd[:, b:b + 1], None, ALU.mult).then_inc(xn_v, 1)

            def norm_split(k, gain0):
                for j in range(4):
                    dve.wait_ge(nT_hi, 4 * k + j + 1)
                    for t in range(2):
                        kt = 2 * j + t
                        ins = dve.scalar_tensor_tensor(out=act_lo[:, kt, :], in0=bank[4 - 4 * (k % 2) + j][:, t * SEQ:(t + 1) * SEQ],
                                                       scalar=prm[:, gain0 + kt:gain0 + kt + 1],
                                                       in1=act_hi[:, kt, :].bitcast(F32), op0=ALU.mult, op1=ALU.subtract)
                    ins.then_inc(nT_lo, 1)

            dve.wait_ge(prm_t, 1)
            dve.tensor_copy(prm[:], bank[0][:, 0:102]).then_inc(prm_r, 1)
            def rope(dst, src, b, heads):
                sin = trig[:, 0, b, :].unsqueeze(1).to_broadcast([P, heads, HALF])
                cos = trig[:, 1, b, :].unsqueeze(1).to_broadcast([P, heads, HALF])
                ra, rb = rope_a[:, 0:heads, :], rope_b[:, 0:heads, :]
                for j in range(2):
                    hs = slice(HALF * j, HALF * j + HALF)
                    dve.tensor_tensor(ra[:, :, hs], src[:, :, hs], cos, ALU.mult)
                    ins = dve.tensor_tensor(rb[:, :, hs], src[:, :, hs], sin, ALU.mult)
                step(ins)
                dve.tensor_tensor(dst[:, :, 0:HALF], ra[:, :, 0:HALF], rb[:, :, HALF:], ALU.subtract)
                return dve.tensor_tensor(dst[:, :, HALF:], ra[:, :, HALF:], rb[:, :, 0:HALF], ALU.add)

            for l in range(DEPTH):
                first = FIRST["mix", l]
                norm(2 * l)
                if l == 0:
                    dve.wait_ge(pos_in, 16)
                    step(dve.tensor_copy(pos_f[:], pos_i[:]))
                    dve.wait_ge(consts, 1)
                    for b in range(NB):
                        ins = dve.tensor_scalar(ang[:, b, :], inv[:], pos_f[:, b:b + 1], None, ALU.mult)
                    step(ins)
                    rnd = 1.5 * 2.0 ** 23
                    for w in range(2):
                        ins = dve.tensor_scalar(turn[:, w], ang, 1.0 / (2 * math.pi), 0.25 * w, ALU.mult, ALU.add)
                    step(ins)
                    step(dve.tensor_scalar(turn, turn, rnd, -rnd, ALU.add, ALU.add))
                    c1 = 6.28125
                    c2 = float(np.float32(2 * math.pi - c1))
                    for w in range(2):
                        ins = dve.scalar_tensor_tensor(out=trig_in[:, w], in0=turn[:, w], scalar=-c1, in1=ang, op0=ALU.mult, op1=ALU.add)
                    step(ins)
                    step(dve.scalar_tensor_tensor(out=trig_in, in0=turn, scalar=-c2, in1=trig_in, op0=ALU.mult, op1=ALU.add))
                    step(dve.tensor_scalar(trig_in[:, 1], trig_in[:, 1], math.pi / 2, None, ALU.add))
                    lim = 3.1415925
                    dve.tensor_scalar(trig_in, trig_in, lim, -lim, ALU.min, ALU.max).then_inc(angle_r, 1)
                    lo(first, 0, 4 * ZT)
                norm_split(2 * l, l * KT)
                if l == 0:
                    lo(first, 1, 4 * ZT)
                    dve.wait_ge(prm_r, 1)
                    dve.tensor_scalar(lru_c[:, 1:3, :], prm[:, 72:88].rearrange("p (w c) -> p w c", w=2), 0.5, None, ALU.mult)
                    dve.wait_ge(lam_e, 2)
                    dve.tensor_scalar(lru_c[:, 3, :], lru_c[:, 0, :], -LRU_C / 2, None, ALU.mult)
                    step(dve.tensor_scalar(lru_c[:, 0, :], lru_c[:, 0, :], -LRU_C / 4, None, ALU.mult))
                    dve.tensor_copy(dif[:], pos_f[:]).then_inc(lru_r, 1)
                    dve.wait_ge(trig_r, 1)
                lo(first, 2)
                lo(first, 3)
                dve.wait_ge(zrstd_r, l + 1)
                for b in range(NB):
                    dve.tensor_scalar(cn[:, b, 0:QL], bank[b][:, 0:QL], zrstd[:, 0, b:b + 1], None, ALU.mult)
                    ins = dve.tensor_scalar(cn[:, b, QL:], bank[b][:, QL:QL + KVL], zrstd[:, 1, b:b + 1], None, ALU.mult)
                ins.then_inc(cn_r, 1)
                for b in range(NB):
                    ins = rope(kr[:, b, :].unsqueeze(1), bank[b][:, QL + KVL:ZT].unsqueeze(1), b, 1)
                    if b == 0:
                        step(ins)
                ins.then_inc(kr_r, 1)
                lo(first, 4)

                def conv(j):
                    for t in range(LT):
                        w = 32 + (l * CONV_W + j) * LT + t
                        src = xl[:, t, j:j + SEQ]
                        if j == CONV_W - 1:
                            cb = 64 + l * LT + t
                            ins = dve.tensor_scalar(xc[:, t, :], src, prm[:, w:w + 1], prm[:, cb:cb + 1], ALU.mult, ALU.add)
                        else:
                            ins = dve.scalar_tensor_tensor(out=xc[:, t, :], in0=src, scalar=prm[:, w:w + 1], in1=xc[:, t, :],
                                                           op0=ALU.mult, op1=ALU.add)
                    if j:
                        step(ins)
                    else:
                        ins.then_inc(xc_r, 1)

                dve.wait_ge(xl_r, l + 1)
                conv(3)
                conv(2)
                dve.wait_ge(cT_hi, l + 1)
                for t in range(CT):
                    g = 96 + 2 * l + t if t < QL // P else 100 + l
                    ins = dve.scalar_tensor_tensor(out=c_lo[:, t, :], in0=bank[2 + t // 2][:, (t % 2) * SEQ:(t % 2 + 1) * SEQ],
                                                   scalar=prm[:, g:g + 1], in1=c_hi[:, t, :].bitcast(F32),
                                                   op0=ALU.mult, op1=ALU.subtract)
                ins.then_inc(cT_lo, 1)
                lo(first, 5, QL // P * N_HEADS * QK)
                conv(1)
                conv(0)
                lo(first, 6)
                lo(first, 7, KVL // P * w_ukv.shape[2])

                def lru_part(i):
                    if i == 0:
                        dve.wait_ge(sq_r, l + 1)
                        dve.wait_ge(a_r, l + 1)
                        step(dve.scalar_tensor_tensor(out=ts[:], in0=ta[:], scalar=1.0, in1=ts[:], op0=ALU.add, op1=ALU.mult))
                        step(dve.memset(ts[:, :, 0:1], 1.0))
                    elif i == 1:
                        dve.wait_ge(iw_r, l + 1)
                        step(dve.tensor_tensor(tb[:], tb[:], ts[:], ALU.mult))
                    elif i <= 3:
                        for t in (2 * i - 4, 2 * i - 3):
                            ins = dve.tensor_tensor_scan(ts[:, t, :], ta[:, t, :], tb[:, t, :], 0.0, ALU.mult, ALU.add)
                        step(ins)
                    elif i == 4:
                        dve.wait_ge(gg_r, l + 1)
                        dve.scalar_tensor_tensor(out=ts[:], in0=ts[:], scalar=0.25, in1=gg[:], op0=ALU.mult, op1=ALU.mult).then_inc(lru_o, 1)

                dve.wait_ge(used, first + 6)
                for b in range(NB):
                    for j in range(2):
                        ins = dve.tensor_copy(qcat[:, b, 4 * j:4 * j + 4, :],
                                              bank[2 + 2 * b + j][:, 0:4 * QK].rearrange("p (h d) -> p h d", h=4))
                ins.then_inc(q_c, 1)
                dve.wait_ge(q_c, l + 1)
                for b in range(NB):
                    rq = qcat[:, b, :, QK_NOPE:]
                    ins = rope(rq, rq, b, N_HEADS)
                    if b == 0:
                        step(ins)
                ins.then_inc(q_r, 1)
                lo(first, 8)
                dve.wait_ge(used, first + 8)
                for part, made in ((0, k_r), (1, v_r)):
                    for b in range(NB):
                        for j in range(2):
                            src = bank[4 + 2 * j + b][:].rearrange("p (h d) -> p h d", h=4)
                            hs = slice(4 * j, 4 * j + 4)
                            if part == 0:
                                ins = dve.tensor_copy(kcat[:, b, hs, 0:QK_NOPE], src[:, :, 0:QK_NOPE])
                            else:
                                ins = dve.tensor_copy(vv[:, b, hs, :], src[:, :, QK_NOPE:])
                    ins.then_inc(made, 1)

                def mask_max(h):
                    n = N_HEADS * l + h
                    dve.wait_ge(s_p, n + 1)
                    if n >= 2:
                        dve.wait_ge(pT_p, n - 1)
                    for j, (c0, c1) in enumerate(((0, P), (P, 3 * P))):
                        ins = dve.tensor_tensor_reduce(pr[:, h % 2, c0:c1], bank[2 + h % 2][:, c0:c1], mask[:, c0:c1], 1.0, -3e38,
                                                       ALU.add, ALU.max, mx[:, h % 2, j:j + 1])
                    step(ins)
                    dve.tensor_scalar(nmx[:, h % 2, :], mx[:, h % 2, :], -SCALE, None, ALU.mult).then_inc(s_r, 1)

                def normalise(h):
                    n = N_HEADS * l + h
                    dve.wait_ge(p_r, n + 1)
                    step(dve.reciprocal(ri[:, h % 2, :], rs[:, h % 2, :]))
                    for j, (c0, c1) in enumerate(((0, P), (P, 3 * P))):
                        ins = dve.tensor_scalar(pr[:, h % 2, c0:c1], pr[:, h % 2, c0:c1], ri[:, h % 2, j:j + 1], None, ALU.mult)
                    ins.then_inc(pn_r, 1)

                def o_split(g):
                    dve.wait_ge(o_hi, 2 * l + g + 1)
                    a = slice(LT + 2 * g, LT + 2 * g + 2)
                    dve.tensor_tensor(act_lo[:, a, :], bank[6 + g][:].rearrange("p (t n) -> p t n", t=2),
                                      act_hi[:, a, :].bitcast(F32), ALU.subtract).then_inc(o_lo, 1)

                for i in range(N_HEADS + 3):
                    if 2 <= i <= N_HEADS + 1:
                        normalise(i - 2)
                    if 1 <= i <= N_HEADS:
                        mask_max(i - 1)
                    if 2 <= i <= 6:
                        lru_part(i - 2)
                    if i == 7:
                        lo(first, 9)
                    if i == 8:
                        o_split(0)
                lo(first, 10)
                o_split(1)
                lo(first, 11)
                f0 = EXPERT0 if l else FIRST["dense", 0]
                lo(f0, 0)
                lo(f0, 1)
                dve.wait_ge(first_rows, 2 * l + 1)
                for b in range(NB):
                    if b:
                        dve.wait_ge(used, first + MIX_CHUNKS)
                    for j in range(2):
                        ins = dve.tensor_tensor(xs[:, b, 512 * j:512 * j + 512], xs[:, b, 512 * j:512 * j + 512], bank[2 * b + j][:], ALU.add)
                    ins.then_inc(mix_r, 1)
                norm(2 * l + 1)
                if l == 0:
                    norm_split(1, 16)
                    dense(vec_dense_ops(dve), lambda c: lo(f0, c))
                    lo(FIRST["mix", 1], 0, 4 * ZT)
                    lo(FIRST["mix", 1], 1, 4 * ZT)
                    dve.wait_ge(first_rows, 2)
                    for b in range(NB):
                        if b:
                            dve.wait_ge(used, FIRST["mix", 1])
                        for j in range(2):
                            ins = dve.tensor_tensor(xs[:, b, 512 * j:512 * j + 512], xs[:, b, 512 * j:512 * j + 512], bank[2 * b + j][:], ALU.add)
                        ins.then_inc(y_r, 1)

            dve.wait_ge(rw_h, 1)
            dve.tensor_tensor(rw_lo, rw, rw_hi.bitcast(F32), ALU.subtract).then_inc(rw_r, 1)
            norm_split(3, 24)
            dve.wait_ge(lg_p, 1)
            dve.tensor_copy(lgT[:], bank[6][0:E, 0:SEQ]).then_inc(lgT_r, 1)
            dve.wait_ge(lg_p, 2)
            step(dve.tensor_copy(lg, bank[7][:, 0:NB * E].rearrange("p (b e) -> p b e", b=NB)))
            for b in range(NB):
                ins = dve.max(top[:, b, :], lg[:, b, :])
            step(ins)
            dve.tensor_tensor(dif[:].unsqueeze(2), top[:, :, 0:1], top[:, :, 1:2], ALU.subtract).then_inc(lg_r, 1)
            for b in range(NB):
                ins = dve.max_index(topi[:, b, :], top[:, b, :], lg[:, b, :])
            step(ins)
            step(dve.tensor_copy(topf, topi))
            for b in range(NB):
                for k in range(TOP_K):
                    ins = dve.tensor_scalar(oh[:, k, b, :], i8[:], topf[:, b, k:k + 1], None, ALU.is_equal)
            step(ins)
            dve.tensor_tensor(pick, oh[:, 0], oh[:, 1], ALU.add).then_inc(pick_r, 1)
            for b in range(NB):
                dve.wait_ge(xg_a, b + 1)
                dve.tensor_tensor(xgain[:, b, :], xgain[:, b, :], xg[0][:, b, :], ALU.subtract).then_inc(xg_v, 1)
            dve.wait_ge(tw_r, 1)
            dve.tensor_scalar(tw[:, 1, :], tw[:, 0, :], -0.5, 0.5, ALU.mult, ALU.add).then_inc(tw_r, 1)
            dve.wait_ge(tw_r, 2)
            step(dve.tensor_scalar(tw[:, 0, :], tw[:, 0, :], 0.5, 0.5, ALU.mult, ALU.add))
            for b in range(NB):
                ins = dve.tensor_scalar(gates[:, b, 0:E], oh[:, 0, b, :], tw[:, 0, b:b + 1], None, ALU.mult)
            step(ins)
            for b in range(NB):
                ins = dve.scalar_tensor_tensor(out=gates[:, b, 0:E], in0=oh[:, 1, b, :], scalar=tw[:, 1, b:b + 1], in1=gates[:, b, 0:E],
                                               op0=ALU.mult, op1=ALU.add)
            step(ins)
            dve.wait_ge(place_p, 1)
            over, upto = (jb[:, k, :] for k in range(2))
            dve.tensor_scalar(over, bank[7][:, NB * E:(NB + 1) * E], P + 0.5, None, ALU.is_gt).then_inc(sc_r, NB)
            step(dve.scalar_tensor_tensor(out=place[:, :, 0:E], in0=bank[7][:, 0:NB * E].rearrange("p (b e) -> p b e", b=NB),
                                          scalar=1.0, in1=pick, op0=ALU.add, op1=ALU.mult))
            step(dve.tensor_scalar(place[:, :, 0:E], place[:, :, 0:E], -1.0, None, ALU.add))

            def matrix(j):
                if not isinstance(j, int):
                    dve.wait_ge(sT_p, j)
                for b in range(NB):
                    ins = dve.tensor_copy(cur[:, 0, b:b + 1], place[:, b, bass.ds(j, 1)])
                ins.then_inc(cur_r, 1)
                dve.wait_ge(cur_r, j + 1)
                for b in range(NB):
                    ins = dve.tensor_scalar(sel[:, b, :], slot, cur[:, 0, b:b + 1], None, ALU.is_equal)
                ins.then_inc(sel_r, 1)

            dve.wait_ge(consts, 2)
            matrix(0)
            for b in range(NB):
                dve.wait_ge(xg_a, NB + b + 1)
                dve.tensor_tensor(xg[2][:, b, :], xgain[:, b, :], xg[1][:, b, :], ALU.subtract).then_inc(xg_v, 1)
            lo(EXPERT0, 2)
            def gathered(j):
                dve.wait_ge(xT_hi, j + 1)
                for k in range(2):
                    a = slice(4 * k, 4 * k + 4)
                    ins = dve.tensor_tensor(act_lo[:, a, 0:P], bank[k][:].rearrange("p (k n) -> p k n", k=4),
                                            act_hi[:, a, 0:P].bitcast(F32), ALU.subtract)
                ins.then_inc(xT_lo, 1)

            def outputs(i):
                dve.wait_ge(yg_hi, i + 1)
                for k in range(2):
                    w = slice(512 * k, 512 * k + 512)
                    ins = dve.tensor_tensor(y_lo[:, w], bank[2 + k][:], y_hi[:, w].bitcast(F32), ALU.subtract)
                ins.then_inc(yg_lo, 1)

            def token_gates(i):
                for b in range(NB):
                    ins = dve.tensor_copy(cur[:, 1, b:b + 1], gates[:, b, bass.ds(i, 1)])
                ins.then_inc(gate_r, 1)
                dve.wait_ge(gate_r, i + 1)

            def add(i, b):
                dve.wait_ge(sc_p, i + 1)
                for j in range(2):
                    w = slice(512 * j, 512 * j + 512)
                    ins = dve.scalar_tensor_tensor(out=xs[:, b, w], in0=bank[2 * b + j][:], scalar=cur[:, 1, b:b + 1],
                                                   in1=xs[:, b, w], op0=ALU.mult, op1=ALU.add)
                ins.then_inc(sc_r, 1)

            def outputs_and_gates(i):
                outputs(i)
                token_gates(i)

            def job(i, more):
                job_rest(vec_unit_ops(dve, DENSE_U + UNITS * i), lambda c: lo(EXPERT0, c, i=i),
                         lambda: matrix(i + 1) if more else None, lambda: gathered(i + 1) if more else None,
                         lambda: lo(EXPERT0, 0, i=i + 1) if more else None)
                if more:
                    job_start(vec_unit_ops(dve, DENSE_U + UNITS * (i + 1)), lambda c: lo(EXPERT0, c, i=i + 1),
                              lambda: outputs_and_gates(i), lambda: add(i, 1), lambda: add(i, 0))

            gathered(0)
            hit = [jb[:, 2 + j, :] for j in range(MORE)]
            step(dve.tensor_tensor_scan(upto, over, over, 0.0, ALU.add, ALU.max))
            for j in range(MORE):
                ins = dve.scalar_tensor_tensor(out=hit[j], in0=upto, scalar=float(j + 1), in1=over, op0=ALU.is_equal, op1=ALU.mult)
            step(ins)
            dve.tensor_scalar(jf[:, 0:1], upto[0:1, E - 1:E], float(E - 1), None, ALU.add)
            for j in range(MORE):
                ins = dve.tensor_tensor(jb[0:1, 5 + j, :], hit[j][0:1], i8[0:1, :], ALU.mult)
            step(ins)
            step(dve.tensor_reduce(jf[:, 1:1 + MORE], jb[0:1, 5:5 + MORE, :], AX, ALU.add))
            dve.tensor_copy(jobs[:], jf[:]).then_inc(jobs_r, 1)
            for j in range(MORE):
                for b in range(NB):
                    dve.scalar_tensor_tensor(out=wide[:, 0, j, b, :], in0=place[:, b, 0:E], scalar=1.0 - P, in1=hit[j], op0=ALU.add, op1=ALU.mult)
                    ins = dve.tensor_tensor(wide[:, 1, j, b, :], gates[:, b, 0:E], hit[j], ALU.mult)
            step(ins)
            for j in range(MORE):
                dve.tensor_reduce(place[:, :, E + j], wide[:, 0, j], AX, ALU.add)
                ins = dve.tensor_reduce(gates[:, :, E + j], wide[:, 1, j], AX, ALU.add)
            step(ins)
            step(dve.tensor_scalar(place[:, :, E:E + MORE], place[:, :, E:E + MORE], -1.0, None, ALU.add))
            job_start(vec_unit_ops(dve, DENSE_U), lambda c: lo(EXPERT0, c) if c > 2 else None, lambda: None,
                      lambda: None, lambda: None)
            last = dve.value_load(jobs[0:1, 0:1], min_val=E - 1, max_val=E - 1 + MORE)
            with dve.Fori(0, last) as i:
                job(i, True)
            job(last, False)
            outputs_and_gates(last)
            for b in range(NB):
                add(last, b)
            dve.wait_ge(grow_in, 32)
            for b in range(NB):
                dve.wait_ge(rstd_r, NB * 2 * DEPTH + b + 1)
                dve.scalar_tensor_tensor(out=xn[:, b, :], in0=xs[:, b, :], scalar=rstd[:, b:b + 1], in1=grow,
                                         op0=ALU.mult, op1=ALU.mult).then_inc(out_r, 1)

        @block.tensor
        def _(pe):
            def chunk(first, c, i=0):
                pe.wait_ge(lo_made, nth(first, c, i) + 1)
                return split_slot(first, c)

            def three(o, a_h, a_l, b_h, b_l, start, stop, **k):
                pe.matmul(o, a_l, b_h, start=start, stop=False, **k)
                pe.matmul(o, a_h, b_l, start=False, stop=False, **k)
                return pe.matmul(o, a_h, b_h, start=False, stop=stop, **k)

            def dense_gate_up(s):
                if s >= 2:
                    pe.wait_ge(hid_r, s - 1)
                for k in range(2):
                    c = DENSE_ORDER.index(("gu", s, k))
                    sl = chunk(FIRST["dense", 0], c)
                    for kk in range(4):
                        kt = 4 * k + kk
                        if s == 0 and kt % 2 == 0:
                            pe.wait_ge(nT_lo, 4 + kt // 2 + 1)
                        for w in range(2):
                            for j in range(2):
                                o = bank[4 + 2 * (s % 2) + w][:, j * SEQ:(j + 1) * SEQ]
                                m = slice((2 * kk + w) * FW + j * P, (2 * kk + w) * FW + (j + 1) * P)
                                ins = three(o, w_hi[:, sl, m], w_lo[:, sl, m], act_hi[:, kt, :], act_lo[:, kt, :],
                                            start=(kt == 0 and j == 0), stop=(kt == KT - 1), skip_group_check=True)
                    ins.then_inc(used, 1)

            def dense_down(s):
                sl = chunk(FIRST["dense", 0], DENSE_ORDER.index(("down", s, 0)))
                pe.wait_ge(hT_lo, s + 1)
                for b in range(NB):
                    for j in range(2):
                        m = slice(b * P, (b + 1) * P)
                        for n in range(2):
                            w = slice(j * D + 512 * n, j * D + 512 * (n + 1))
                            ins = three(bank[2 * b + n][:], sm_hi[:, s % SLOTS, j, m], sm_lo[:, s % SLOTS, j, m],
                                        w_hi[:, sl, w], w_lo[:, sl, w], start=(s == 0 and j == 0),
                                        stop=(s == DENSE_UNITS - 1 and j == 1))
                    if b == 0 and s == DENSE_UNITS - 1:
                        ins.then_inc(first_rows, 1)
                ins.then_inc(used, 1)

            def expert_products(u0, i):
                def gate_up(s):
                    if s != 1:
                        pe.wait_ge(hid_r, u0 + max(s - 1, 0))
                    for k in range(2):
                        sl = chunk(EXPERT0, EXPERT_ORDER.index(("gu", s, k)), i)
                        for kk in range(4):
                            kt = 4 * k + kk
                            n = slice(kk * 2 * FW, (kk + 1) * 2 * FW)
                            ins = three(bank[4 + s % 2][:], act_hi[:, kt, 0:P], act_lo[:, kt, 0:P], w_hi[:, sl, n], w_lo[:, sl, n],
                                        start=(kt == 0), stop=(kt == KT - 1))
                        ins.then_inc(used, 1)

                def turn(s):
                    pe.wait_ge(hid_r, u0 + s + 1)
                    if s != 1:
                        pe.wait_ge(hT_lo, u0 + max(s - 1, 0))
                    h = hid[:, s % 2, :].rearrange("p (n j) -> p j n", j=2)
                    for j in range(2):
                        ins = pe.transpose(bank[6 + s % 2][:, j * P:(j + 1) * P], h[:, j, :], ident[:])
                    ins.then_inc(hT_p, 1)

                def down(s):
                    sl = chunk(EXPERT0, EXPERT_ORDER.index(("down", s, 0)), i)
                    pe.wait_ge(hT_lo, u0 + s + 1)
                    for j in range(2):
                        m = slice(j * P, (j + 1) * P)
                        for n in range(2):
                            w = slice(j * D + 512 * n, j * D + 512 * (n + 1))
                            ins = three(bank[2 + n][:], sm_hi[:, s % SLOTS, 0, m], sm_lo[:, s % SLOTS, 0, m],
                                        w_hi[:, sl, w], w_lo[:, sl, w], start=(s == 0 and j == 0),
                                        stop=(s == UNITS - 1 and j == 1))
                    ins.then_inc(used, 1)

                return gate_up, turn, down

            def norm_turn(k):
                for b in range(NB):
                    pe.wait_ge(xn_v, NB * k + b + 1)
                    for kt in range(KT):
                        c = (kt % 2) * SEQ + b * P
                        ins = pe.transpose(bank[4 - 4 * (k % 2) + kt // 2][:, c:c + P], xn[:, b, kt * P:(kt + 1) * P], ident[:])
                        if b and kt % 2:
                            ins.then_inc(nT, 1)

            pe.wait_ge(consts, 1)
            pe.wait_ge(rows_in, 16 * 9)
            pe.transpose(bank[0][:, 0:102], rows, ident[0:102, 0:102]).then_inc(prm_t, 1)
            pe.wait_ge(prm_r, 1)

            for l in range(DEPTH):
                first = FIRST["mix", l]
                norm_turn(2 * l)
                for k in range(2):
                    s = chunk(first, k)
                    wh = w_hi[:, s, 0:4 * ZT].rearrange("p (k n) -> p k n", k=4)
                    wl = w_lo[:, s, 0:4 * ZT].rearrange("p (k n) -> p k n", k=4)
                    for kk in range(4):
                        kt = 4 * k + kk
                        if kt % 2 == 0:
                            pe.wait_ge(nT_lo, 8 * l + kt // 2 + 1)
                        for b in range(NB):
                            m = slice(b * P, (b + 1) * P)
                            ins = three(bank[b][:, 0:ZT], act_hi[:, kt, m], act_lo[:, kt, m], wh[:, kk, :], wl[:, kk, :],
                                        start=(kt == 0), stop=(kt == KT - 1))
                    ins.then_inc(used, 1)

                def wide_product(chunks, banks):
                    for c, k in chunks:
                        s = chunk(first, c)
                        wh = w_hi[:, s, :].rearrange("p (k n) -> p k n", k=4)
                        wl = w_lo[:, s, :].rearrange("p (k n) -> p k n", k=4)
                        for kk in range(4):
                            kt = 4 * k + kk
                            for t in range(LT):
                                o = bank[banks + t // 2][:, (t % 2) * SEQ:(t % 2 + 1) * SEQ]
                                m = slice(t * P, (t + 1) * P)
                                ins = three(o, wh[:, kk, m], wl[:, kk, m], act_hi[:, kt, :], act_lo[:, kt, :],
                                            start=(kt == 0 and t % 2 == 0), stop=(kt == KT - 1), skip_group_check=True)
                        ins.then_inc(used, 1)

                pe.wait_ge(nT_lo, 8 * l + 4)
                wide_product(((2, 0), (3, 1)), 4)
                pe.wait_ge(cn_r, l + 1)
                for t in range(CT):
                    for b in range(NB):
                        c = (t % 2) * SEQ + b * P
                        ins = pe.transpose(bank[2 + t // 2][:, c:c + P], cn[:, b, t * P:(t + 1) * P], ident[:])
                ins.then_inc(cT, 1)
                wide_product(((4, 0),), 6)
                pe.wait_ge(cT_lo, l + 1)
                pe.wait_ge(xl_r, l + 1)
                QT = QL // P
                s = chunk(first, 5)
                wh = w_hi[:, s, 0:QT * N_HEADS * QK].rearrange("p (k n) -> p k n", k=QT)
                wl = w_lo[:, s, 0:QT * N_HEADS * QK].rearrange("p (k n) -> p k n", k=QT)
                for b in range(NB):
                    m = slice(b * P, (b + 1) * P)
                    for j in range(2):
                        n = slice(j * 4 * QK, (j + 1) * 4 * QK)
                        for kt in range(QT):
                            ins = three(bank[2 + 2 * b + j][:, 0:4 * QK], c_hi[:, kt, m], c_lo[:, kt, m], wh[:, kt, n], wl[:, kt, n],
                                        start=(kt == 0), stop=(kt == QT - 1))
                ins.then_inc(used, 1)

                def gate_product(w):
                    for t in range(LT):
                        ins = pe.matmul(bank[2 * w + t // 2][:, (t % 2) * SEQ:(t % 2 + 1) * SEQ], gate_bd[:, w, t, :],
                                        xc[:, t, :], start=True, stop=True)
                    ins.then_inc(gate_p, 1)

                pe.wait_ge(xc_r, l + 1)
                pe.wait_ge(bd_in, 64 * (l + 1))
                pe.wait_ge(kr_r, l + 1)
                gate_product(0)
                wide_product(((6, 1),), 6)
                pe.wait_ge(q_c, l + 1)
                gate_product(1)
                pe.wait_ge(yg_r, l + 1)
                s = chunk(first, 7)
                for b in range(NB):
                    m = slice(b * P, (b + 1) * P)
                    for j in range(2):
                        n = slice(j * 512, (j + 1) * 512)
                        ins = three(bank[4 + 2 * j + b][:], c_hi[:, QT, m], c_lo[:, QT, m], w_hi[:, s, n], w_lo[:, s, n],
                                    start=True, stop=True)
                ins.then_inc(used, 1)

                def qk_turn(h):
                    n = N_HEADS * l + h
                    if n >= 2:
                        pe.wait_ge(qkT_r, n - 1)
                    for b in range(NB):
                        pe.transpose(bank[h % 2][0:QK, b * P:(b + 1) * P], qcat[:, b, h, :], ident[:])
                    for b in range(NB):
                        ins = pe.transpose(bank[h % 2][0:QK, SEQ + b * P:SEQ + (b + 1) * P], kcat[:, b, h, :], ident[:])
                    ins.then_inc(qkT_p, 1)

                def scores(h):
                    n = N_HEADS * l + h
                    pe.wait_ge(qkT_r, n + 1)
                    if n >= 2:
                        pe.wait_ge(s_r, n - 1)
                    t = qkT[:, h % 2, :]
                    pe.matmul(bank[2 + h % 2][:, 0:P], t[:, 0:P], t[:, SEQ:SEQ + P], start=True, stop=True)
                    pe.matmul(bank[2 + h % 2][:, P:3 * P], t[:, P:2 * P], t[:, SEQ:2 * SEQ], start=True, stop=True).then_inc(s_p, 1)

                def p_turn(h):
                    n = N_HEADS * l + h
                    pe.wait_ge(pn_r, n + 1)
                    if n >= 2:
                        pe.wait_ge(pT_r, n - 1)
                    for src, dst in ((0, 0), (P, P), (2 * P, 2 * P)):
                        ins = pe.transpose(bank[4 + h % 2][:, dst:dst + P], pr[:, h % 2, src:src + P], ident[:])
                    ins.then_inc(pT_p, 1)

                def values(h):
                    n = N_HEADS * l + h
                    pe.wait_ge(pT_r, n + 1)
                    r = slice((h % 2) * V_HEAD, (h % 2 + 1) * V_HEAD)
                    c = (h // 2 % 2) * SEQ
                    o = bank[6 + h // 4]
                    pe.matmul(o[r, c:c + SEQ], vv[:, 0, h, :], pT[:, h % 2, 0:SEQ], start=True, stop=False)
                    pe.matmul(o[r, c + P:c + SEQ], vv[:, 1, h, :], pT[:, h % 2, SEQ:], start=False, stop=True).then_inc(o_p, 1)

                pe.wait_ge(q_r, l + 1)
                pe.wait_ge(decay_r, l + 1)
                pe.wait_ge(k_r, l + 1)
                pe.wait_ge(kr_c, l + 1)

                def out_product(c):
                    s = chunk(first, 8 + c)
                    for b in range(NB):
                        for kk in range(2):
                            kt = 2 * c + kk
                            for j in range(2):
                                m, n = slice(b * P, (b + 1) * P), slice(kk * D + 512 * j, kk * D + 512 * (j + 1))
                                ins = three(bank[2 * b + j][:], act_hi[:, kt, m], act_lo[:, kt, m], w_hi[:, s, n], w_lo[:, s, n],
                                            start=(kt == 0), stop=(kt == KT - 1))
                        if b == 0 and c == 3:
                            ins.then_inc(first_rows, 1)
                    ins.then_inc(used, 1)

                for i in range(N_HEADS + 3):
                    if i == 1:
                        pe.wait_ge(gate_t, l + 1)
                    if i == 2:
                        pe.wait_ge(v_r, l + 1)
                    if i < N_HEADS:
                        qk_turn(i)
                    if 1 <= i <= N_HEADS:
                        scores(i - 1)
                    if 2 <= i <= N_HEADS + 1:
                        p_turn(i - 2)
                    if i >= 3:
                        values(i - 3)
                    if i == N_HEADS:
                        pe.wait_ge(lru_lo, l + 1)
                        pe.wait_ge(s_r, N_HEADS * (l + 1))
                        out_product(0)
                    if i == N_HEADS + 1:
                        out_product(1)
                for c in (2, 3):
                    pe.wait_ge(o_lo, 2 * l + c - 1)
                    out_product(c)
                norm_turn(2 * l + 1)
                if l == 0:
                    for s in range(DENSE_UNITS + 1):
                        if s < DENSE_UNITS:
                            dense_gate_up(s)
                        if s:
                            dense_down(s - 1)

            pe.wait_ge(rw_r, 1)
            for kt in range(KT):
                if kt % 2 == 0:
                    pe.wait_ge(nT_lo, 4 * 3 + kt // 2 + 1)
                n = slice(kt * E, (kt + 1) * E)
                ins = three(bank[6][0:E, 0:SEQ], rw_hi[:, n], rw_lo[:, n], act_hi[:, kt, :], act_lo[:, kt, :],
                            start=(kt == 0), stop=(kt == KT - 1))
            ins.then_inc(lg_p, 1)
            pe.wait_ge(lgT_r, 1)
            for b in range(NB):
                ins = pe.transpose(bank[7][:, b * E:(b + 1) * E], lgT[:, b * P:(b + 1) * P], ident[0:E, 0:E])
            ins.then_inc(lg_p, 1)
            pe.wait_ge(pick_r, 1)
            pe.wait_ge(consts, 2)
            pe.matmul(bank[7][:, 0:E], before, pick[:, 0, :], start=True, stop=True)
            pe.matmul(bank[7][:, E:2 * E], before, pick[:, 1, :], start=True, stop=False)
            pe.matmul(bank[7][:, E:2 * E], ones, pick[:, 0, :], start=False, stop=True)
            for b in range(NB):
                ins = pe.matmul(bank[7][:, 2 * E:3 * E], ones, pick[:, b, :], start=(b == 0), stop=(b == NB - 1))
            ins.then_inc(place_p, 1)
            def products(j):
                return expert_products(DENSE_U + UNITS * j, j)

            def gather(j):
                pe.wait_ge(sel_r, j + 1)
                pe.wait_ge(sc_r, NB * j if not isinstance(j, int) else NB)
                for k in range(3):
                    if isinstance(j, int):
                        pe.wait_ge(*((xg_a, NB), (xg_a, 2 * NB), (xg_v, 2 * NB))[k])
                    for kt in range(KT):
                        f = slice(kt * P, (kt + 1) * P)
                        for b in range(NB):
                            ins = pe.matmul(bank[kt // 4][:, (kt % 4) * P:(kt % 4 + 1) * P], xg[k][:, b, f], sel[:, b, :],
                                            start=(k == 0 and b == 0 and kt % 4 == 0), stop=(k == 2 and b == NB - 1),
                                            skip_group_check=True)
                ins.then_inc(xT_p, 1)

            def scatter(i):
                pe.wait_ge(yg_lo, i + 1)
                for b in (1, 0):
                    for j in range(2):
                        w = slice(512 * j, 512 * (j + 1))
                        pe.matmul(bank[2 * b + j][:], sel_t[:, b, :], y_lo[:, w], start=True, stop=False)
                        ins = pe.matmul(bank[2 * b + j][:], sel_t[:, b, :], y_hi[:, w], start=False, stop=True)
                ins.then_inc(sc_p, 1)

            def job_begin(j):
                gate_up, turn, down = products(j)
                pe.wait_ge(xT_lo, j + 1)
                gate_up(0)
                gate_up(1)
                for b in range(NB):
                    ins = pe.matmul(bank[7][:, b * P:(b + 1) * P], sel[:, b, :], ident_b[:], start=True, stop=True)
                ins.then_inc(sT_p, 1)
                turn(0)

            def job(i, more):
                gate_up, turn, down = products(i)
                for s in range(2, UNITS):
                    gate_up(s)
                    if s == 2:
                        pe.wait_ge(sT_r, i + 1)
                    turn(s - 1)
                    if s == 2:
                        pe.wait_ge(sc_r, NB * i + 1)
                    down(s - 2)
                if more:
                    gather(i + 1)
                turn(UNITS - 1)
                down(UNITS - 2)
                down(UNITS - 1)
                if more:
                    job_begin(i + 1)
                scatter(i)

            gather(0)
            job_begin(0)
            pe.wait_ge(jobs_r, 1)
            last = pe.value_load(jobs[0:1, 0:1], min_val=E - 1, max_val=E - 1 + MORE)
            with pe.Fori(0, last) as i:
                job(i, True)
            job(last, False)


_INS = ['x', 'positions', 'norm_mix', 'w_in', 'conv_w', 'conv_b', 'lru_wa', 'lru_ba', 'lru_wx', 'lru_bx',
        'lru_lambda', 'q_norm', 'w_uq', 'kv_norm', 'w_ukv', 'w_out', 'norm_ffn', 'dense_w_gate',
        'dense_w_up', 'dense_w_down', 'router_w', 'expert_w_gate', 'expert_w_up', 'expert_w_down',
        'norm_final']


def kernel(**inputs):
    import concourse.bacc as _bacc
    from concourse.bass_utils import run_bass_kernel_spmd as _run

    nc = _bacc.Bacc("TRN2", target_bir_lowering=False, num_devices=1)
    arrays, args = {}, []
    for name in _INS:
        a = np.ascontiguousarray(inputs[name])
        arrays[f"in_{name}"] = a
        args.append(nc.dram_tensor(f"in_{name}", a.shape, mybir.dt.from_np(a.dtype), kind="ExternalInput").ap())
    out = nc.dram_tensor("out_x", inputs["x"].shape, F32, kind="ExternalOutput").ap()
    trunk(nc, *args, out)
    return _run(nc, [arrays], core_ids=[0]).results[0]["out_x"]
```
